# Optimizing a Trainium2 kernel written in Bass

```python
import math
import jax, jax.numpy as jnp
from jax import lax
import numpy as np

D_MODEL = 1024
BATCH = 1
SEQ = 1024
DEPTH = 2
DEC_BATCH = 8
DEC_SEQ = 16
PAST_LEN = 2048

CHUNK = 64
HEAD_DIM = 64
ROPE_THETA = 10000.0
NORM_EPS = 1e-6
Q_BLOCK = 128
NEG_INF = -1e30
SCALE = HEAD_DIM ** -0.5
A_Q_HEADS = 8
A_KV_HEADS = 2
A_GROUP = A_Q_HEADS // A_KV_HEADS
WINDOW = 128
WINDOW_CHUNKS = WINDOW // CHUNK
B_HEADS = 4
C_HEADS = 16
FORGET_BIAS_CENTER = 4.0
D_FF = -(-(8 * D_MODEL) // (3 * 256)) * 256
N_EVEN = (DEPTH + 1) // 2
N_ODD = DEPTH // 2
A_Q_W = A_Q_HEADS * HEAD_DIM
A_KV_W = A_KV_HEADS * HEAD_DIM
B_QK_W = 2 * B_HEADS * HEAD_DIM
B_V_W = B_HEADS * 2 * HEAD_DIM
AB_IN = A_Q_W + 2 * A_KV_W + 2 * B_QK_W + B_V_W
AB_OUT = A_Q_W + B_V_W
AB_SPLITS = (A_Q_W, A_Q_W + A_KV_W, A_Q_W + 2 * A_KV_W, A_Q_W + 2 * A_KV_W + B_QK_W, A_Q_W + 2 * A_KV_W + 2 * B_QK_W)
C_W = C_HEADS * HEAD_DIM
C_IN = 3 * C_W + C_HEADS

kernel_name = 'hybrid_streaming_encoder_step'

def _rmsnorm(x, g):
    x32 = x.astype(jnp.float32)
    y = x32 * lax.rsqrt(jnp.mean(x32 * x32, axis=-1, keepdims=True) + NORM_EPS)
    return (y * g.astype(jnp.float32)).astype(x.dtype)

def _rope(x, pos):
    half = HEAD_DIM // 2
    inv_freq = ROPE_THETA ** (-jnp.arange(half, dtype=jnp.float32) / half)
    ang = pos.astype(jnp.float32)[:, None] * inv_freq[None, :]
    cos = jnp.cos(ang)[:, None, :]
    sin = jnp.sin(ang)[:, None, :]
    x32 = x.astype(jnp.float32)
    x1, x2 = x32[..., :half], x32[..., half:]
    return jnp.concatenate([x1 * cos - x2 * sin, x2 * cos + x1 * sin], axis=-1).astype(x.dtype)

def _to_blocks(a):
    b, t = a.shape[:2]
    return jnp.moveaxis(a.reshape((b, t // Q_BLOCK, Q_BLOCK) + a.shape[2:]), 1, 0)

def _from_blocks(a):
    a = jnp.moveaxis(a, 0, 1)
    return a.reshape((a.shape[0], a.shape[1] * a.shape[2]) + a.shape[3:])

def _lambda_init(layer):
    return 0.8 - 0.6 * math.exp(-0.3 * layer)

def _softmax_with_sink(scores, sink):
    s = jnp.broadcast_to(sink.astype(jnp.float32)[:, :, None, None], scores.shape[:-1] + (1,))
    p = jax.nn.softmax(jnp.concatenate([scores, s], axis=-1), axis=-1)
    return p[..., :-1]

def _window_attend_prompt(q, k, v, sink):
    b, t = q.shape[:2]
    n_c = t // CHUNK
    n_s = (WINDOW_CHUNKS + 1) * CHUNK
    qc = q.reshape(b, n_c, CHUNK, A_KV_HEADS, A_GROUP, HEAD_DIM)

    def band(a):
        ac = a.reshape(b, n_c, CHUNK, A_KV_HEADS, HEAD_DIM)
        ap = jnp.pad(ac, ((0, 0), (WINDOW_CHUNKS, 0), (0, 0), (0, 0), (0, 0)))
        return jnp.concatenate([ap[:, j:j + n_c] for j in range(WINDOW_CHUNKS + 1)], axis=2)

    kb, vb = band(k), band(v)
    kpos = (jnp.arange(n_c)[:, None] - WINDOW_CHUNKS) * CHUNK + jnp.arange(n_s)[None, :]
    valid = (kpos >= 0)[None, :, None, None, None, :]
    scores = jnp.einsum('bcqkgd,bcskd->bckgqs', qc, kb).astype(jnp.float32) * SCALE
    scores = jnp.where(valid, scores, NEG_INF)
    p = _softmax_with_sink(scores, sink.reshape(A_KV_HEADS, A_GROUP))
    out = jnp.einsum('bckgqs,bcskd->bcqkgd', p.astype(v.dtype), vb)
    return out.reshape(b, t, A_Q_HEADS, HEAD_DIM)

def _window_attend_general(q, k, v, qpos, kpos, sink):
    b, tq = q.shape[:2]
    qg = q.reshape(b, tq, A_KV_HEADS, A_GROUP, HEAD_DIM)
    scores = jnp.einsum('btkgd,bskd->bkgts', qg, k).astype(jnp.float32) * SCALE
    qc = (qpos // CHUNK)[:, None]
    kc = (kpos // CHUNK)[None, :]
    mask = (kc <= qc) & (kc >= qc - WINDOW_CHUNKS)
    scores = jnp.where(mask, scores, NEG_INF)
    p = _softmax_with_sink(scores, sink.reshape(A_KV_HEADS, A_GROUP))
    out = jnp.einsum('bkgts,bskd->btkgd', p.astype(v.dtype), v)
    return out.reshape(b, tq, A_Q_HEADS, HEAD_DIM)

def _diff_lambda(b_lambda, lam_init):
    l = b_lambda.astype(jnp.float32)
    return jnp.exp(jnp.sum(l[0] * l[1])) - jnp.exp(jnp.sum(l[2] * l[3])) + lam_init

def _diff_attend(q, k, v, qpos, kpos, lam):
    b, tq = q.shape[:2]
    tk = k.shape[1]
    q2 = q.reshape(b, tq, B_HEADS, 2, HEAD_DIM)
    k2 = k.reshape(b, tk, B_HEADS, 2, HEAD_DIM)
    scores = jnp.einsum('bthed,bshed->bhets', q2, k2).astype(jnp.float32) * SCALE
    mask = (kpos // CHUNK)[None, :] <= (qpos // CHUNK)[:, None]
    p = jax.nn.softmax(jnp.where(mask, scores, NEG_INF), axis=-1)
    attn = p[:, :, 0] - lam * p[:, :, 1]
    return jnp.einsum('bhts,bshd->bthd', attn.astype(v.dtype), v)

def _fox_attend(q, k, v, cq, ck, qpos, kpos):
    scores = jnp.einsum('bthd,bshd->bhts', q, k).astype(jnp.float32) * SCALE
    scores = scores + jnp.moveaxis(cq, 1, 2)[..., :, None] - jnp.moveaxis(ck, 1, 2)[..., None, :]
    mask = kpos[None, :] <= qpos[:, None]
    p = jax.nn.softmax(jnp.where(mask, scores, NEG_INF), axis=-1)
    return jnp.einsum('bhts,bshd->bthd', p.astype(v.dtype), v)

def _ab_project(h, w_in, pos):
    b, t, _ = h.shape
    qa, ka, va, qb, kb, vb = jnp.split(h @ w_in, AB_SPLITS, axis=-1)
    qa = _rope(qa.reshape(b, t, A_Q_HEADS, HEAD_DIM), pos)
    ka = _rope(ka.reshape(b, t, A_KV_HEADS, HEAD_DIM), pos)
    va = va.reshape(b, t, A_KV_HEADS, HEAD_DIM)
    qb = _rope(qb.reshape(b, t, 2 * B_HEADS, HEAD_DIM), pos)
    kb = _rope(kb.reshape(b, t, 2 * B_HEADS, HEAD_DIM), pos)
    vb = vb.reshape(b, t, B_HEADS, 2 * HEAD_DIM)
    return qa, ka, va, qb, kb, vb

def _ab_merge(oa, ob, w_sub, lam_init, w_out):
    b, t = oa.shape[:2]
    ob = _rmsnorm(ob, w_sub) * (1.0 - lam_init)
    cat = jnp.concatenate([oa.reshape(b, t, A_Q_W), ob.reshape(b, t, B_V_W)], axis=-1)
    return cat @ w_out

def _mixer_ab_prompt(h, pos, w_in, w_out, sink, b_lambda, w_sub, lam_init):
    qa, ka, va, qb, kb, vb = _ab_project(h, w_in, pos)
    oa = _window_attend_prompt(qa, ka, va, sink)
    lam = _diff_lambda(b_lambda, lam_init)
    ob = _from_blocks(lax.map(lambda blk: _diff_attend(blk[0], kb, vb, blk[1], pos, lam),
                              (_to_blocks(qb), pos.reshape(-1, Q_BLOCK))))
    win = min(WINDOW, h.shape[1])
    return _ab_merge(oa, ob, w_sub, lam_init, w_out), (ka[:, -win:], va[:, -win:], kb, vb)

def _mixer_ab_sample(h, pos, c_ak, c_av, c_bk, c_bv, w_in, w_out, sink, b_lambda, w_sub, lam_init):
    qa, ka, va, qb, kb, vb = _ab_project(h, w_in, pos)
    past = c_bk.shape[1]
    win = c_ak.shape[1]
    ak_all = jnp.concatenate([c_ak, ka], axis=1)
    av_all = jnp.concatenate([c_av, va], axis=1)
    apos = jnp.concatenate([past - win + jnp.arange(win, dtype=jnp.int32), pos])
    oa = _window_attend_general(qa, ak_all, av_all, pos, apos, sink)
    lam = _diff_lambda(b_lambda, lam_init)
    bk_all = jnp.concatenate([c_bk, kb], axis=1)
    bv_all = jnp.concatenate([c_bv, vb], axis=1)
    bpos = jnp.concatenate([jnp.arange(past, dtype=jnp.int32), pos])
    ob = _diff_attend(qb, bk_all, bv_all, pos, bpos, lam)
    return _ab_merge(oa, ob, w_sub, lam_init, w_out), (ak_all[:, -win:], av_all[:, -win:], kb, vb)

def _c_project(h, w_in, b_f):
    b, t, _ = h.shape
    q, k, v, f = jnp.split(h @ w_in, (C_W, 2 * C_W, 3 * C_W), axis=-1)
    q = q.reshape(b, t, C_HEADS, HEAD_DIM)
    k = k.reshape(b, t, C_HEADS, HEAD_DIM)
    v = v.reshape(b, t, C_HEADS, HEAD_DIM)
    logf = jax.nn.log_sigmoid(f.astype(jnp.float32) + b_f.astype(jnp.float32))
    return q, k, v, logf

def _mixer_c_prompt(h, pos, w_in, b_f, w_out):
    b, t, _ = h.shape
    q, k, v, logf = _c_project(h, w_in, b_f)
    c = jnp.cumsum(logf, axis=1)
    o = _from_blocks(lax.map(lambda blk: _fox_attend(blk[0], k, v, blk[1], c, blk[2], pos),
                             (_to_blocks(q), _to_blocks(c), pos.reshape(-1, Q_BLOCK))))
    return o.reshape(b, t, C_W) @ w_out, (k, v, logf)

def _mixer_c_sample(h, pos, c_k, c_v, c_logf, w_in, b_f, w_out):
    b, t, _ = h.shape
    past = c_k.shape[1]
    q, k, v, logf = _c_project(h, w_in, b_f)
    logf_all = jnp.concatenate([c_logf.astype(jnp.float32), logf], axis=1)
    c_all = jnp.cumsum(logf_all, axis=1)
    k_all = jnp.concatenate([c_k, k], axis=1)
    v_all = jnp.concatenate([c_v, v], axis=1)
    kpos = jnp.concatenate([jnp.arange(past, dtype=jnp.int32), pos])
    o = _fox_attend(q, k_all, v_all, c_all[:, past:], c_all, pos, kpos)
    return o.reshape(b, t, C_W) @ w_out, (k, v, logf)

def _swiglu(h, w_in, w_out):
    gate, up = jnp.split(h @ w_in, 2, axis=-1)
    return (jax.nn.silu(gate) * up) @ w_out

def setup_inputs(seed: int = 0) -> dict:
    key = jax.random.key(seed)
    ks = jax.random.split(key, 20)

    def nrm(k, shape, scale=1.0):
        return jax.random.normal(k, shape, jnp.float32) * scale

    win = min(WINDOW, PAST_LEN)
    return {
        'x_prompt': nrm(ks[0], (BATCH, SEQ, D_MODEL)),
        'x_sample': nrm(ks[1], (DEC_BATCH, DEC_SEQ, D_MODEL)),
        'cache_a_k': nrm(ks[2], (N_EVEN, DEC_BATCH, win, A_KV_HEADS, HEAD_DIM)),
        'cache_a_v': nrm(ks[3], (N_EVEN, DEC_BATCH, win, A_KV_HEADS, HEAD_DIM)),
        'cache_b_k': nrm(ks[4], (N_EVEN, DEC_BATCH, PAST_LEN, 2 * B_HEADS, HEAD_DIM)),
        'cache_b_v': nrm(ks[5], (N_EVEN, DEC_BATCH, PAST_LEN, B_HEADS, 2 * HEAD_DIM)),
        'cache_c_k': nrm(ks[6], (N_ODD, DEC_BATCH, PAST_LEN, C_HEADS, HEAD_DIM)),
        'cache_c_v': nrm(ks[7], (N_ODD, DEC_BATCH, PAST_LEN, C_HEADS, HEAD_DIM)),
        'cache_c_logf': jax.nn.log_sigmoid(FORGET_BIAS_CENTER + nrm(ks[8], (N_ODD, DEC_BATCH, PAST_LEN, C_HEADS))),
        'norm_gains': 1.0 + nrm(ks[9], (DEPTH, 4, D_MODEL), 0.02),
        'w_ab_in': nrm(ks[10], (N_EVEN, D_MODEL, AB_IN), D_MODEL ** -0.5),
        'w_ab_out': nrm(ks[11], (N_EVEN, AB_OUT, D_MODEL), AB_OUT ** -0.5),
        'a_sinks': nrm(ks[12], (N_EVEN, A_Q_HEADS), 0.5),
        'b_lambda': nrm(ks[13], (N_EVEN, 4, HEAD_DIM), 0.1),
        'b_subln': 1.0 + nrm(ks[14], (N_EVEN, 2 * HEAD_DIM), 0.02),
        'w_c_in': nrm(ks[15], (N_ODD, D_MODEL, C_IN), D_MODEL ** -0.5),
        'c_forget_bias': FORGET_BIAS_CENTER + nrm(ks[16], (N_ODD, C_HEADS), 0.1),
        'w_c_out': nrm(ks[17], (N_ODD, C_W, D_MODEL), C_W ** -0.5),
        'w_ffn_in': nrm(ks[18], (DEPTH, D_MODEL, 2 * D_FF), D_MODEL ** -0.5),
        'w_ffn_out': nrm(ks[19], (DEPTH, D_FF, D_MODEL), D_FF ** -0.5),
    }

def reference(x_prompt, x_sample, cache_a_k, cache_a_v, cache_b_k, cache_b_v, cache_c_k, cache_c_v,
              cache_c_logf, norm_gains, w_ab_in, w_ab_out, a_sinks, b_lambda, b_subln, w_c_in,
              c_forget_bias, w_c_out, w_ffn_in, w_ffn_out):
    t_p = x_prompt.shape[1]
    t_s = x_sample.shape[1]
    past = cache_b_k.shape[2]
    pos_p = jnp.arange(t_p, dtype=jnp.int32)
    pos_s = past + jnp.arange(t_s, dtype=jnp.int32)
    yp, ys = x_prompt, x_sample
    ap_k, ap_v, bp_k, bp_v, cp_k, cp_v, cp_f = [], [], [], [], [], [], []
    as_k, as_v, bs_k, bs_v, cs_k, cs_v, cs_f = [], [], [], [], [], [], []
    for layer in range(DEPTH):
        g = norm_gains[layer]
        if layer % 2 == 0:
            e = layer // 2
            prm = (w_ab_in[e], w_ab_out[e], a_sinks[e], b_lambda[e], b_subln[e], _lambda_init(layer))
            mp, (ak, av, bk, bv) = _mixer_ab_prompt(_rmsnorm(yp, g[0]), pos_p, *prm)
            ms, (sak, sav, sbk, sbv) = _mixer_ab_sample(_rmsnorm(ys, g[0]), pos_s, cache_a_k[e], cache_a_v[e],
                                                        cache_b_k[e], cache_b_v[e], *prm)
            ap_k.append(ak); ap_v.append(av); bp_k.append(bk); bp_v.append(bv)
            as_k.append(sak); as_v.append(sav); bs_k.append(sbk); bs_v.append(sbv)
        else:
            o = layer // 2
            mp, (ck, cv, cf) = _mixer_c_prompt(_rmsnorm(yp, g[0]), pos_p, w_c_in[o], c_forget_bias[o], w_c_out[o])
            ms, (sck, scv, scf) = _mixer_c_sample(_rmsnorm(ys, g[0]), pos_s, cache_c_k[o], cache_c_v[o],
                                                  cache_c_logf[o], w_c_in[o], c_forget_bias[o], w_c_out[o])
            cp_k.append(ck); cp_v.append(cv); cp_f.append(cf)
            cs_k.append(sck); cs_v.append(scv); cs_f.append(scf)
        yp = yp + _rmsnorm(mp, g[1])
        ys = ys + _rmsnorm(ms, g[1])
        yp = yp + _rmsnorm(_swiglu(_rmsnorm(yp, g[2]), w_ffn_in[layer], w_ffn_out[layer]), g[3])
        ys = ys + _rmsnorm(_swiglu(_rmsnorm(ys, g[2]), w_ffn_in[layer], w_ffn_out[layer]), g[3])
    return (yp, ys,
            jnp.stack(ap_k), jnp.stack(ap_v), jnp.stack(bp_k), jnp.stack(bp_v),
            jnp.stack(cp_k), jnp.stack(cp_v), jnp.stack(cp_f),
            jnp.stack(as_k), jnp.stack(as_v), jnp.stack(bs_k), jnp.stack(bs_v),
            jnp.stack(cs_k), jnp.stack(cs_v), jnp.stack(cs_f))


_drawn_inputs = setup_inputs


def setup_inputs(seed=0):
    import zlib

    import numpy as np

    out = dict(_drawn_inputs(seed))
    spreads = {}
    factors = {'a_sinks': 8.0, 'b_lambda': 3.737, 'b_subln': 2.94}
    for name, (base, spread) in spreads.items():
        noise = np.random.default_rng([zlib.crc32(name.encode()), seed]).standard_normal(out[name].shape)
        drawn = base * np.exp(spread * noise) if base else spread * noise
        out[name] = __import__('jax').numpy.asarray(drawn.astype(out[name].dtype))
    for name, factor in factors.items():
        out[name] = (out[name] * factor).astype(out[name].dtype)
    return out
```

```python
import math
from contextlib import ExitStack, contextmanager

import numpy as np

import concourse.bass as bass
from concourse import mybir

F32 = mybir.dt.float32
F32R = mybir.dt.float32r
BF16 = mybir.dt.bfloat16
ALU = mybir.AluOpType
ACT = mybir.ActivationFunctionType
AX = mybir.AxisListType

P = 128
D = 1024
KT = D // P
PROMPT = 1024
TILES_P = PROMPT // P
TILES = TILES_P + 1
TOKENS = TILES * P
STREAMS, FRAMES, PAST = 8, 16, 2048
DH = 64
HALF = DH // 2
CHUNK = 64
SCALE = DH ** -0.5
EPS = 1e-6
NEG = -1e30
A_Q, A_KV, B_H, C_H = 8, 2, 4, 16
A_GROUP = A_Q // A_KV
AB_IN = A_Q * DH + 2 * A_KV * DH + 3 * 2 * B_H * DH
C_IN = 3 * D + C_H
D_FF = 2816
WIN = 128
LAM_INIT = 0.8 - 0.6 * math.exp(0.0)
QA, KA, VA, QB, KB, VB = 0, 512, 640, 768, 1280, 1792


def rows(ap, count=P):
    return bass.AP(ap.tensor, ap.offset, [[0, count]] + [list(x) for x in ap.ap[1:]])


class Stage:

    def __init__(self, nc, name):
        self.nc, self.name, self.ctx = nc, name, ExitStack()

    def __enter__(self):
        self.before = self.nc.snapshot_sems()
        return self

    def __exit__(self, *exc):
        self.ctx.close()
        self.nc.clear_and_free_semaphores(self.nc.allocated_since(self.before))
        self.nc.all_engine_barrier()

    def sb(self, name, shape, dtype=F32):
        return self.ctx.enter_context(self.nc.sbuf_tensor(f"{self.name}_{name}", shape, dtype))

    def ps(self, name, shape, dtype=F32):
        return self.ctx.enter_context(self.nc.psum_tensor(f"{self.name}_{name}", shape, dtype))

    def sem(self, name):
        return self.nc.alloc_semaphore(f"{self.name}_{name}")

    def sems(self, name, n):
        return [self.sem(f"{name}{k}") for k in range(n)]

    def block(self):
        return self.ctx.enter_context(self.nc.Block())


def make_identity(pool, ident, done):
    pool.memset(ident[:], 0.0).then_inc(done, 1)
    pool.wait_ge(done, 1)
    pool.affine_select(out=ident[:], in_=ident[:], compare_op=ALU.not_equal, fill=1.0, base=0,
                       pattern=[[-1, P]], channel_multiplier=1).then_inc(done, 1)


def norm_to_columns(nc, name, x_tile, gain, ht_hi, ht_lo):
    with Stage(nc, name) as st:
        x = st.sb("x", [P, 2, D])
        h = st.sb("h", [P, 2, D])
        squares = st.sb("squares", [P, D])
        g = st.sb("g", [P, D])
        ident = st.sb("ident", [P, P])
        total, var, root, inv = (st.sb(n, [P, TILES]) for n in ("total", "var", "root", "inv"))
        turned = st.ps("turned", [P, 2, KT, P])
        g_loaded, ident_done = st.sem("g_loaded"), st.sem("ident_done")
        x_loaded = st.sems("x_loaded", 2)
        total_done, var_done, root_done, inv_done, h_done, turned_done, hi_done, lo_done = (
            st.sem(n) for n in ("total_done", "var_done", "root_done", "inv_done", "h_done",
                                "turned_done", "hi_done", "lo_done"))
        block = st.block()

        @block.sync
        def _(sp):
            sp.dma_start(g[:], rows(gain)).then_inc(g_loaded, 16)
            for t in range(TILES):
                if t >= 2:
                    sp.wait_ge(h_done, t - 1)
                sp.dma_start(x[:, t % 2, :], x_tile(t)).then_inc(x_loaded[t % 2], 16)

        @block.gpsimd
        def _(pool):
            make_identity(pool, ident, ident_done)

        @block.scalar
        def _(act):
            for t in range(TILES + 1):
                if t < TILES:
                    act.wait_ge(x_loaded[t % 2], 16 * (t // 2 + 1))
                    if t >= 1:
                        act.wait_ge(total_done, t)
                    act.activation(squares[:], x[:, t % 2, :], ACT.Square,
                                   accum_out=total[:, t:t + 1]).then_inc(total_done, 1)
                    act.wait_ge(var_done, t + 1)
                    act.activation(root[:, t:t + 1], var[:, t:t + 1], ACT.Sqrt).then_inc(root_done, 1)
                if t >= 1:
                    u = t - 1
                    act.wait_ge(turned_done, u + 1)
                    act.activation(ht_hi[:, :, u * P:(u + 1) * P], turned[:, u % 2, :, :],
                                   ACT.Copy).then_inc(hi_done, 1)

        @block.vector
        def _(dve):
            dve.wait_ge(g_loaded, 16)
            for t in range(TILES + 1):
                if t < TILES:
                    dve.wait_ge(total_done, t + 1)
                    dve.tensor_scalar(var[:, t:t + 1], total[:, t:t + 1], 1.0 / D, EPS, ALU.mult,
                                      ALU.add).then_inc(var_done, 1)
                    dve.wait_ge(root_done, t + 1)
                    dve.reciprocal(inv[:, t:t + 1], root[:, t:t + 1]).then_inc(inv_done, 1)
                    dve.wait_ge(inv_done, t + 1)
                    if t >= 2:
                        dve.wait_ge(turned_done, t - 1)
                    dve.scalar_tensor_tensor(out=h[:, t % 2, :], in0=x[:, t % 2, :],
                                             scalar=inv[:, t:t + 1], in1=g[:], op0=ALU.mult,
                                             op1=ALU.mult).then_inc(h_done, 1)
                if t >= 1:
                    u = t - 1
                    dve.wait_ge(hi_done, u + 1)
                    dve.tensor_tensor(ht_lo[:, :, u * P:(u + 1) * P], turned[:, u % 2, :, :],
                                      ht_hi[:, :, u * P:(u + 1) * P].bitcast(F32),
                                      ALU.subtract).then_inc(lo_done, 1)

        @block.tensor
        def _(pe):
            pe.wait_ge(ident_done, 2)
            for t in range(TILES):
                pe.wait_ge(h_done, t + 1)
                if t >= 2:
                    pe.wait_ge(lo_done, t - 1)
                for k in range(KT):
                    last = pe.transpose(turned[:, t % 2, k, :], h[:, t % 2, k * P:(k + 1) * P], ident[:])
                last.then_inc(turned_done, 1)


def project(nc, name, x_tile, gain, w, y):
    n = w.shape[1]
    pieces = next(c for c in range(2, 64, 2) if n % c == 0 and n // c <= 512 and n // c % 2 == 0)
    width = n // pieces
    w_v = w.rearrange("(k p) n -> p k n", p=P)
    with Stage(nc, name) as st:
        ht_hi = st.sb("ht_hi", [P, KT, TOKENS], F32R)
        ht_lo = st.sb("ht_lo", [P, KT, TOKENS], F32R)
        norm_to_columns(nc, name + "n", x_tile, gain, ht_hi, ht_lo)
        raw = st.sb("raw", [P, 2, KT, width])
        w_hi = st.sb("w_hi", [P, 2, KT, width], F32R)
        w_lo = st.sb("w_lo", [P, 2, KT, width], F32R)
        out = st.sb("out", [P, 3, width])
        acc = st.ps("acc", [P, 3, 512])
        raw_loaded = st.sems("raw_loaded", 2)
        stored = st.sems("stored", 3)
        hi_done = st.sem("hi_done")
        lo_done = st.sem("lo_done")
        mm_done = st.sem("mm_done")
        out_done = st.sem("out_done")
        block = st.block()

        @block.scalar
        def _(act):
            def load(c, s, turn):
                act.wait_ge(lo_done, c + 1)
                act.dma_start(raw[:, s], w_v[:, :, bass.ds(c * width, width)]).then_inc(raw_loaded[s], 16)

            def split(c, s, turn):
                act.wait_ge(raw_loaded[s], 16 * turn + 16)
                act.wait_ge(mm_done, TILES * c + TILES)
                act.activation(w_hi[:, s], raw[:, s], ACT.Copy).then_inc(hi_done, 1)

            load(0, 0, 0)
            with act.Fori(0, pieces // 2 - 1) as i:
                load(2 * i + 1, 1, i)
                split(2 * i, 0, i)
                load(2 * i + 2, 0, i + 1)
                split(2 * i + 1, 1, i)
            load(pieces - 1, 1, pieces // 2 - 1)
            split(pieces - 2, 0, pieces // 2 - 1)
            split(pieces - 1, 1, pieces // 2 - 1)

        @block.vector
        def _(dve):
            dve.nop().then_inc(lo_done, 2)
            dve.nop().then_inc(out_done, 3)

            def split(c, s):
                dve.wait_ge(hi_done, c + 1)
                dve.tensor_tensor(w_lo[:, s], raw[:, s], w_hi[:, s].bitcast(F32),
                                  ALU.subtract).then_inc(lo_done, 1)

            def copy_out(c, t, i):
                dve.wait_ge(mm_done, 2 * TILES + TILES * c + t + 1)
                dve.wait_ge(stored[t % 3], 16 * (3 * c + t // 3) + 16)
                dve.tensor_copy(out[:, t % 3], acc[:, t % 3, 0:width]).then_inc(out_done, 1)

            split(0, 0)
            with dve.Fori(0, pieces // 2 - 1) as i:
                for s in range(2):
                    split(2 * i + s + 1, (s + 1) % 2)
                    for t in range(TILES):
                        copy_out(2 * i + s, t, i)
            for c in (pieces - 2, pieces - 1):
                if c < pieces - 1:
                    split(c + 1, (c + 1) % 2)
                for t in range(TILES):
                    copy_out(c, t, 0)

        @block.tensor
        def _(pe):
            pe.nop().then_inc(mm_done, 2 * TILES)
            with pe.Fori(0, pieces // 2) as i:
                for s in range(2):
                    c = 2 * i + s
                    pe.wait_ge(lo_done, c + 3)
                    for t in range(TILES):
                        pe.wait_ge(out_done, TILES * c + t + 1)
                        token = slice(t * P, (t + 1) * P)
                        for k in range(KT):
                            for j, (a, b) in enumerate(((ht_hi, w_hi), (ht_hi, w_lo), (ht_lo, w_hi))):
                                last = pe.matmul(acc[:, t % 3, 0:width], a[:, k, token], b[:, s, k, :],
                                                 start=(k == 0 and j == 0), stop=(k == KT - 1 and j == 2))
                        last.then_inc(mm_done, 1)

        @block.sync
        def _(sp):
            for q in stored:
                sp.nop().then_inc(q, 16)
            with sp.Fori(0, pieces // 2) as i:
                for s in range(2):
                    c = 2 * i + s
                    for t in range(TILES):
                        sp.wait_ge(out_done, 3 + TILES * c + t + 1)
                        sp.dma_start(y[t * P:(t + 1) * P, bass.ds(c * width, width)],
                                     out[:, t % 3]).then_inc(stored[t % 3], 16)
            for q in stored:
                sp.wait_ge(q, 16 * (3 * pieces + 1))


def turn_columns(nc, name, y, groups, tables, qkt, direct, outputs):
    width = sum(n for _, n in groups)
    blocks = width // P
    heads = width // DH
    with Stage(nc, name) as st:
        z = st.sb("z", [P, 2, width])
        ident = st.sb("ident", [P, P])
        cols = st.sb("cols", [P, 2, blocks, P])
        half = (blocks + 1) // 2
        turned = st.ps("turned", [P, 2, 4 * ((half + 3) // 4), P])
        ident_done, table_loaded, direct_done = (st.sem(n) for n in ("ident_done", "table_loaded", "direct_done"))
        z_loaded, cols_stored, rows_stored = (st.sems(n, 2) for n in ("z_loaded", "cols_stored", "rows_stored"))
        cos_done, sin_done, rot_done, turned_done, cols_done = (
            st.sem(n) for n in ("cos_done", "sin_done", "rot_done", "turned_done", "cols_done"))
        if tables is not None:
            table = st.sb("table", [P, TILES, 2, DH])
            zc = st.sb("zc", [P, 2, width])
            zs = st.sb("zs", [P, 2, width])
            ready, ready_sem = zc, rot_done
        else:
            ready, ready_sem = z, None
        n_out = [len(outputs(t, ready[:, t % 2, :])) for t in range(TILES)]
        block = st.block()

        def heads_of(ap):
            return ap.rearrange("p (h d) -> p h d", d=DH)

        @block.sync
        def _(sp):
            if tables is not None:
                sp.dma_start(table[:], tables).then_inc(table_loaded, 16)
            for t in range(TILES):
                s = t % 2
                if t >= 2:
                    sp.wait_ge(turned_done, 2 * (t - 1))
                    if tables is not None:
                        sp.wait_ge(rot_done, t - 1)
                    elif sum(n_out[s:t - 1:2]):
                        sp.wait_ge(rows_stored[s], 16 * sum(n_out[s:t - 1:2]))
                at = 0
                for first, n in groups:
                    sp.dma_start(z[:, s, at:at + n], y[t * P:(t + 1) * P, first:first + n]).then_inc(z_loaded[s], 16)
                    at += n
                if t == 1:
                    for dst, src in direct:
                        sp.dma_start(dst, src).then_inc(direct_done, 16)
            sp.wait_ge(direct_done, 16 * len(direct))

        @block.gpsimd
        def _(pool):
            make_identity(pool, ident, ident_done)
            if tables is None:
                return
            pool.wait_ge(table_loaded, 16)
            for t in range(TILES):
                s = t % 2
                pool.wait_ge(z_loaded[s], 16 * len(groups) * (t // 2 + 1))
                if t >= 2:
                    pool.wait_ge(rot_done, t - 1)
                zv, sv = heads_of(z[:, s, :]), heads_of(zs[:, s, :])
                for a, b in ((0, HALF), (HALF, 0)):
                    pool.tensor_tensor(sv[:, :, a:a + HALF], zv[:, :, b:b + HALF],
                                       table[:, t, 1:2, a:a + HALF].to_broadcast([P, heads, HALF]),
                                       ALU.mult).then_inc(sin_done, 1)

        @block.vector
        def _(dve):
            if tables is not None:
                dve.wait_ge(table_loaded, 16)
                for t in range(TILES):
                    s = t % 2
                    dve.wait_ge(z_loaded[s], 16 * len(groups) * (t // 2 + 1))
                    if t >= 2:
                        dve.wait_ge(turned_done, 2 * (t - 1))
                        if sum(n_out[s:t - 1:2]):
                            dve.wait_ge(rows_stored[s], 16 * sum(n_out[s:t - 1:2]))
                    dve.tensor_tensor(heads_of(zc[:, s, :]), heads_of(z[:, s, :]),
                                      table[:, t, 0:1, :].to_broadcast([P, heads, DH]),
                                      ALU.mult).then_inc(cos_done, 1)
                    dve.wait_ge(cos_done, t + 1)
                    dve.wait_ge(sin_done, 2 * t + 2)
                    dve.tensor_tensor(zc[:, s, :], zc[:, s, :], zs[:, s, :], ALU.add).then_inc(rot_done, 1)

        @block.tensor
        def _(pe):
            pe.wait_ge(ident_done, 2)
            for t in range(TILES):
                s = t % 2
                if tables is not None:
                    pe.wait_ge(rot_done, t + 1)
                else:
                    pe.wait_ge(z_loaded[s], 16 * len(groups) * (t // 2 + 1))
                for part, (a, b) in enumerate(((0, half), (half, blocks))):
                    if t >= 1:
                        pe.wait_ge(cols_done, 2 * (t - 1) + part + 1)
                    for j in range(a, b):
                        last = pe.transpose(turned[:, part, j - a, :], ready[:, s, j * P:(j + 1) * P], ident[:])
                    last.then_inc(turned_done, 1)

        @block.scalar
        def _(act):
            q_v = qkt.rearrange("(j p) n -> p j n", p=P)
            for t in range(TILES):
                s = t % 2
                if t >= 2:
                    act.wait_ge(cols_stored[s], 16 * (t // 2))
                for part, (a, b) in enumerate(((0, half), (half, blocks))):
                    act.wait_ge(turned_done, 2 * t + part + 1)
                    act.activation(cols[:, s, a:b, :], turned[:, part, 0:b - a, :], ACT.Copy).then_inc(cols_done, 1)
                act.wait_ge(cols_done, 2 * t + 2)
                act.dma_start(q_v[:, :, t * P:(t + 1) * P], cols[:, s]).then_inc(cols_stored[s], 16)
                if tables is not None:
                    act.wait_ge(rot_done, t + 1)
                else:
                    act.wait_ge(z_loaded[s], 16 * len(groups) * (t // 2 + 1))
                for dst, src in outputs(t, ready[:, s, :]):
                    act.dma_start(dst, src).then_inc(rows_stored[s], 16)
            for s in range(2):
                act.wait_ge(cols_stored[s], 16 * len(range(s, TILES, 2)))
                if sum(n_out[s::2]):
                    act.wait_ge(rows_stored[s], 16 * sum(n_out[s::2]))


def prompt_attention(nc, name, trips, q_rows, k_rows, v_cols, o_cols, qkt, y, o, dv, window=False,
                     causal=False, sinks=None, b_lambda=None, ck8=None):
    kd = DH if ck8 is None else DH + 1
    units = 2 * TILES_P
    diff = b_lambda is not None
    first = [max(0, t - 1) if window else 0 for t in range(TILES_P)]
    count = [t + 1 - first[t] for t in range(TILES_P)]
    unit_groups, g = [], 0
    for t in range(TILES_P):
        mine = []
        for a in range(0, count[t], 4):
            mine.append((g, a, min(a + 4, count[t])))
            g += 1
        unit_groups.append(mine)
    groups = g
    assert groups % 2 == 0
    with Stage(nc, name) as st:
        qt = st.sb("qt", [kd, 2, PROMPT])
        kt = st.sb("kt", [kd, 2, PROMPT])
        v = st.sb("v", [P, 2, TILES_P, dv])
        probs = st.sb("probs", [P, 2, PROMPT])
        probs_t = st.sb("probs_t", [P, 2, TILES_P, P])
        out = st.sb("out", [P, 2, TILES_P, dv])
        ident = st.sb("ident", [P, P])
        ident_b = st.sb("ident_b", [P, P], BF16)
        mask = st.sb("mask", [P, 2 * P], BF16)
        top, neg_top = st.sb("top", [P, 2]), st.sb("neg_top", [P, 2])
        total, inv = st.sb("total", [P, 4]), st.sb("inv", [P, 2])
        scores = st.ps("scores", [P, 2, PROMPT])
        turned = st.ps("turned", [P, 2, 4, P])
        pv = st.ps("pv", [P, 2, 512])
        setup = st.sem("setup")
        loaded, stored, copied = (st.sems(n, 2) for n in ("loaded", "stored", "copied"))
        scores_done, top_done, neg_done, exp_done, turned_done, pv_done, inv_done, out_done = (
            st.sem(n) for n in ("scores_done", "top_done", "neg_done", "exp_done", "turned_done",
                                "pv_done", "inv_done", "out_done"))
        n_loads = 3 + (ck8 is not None) + (sinks is not None)
        if sinks is not None:
            sink, neg_sink = st.sb("sink", [P, 2]), st.sb("neg_sink", [P, 2])
            sink_exp = st.sb("sink_exp", [P, 4])
            neg_sink_done, sink_exp_done, total_done = (
                st.sem(n) for n in ("neg_sink_done", "sink_exp_done", "total_done"))
        if diff:
            lam = st.sb("lam", [P, 4, DH])
            lam_sum, lam_exp, neg_lam = st.sb("lam_sum", [P, 2]), st.sb("lam_exp", [P, 2]), st.sb("neg_lam", [P, 1])
            lam_loaded, lam_done, lam_exp_done = (st.sem(n) for n in ("lam_loaded", "lam_done", "lam_exp_done"))
        block = st.block()

        @block.sync
        def _(sp):
            if diff:
                sp.dma_start(lam[:], rows(b_lambda.rearrange("(a n) d -> a (n d)", a=1))).then_inc(lam_loaded, 16)
            with sp.Fori(0, trips) as i:
                for e in range(2):
                    sp.wait_ge(pv_done, units * i + TILES_P * e + TILES_P)
                    sp.dma_start(qt[0:DH, e], qkt[bass.ds(q_rows(i, e), DH), 0:PROMPT]).then_inc(loaded[e], 16)
                    sp.dma_start(kt[0:DH, e], qkt[bass.ds(k_rows(i, e), DH), 0:PROMPT]).then_inc(loaded[e], 16)
                    sp.dma_start(v[:, e], y[0:PROMPT, bass.ds(v_cols(i, e), dv)].rearrange(
                        "(t p) d -> p t d", p=P)).then_inc(loaded[e], 16)
                    if ck8 is not None:
                        sp.dma_start(kt[DH:DH + 1, e], ck8[bass.ds(2 * i + e, 1), :]).then_inc(loaded[e], 16)
                    if sinks is not None:
                        s_i = sinks[0:1, bass.ds(2 * i + e, 1)]
                        sp.dma_start(sink[:, e:e + 1], rows(s_i)).then_inc(loaded[e], 16)

        @block.gpsimd
        def _(pool):
            make_identity(pool, ident, setup)
            pool.wait_ge(setup, 2)
            pool.memset(mask[:], 0.0).then_inc(setup, 1)
            pool.wait_ge(setup, 3)
            if causal:
                pool.affine_select(out=mask[:, P:], in_=mask[:, P:], compare_op=ALU.is_ge, fill=NEG,
                                   base=0, pattern=[[-1, P]], channel_multiplier=1).then_inc(setup, 1)
            else:
                pool.memset(mask[0:CHUNK, P + CHUNK:2 * P], NEG).then_inc(setup, 1)
            pool.wait_ge(setup, 4)
            if window:
                pool.memset(mask[CHUNK:P, 0:CHUNK], NEG).then_inc(setup, 1)
            else:
                pool.nop().then_inc(setup, 1)
            pool.wait_ge(setup, 5)
            pool.tensor_copy(ident_b[:], ident[:]).then_inc(setup, 1)
            pool.wait_ge(setup, 6)
            if ck8 is not None:
                pool.memset(qt[DH:DH + 1], 1.0).then_inc(setup, 1)
            else:
                pool.nop().then_inc(setup, 1)

        def group_number(i, e, g):
            return groups * (2 * i + e) + g

        @block.tensor
        def _(pe):
            pe.nop().then_inc(pv_done, units)
            pe.wait_ge(setup, 7)

            def score(i, j):
                e, t = divmod(j, TILES_P)
                n = units * i + j
                if t == 0:
                    pe.wait_ge(loaded[e], 16 * n_loads * i + 16 * n_loads)
                pe.wait_ge(exp_done, n + 1)
                width = count[t] * P
                masked = min(2 * P if window else P, width)
                for a in range(0, width, 512):
                    b = min(a + 512, width)
                    pe.matmul(scores[:, j % 2, a:b], qt[:, e, t * P:(t + 1) * P],
                              kt[:, e, first[t] * P + a:first[t] * P + b], start=True, stop=(b < width))
                pe.matmul(scores[:, j % 2, width - masked:width], ident_b[:], mask[:, 2 * P - masked:],
                          start=False, stop=True).then_inc(scores_done, 1)

            def attend(i, j):
                e, t = divmod(j, TILES_P)
                n = units * i + j
                pe.wait_ge(exp_done, 2 + n + 1)
                for g, a, b in unit_groups[t]:
                    number = group_number(i, e, g - (g % 2))
                    pe.wait_ge(copied[g % 2], (groups // 2) * (2 * i + e) + g // 2 + 1)
                    for x in range(a, b):
                        last = pe.transpose(turned[:, g % 2, x - a, :], probs[:, j % 2, x * P:(x + 1) * P], ident[:])
                    last.then_inc(turned_done, 1)
                for g, a, b in unit_groups[t]:
                    pe.wait_ge(copied[g % 2], 1 + (groups // 2) * (2 * i + e) + g // 2 + 1)
                pe.wait_ge(out_done, n + 1)
                for x in range(count[t]):
                    last = pe.matmul(pv[:, j % 2, 0:dv], probs_t[:, j % 2, x, :], v[:, e, first[t] + x, :],
                                     start=(x == 0), stop=(x == count[t] - 1))
                last.then_inc(pv_done, 1)

            def trip(i, more):
                for j in range(units):
                    if j + 1 < units:
                        score(i, j + 1)
                    elif more:
                        score(i + 1, 0)
                    attend(i, j)

            score(0, 0)
            with pe.Fori(0, trips - 1) as i:
                trip(i, True)
            trip(trips - 1, False)

        def copy_group(eng, i, j, odd):
            e, t = divmod(j, TILES_P)
            for g, a, b in unit_groups[t]:
                if g % 2 != odd:
                    continue
                eng.wait_ge(turned_done, group_number(i, e, g) + 1)
                eng.wait_ge(pv_done, units * i + j + units - 1)
                dst, src = probs_t[:, j % 2, a:b, :], turned[:, odd, 0:b - a, :]
                if odd:
                    eng.activation(dst, src, ACT.Copy).then_inc(copied[1], 1)
                else:
                    eng.tensor_copy(dst, src).then_inc(copied[0], 1)

        @block.scalar
        def _(act):
            act.nop().then_inc(exp_done, 2)
            act.nop().then_inc(copied[1], 1)
            for q in stored:
                act.nop().then_inc(q, 16)
            if diff:
                act.wait_ge(lam_done, 2)
                act.activation(lam_exp[:], lam_sum[:], ACT.Exp).then_inc(lam_exp_done, 1)

            def exponential(i, j):
                e, t = divmod(j, TILES_P)
                n = units * i + j
                act.wait_ge(neg_done, n + 1)
                act.wait_ge(pv_done, n + units - 1)
                act.wait_ge(inv_done, n + 1)
                act.activation(probs[:, j % 2, 0:count[t] * P], scores[:, j % 2, 0:count[t] * P], ACT.Exp,
                               bias=neg_top[:, j % 2:j % 2 + 1], scale=SCALE,
                               accum_out=total[:, j % 4:j % 4 + 1]).then_inc(exp_done, 1)
                if sinks is not None:
                    act.activation(sink_exp[:, j % 4:j % 4 + 1], sink[:, e:e + 1], ACT.Exp,
                                   bias=neg_top[:, j % 2:j % 2 + 1]).then_inc(sink_exp_done, 1)

            def trip(i, more):
                for j in range(units):
                    if j + 1 < units:
                        exponential(i, j + 1)
                    elif more:
                        exponential(i + 1, 0)
                    copy_group(act, i, j, 1)
                    if j == TILES_P or j == units - 1:
                        e = j // TILES_P if j == units - 1 else 0
                        if diff and e == 0:
                            continue
                        act.wait_ge(out_done, 2 + units * i + TILES_P * (e + 1))
                        act.dma_start(o[0:PROMPT, bass.ds(o_cols(i, e), dv)].rearrange("(t p) d -> p t d", p=P),
                                      out[:, e]).then_inc(stored[e], 16)

            exponential(0, 0)
            with act.Fori(0, trips - 1) as i:
                trip(i, True)
            trip(trips - 1, False)
            act.wait_ge(stored[1], 16 * (trips + 1))
            if not diff:
                act.wait_ge(stored[0], 16 * (trips + 1))

        @block.vector
        def _(dve):
            dve.nop().then_inc(copied[0], 1)
            dve.nop().then_inc(out_done, 2)
            dve.nop().then_inc(inv_done, 4)
            if diff:
                dve.wait_ge(lam_loaded, 16)
                for x in range(2):
                    dve.tensor_tensor_reduce(lam[:, 2 * x, :], lam[:, 2 * x, :], lam[:, 2 * x + 1, :], 1.0, 0.0,
                                             ALU.mult, ALU.add, lam_sum[:, x:x + 1]).then_inc(lam_done, 1)
                dve.wait_ge(lam_exp_done, 1)
                dve.tensor_scalar(neg_lam[:], lam_exp[:, 1:2], lam_exp[:, 0:1], -LAM_INIT, ALU.subtract,
                                  ALU.add).then_inc(lam_done, 1)
                dve.wait_ge(lam_done, 3)

            def maximum(i, j):
                e, t = divmod(j, TILES_P)
                n = units * i + j
                if sinks is not None and t == 0:
                    dve.wait_ge(loaded[e], 16 * n_loads * i + 16 * n_loads)
                    dve.tensor_scalar(neg_sink[:, e:e + 1], sink[:, e:e + 1], -1.0, None,
                                      ALU.mult).then_inc(neg_sink_done, 1)
                    dve.wait_ge(neg_sink_done, 2 * i + e + 1)
                dve.wait_ge(scores_done, n + 1)
                dve.tensor_reduce(top[:, j % 2:j % 2 + 1], scores[:, j % 2, 0:count[t] * P], AX.X,
                                  ALU.max).then_inc(top_done, 1)
                dve.wait_ge(top_done, n + 1)
                if sinks is not None:
                    dve.wait_ge(sink_exp_done, n + 2 - 2 + 1)
                    dve.tensor_scalar(neg_top[:, j % 2:j % 2 + 1], top[:, j % 2:j % 2 + 1], -SCALE,
                                      neg_sink[:, e:e + 1], ALU.mult, ALU.min).then_inc(neg_done, 1)
                else:
                    dve.tensor_scalar(neg_top[:, j % 2:j % 2 + 1], top[:, j % 2:j % 2 + 1], -SCALE, None,
                                      ALU.mult).then_inc(neg_done, 1)

            def output(i, j):
                e, t = divmod(j, TILES_P)
                n = units * i + j
                total_j, inv_j = total[:, j % 4:j % 4 + 1], inv[:, j % 2:j % 2 + 1]
                per = 1
                if sinks is not None:
                    dve.wait_ge(sink_exp_done, 2 + n + 1)
                    dve.tensor_tensor(total_j, total_j, sink_exp[:, j % 4:j % 4 + 1], ALU.add).then_inc(total_done, 1)
                    dve.wait_ge(total_done, n + 1)
                dve.wait_ge(exp_done, 2 + n + 1)
                dve.wait_ge(out_done, 2 + n - 1)
                dve.reciprocal(inv_j, total_j).then_inc(inv_done, 1)
                dve.wait_ge(inv_done, 4 + n + 1)
                dve.wait_ge(pv_done, units + n + 1)
                dst, src = out[:, e, t, :], pv[:, j % 2, 0:dv]
                if diff and e == 1:
                    dve.tensor_scalar(src, src, inv_j, neg_lam[:], ALU.mult, ALU.mult).then_inc(lam_done, 1)
                    dve.wait_ge(lam_done, 3 + TILES_P * i + t + 1)
                    if t == 0:
                        dve.wait_ge(stored[1], 16 * i + 16)
                    dve.tensor_tensor(dst, src, out[:, 0, t, :], ALU.add).then_inc(out_done, 1)
                else:
                    if t == 0 and not diff:
                        dve.wait_ge(stored[e], 16 * i + 16)
                    dve.tensor_scalar(dst, src, inv_j, None, ALU.mult).then_inc(out_done, 1)

            def trip(i, more):
                for j in range(units):
                    if j + 1 < units:
                        maximum(i, j + 1)
                    elif more:
                        maximum(i + 1, 0)
                    copy_group(dve, i, j, 0)
                    output(i, j)

            if sinks is not None:
                dve.nop().then_inc(sink_exp_done, 2)
            maximum(0, 0)
            with dve.Fori(0, trips - 1) as i:
                trip(i, True)
            trip(trips - 1, False)


def strided(ap, offset, *dims):
    return bass.AP(ap.tensor, ap.offset + offset, [list(ap.ap[0])] + [list(d) for d in dims])


def sample_attention(nc, name, groups, q_first, qkt, k_cache, v_cache, k_new, v_new, o, o_first,
                     row_odd=None, b_lambda=None, neg_c=None, row_mask=None):
    diff = b_lambda is not None
    width = 4 * P
    parts, per = 4, PAST // 4 // P
    span = per * P
    keys = PAST + FRAMES
    tiles = PAST // P + 1
    pairs = 4 * groups
    bank = 512
    exp_scale = SCALE if diff else 1.0
    KG = 4 * parts + 2
    KE = KG // 2
    SG = parts + 1
    PG = [(a, min(a + 4, tiles)) for a in range(0, tiles, 4)]
    PE_, PO_ = (len(PG) + 1) // 2, len(PG) // 2
    OC = 1 if diff else 2
    with Stage(nc, name) as st:
        kc = st.sb("kc", [P, parts, per, width])
        vc = st.sb("vc", [P, parts, per, width])
        kn, vn = st.sb("kn", [P, width]), st.sb("vn", [FRAMES, width])
        kt = st.sb("kt", [P, 2, 4, span])
        ktn = st.sb("ktn", [P, 4, FRAMES])
        q_all = st.sb("q_all", [P, pairs, P])
        q_blocks = st.sb("q_blocks", [P, 4 * P])
        scores = st.sb("scores", [P, keys])
        probs = st.sb("probs", [P, keys])
        probs_t = st.sb("probs_t", [P, tiles, P])
        top, neg_top, total, inv = (st.sb(n, [P, 1]) for n in ("top", "neg_top", "total", "inv"))
        out_t = st.sb("out_t", [P, pairs, P])
        out = st.sb("out", [P, pairs * P])
        ident = st.sb("ident", [P, P])
        k_ps = st.ps("k_ps", [P, 3, bank])
        s_ps = st.ps("s_ps", [P, 2, bank])
        p_ps = st.ps("p_ps", [P, 2, bank])
        o_ps = st.ps("o_ps", [P, 4, 2, FRAMES])
        setup = st.sem("setup")
        k_loaded, v_loaded = st.sems("k_loaded", parts), st.sems("v_loaded", parts)
        (new_loaded, vnew_loaded, q_loaded, q_done, k_turned, kt_even, kt_odd, s_done, s_copied,
         top_done, neg_done, exp_done, inv_done, norm_done, p_turned, pt_even, pt_odd, pv_done,
         o_done, o_turned, out_done, stored) = (st.sem(n) for n in (
             "new_loaded", "vnew_loaded", "q_loaded", "q_done", "k_turned", "kt_even", "kt_odd",
             "s_done", "s_copied", "top_done", "neg_done", "exp_done", "inv_done", "norm_done",
             "p_turned", "pt_even", "pt_odd", "pv_done", "o_done", "o_turned", "out_done", "stored"))
        if diff:
            lam, lam_sum, lam_exp, neg_lam = (st.sb("lam", [P, 4, DH]), st.sb("lam_sum", [P, 2]),
                                              st.sb("lam_exp", [P, 2]), st.sb("neg_lam", [P, 1]))
            odd, weight = st.sb("odd", [P, 1]), st.sb("weight", [P, 1])
            o_first_head = st.sb("o_first_head", [P, 4, FRAMES])
            lam_loaded, lam_done, lam_exp_done, o_half = (
                st.sem(n) for n in ("lam_loaded", "lam_done", "lam_exp_done", "o_half"))
        else:
            bias, later = st.sb("bias", [P, keys]), st.sb("later", [P, FRAMES])
            bias_loaded, masked, later_loaded = (st.sem(n) for n in ("bias_loaded", "masked", "later_loaded"))
        block = st.block()

        def before(stream, group):
            return (stream, group - 1) if group else (stream - 1, groups - 1)

        def each_unit(eng, step, flush=None):
            for g in range(groups):
                step(0, g, g, g == 0)
            with eng.Fori(1, STREAMS) as b:
                for g in range(groups):
                    step(b, g, groups * b + g, False)
            if flush is not None:
                flush(STREAMS - 1, groups - 1, groups * STREAMS - 1)

        @block.sync
        def _(sp):
            sp.dma_start(q_all[:], qkt[q_first:q_first + pairs * P, PROMPT:TOKENS].rearrange(
                "(j p) n -> p j n", p=P)).then_inc(q_loaded, 16)
            if diff:
                sp.dma_start(lam[:], rows(b_lambda.rearrange("(a n) d -> a (n d)", a=1))).then_inc(lam_loaded, 16)
                sp.dma_start(odd[:], row_odd).then_inc(lam_loaded, 16)
            else:
                sp.dma_start(later[:], row_mask).then_inc(later_loaded, 16)
            sp.wait_ge(setup, 4)
            with sp.Fori(0, STREAMS) as b:
                for g in range(groups):
                    u = groups * b + g
                    c = slice(g * width, (g + 1) * width)
                    for x in range(parts):
                        sp.wait_ge(k_turned, KG * u + 4 * (x + 1))
                        sp.dma_start(kc[:, x], k_cache[bass.ds(b, 1), x * span:(x + 1) * span, c].rearrange(
                            "b (t p) c -> p (b t) c", p=P)).then_inc(k_loaded[x], 16)
                    sp.wait_ge(k_turned, KG * u + KG)
                    sp.dma_start(kn[0:FRAMES], k_new[bass.ds(b * FRAMES, FRAMES), c]).then_inc(new_loaded, 16)
                    if not diff:
                        sp.wait_ge(s_copied, SG * u + SG)
                        for h in range(8):
                            sp.dma_start(bias[h * FRAMES:(h + 1) * FRAMES, :],
                                         rows(neg_c[bass.ds(b * C_H + 8 * g + h, 1), :], FRAMES)
                                         ).then_inc(bias_loaded, 16)
            sp.wait_ge(out_done, 2)
            sp.dma_start(o[PROMPT:TOKENS, o_first:o_first + pairs * P], out[:]).then_inc(stored, 16)
            sp.wait_ge(stored, 16)

        @block.gpsimd
        def _(pool):
            make_identity(pool, ident, setup)
            pool.memset(q_blocks[:], 0.0).then_inc(setup, 1)
            pool.memset(kn[:], 0.0).then_inc(setup, 1)
            if not diff:
                pool.wait_ge(later_loaded, 16)
                with pool.Fori(0, STREAMS) as b:
                    for g in range(groups):
                        u = groups * b + g
                        pool.wait_ge(bias_loaded, 128 * u + 128)
                        pool.tensor_tensor(bias[:, PAST:], bias[:, PAST:], later[:], ALU.add).then_inc(masked, 1)

        @block.tensor
        def _(pe):
            pe.nop().then_inc(k_turned, KG)
            pe.nop().then_inc(s_done, SG)
            pe.nop().then_inc(p_turned, len(PG))
            pe.nop().then_inc(pv_done, 1)
            pe.wait_ge(setup, 4)

            def k_slot_free(u, r):
                back = r - 3 if r >= 3 else r - 3 + KG
                count = KE * u + back // 2 + 1 + (KE if r >= 3 else 0)
                pe.wait_ge(kt_odd if back % 2 else kt_even, count)

            def turn(u, x):
                pe.wait_ge(k_loaded[x], 16 * u + 16)
                for j in range(4):
                    r = 4 * x + j
                    k_slot_free(u, r)
                    for t in range(per):
                        last = pe.transpose(k_ps[:, r % 3, t * P:(t + 1) * P], kc[:, x, t, j * P:(j + 1) * P], ident[:])
                    last.then_inc(k_turned, 1)

            def turn_new(u):
                pe.wait_ge(new_loaded, 16 * u + 16)
                for half in range(2):
                    r = 4 * parts + half
                    k_slot_free(u, r)
                    for j in range(2):
                        last = pe.transpose(k_ps[:, r % 3, j * P:(j + 1) * P],
                                            kn[:, (2 * half + j) * P:(2 * half + j + 1) * P], ident[:])
                    last.then_inc(k_turned, 1)

            def score(u, x):
                new = x == parts
                copies = KE * u + KE + (KE if new else 2 * x + 2)
                pe.wait_ge(kt_even, copies)
                pe.wait_ge(kt_odd, copies)
                pe.wait_ge(s_copied, SG * u + SG + x - 1 if x >= 2 else SG * u + SG - x)
                for j in range(4):
                    last = pe.matmul(s_ps[:, x % 2, 0:FRAMES if new else span], q_blocks[:, j * P:(j + 1) * P],
                                     ktn[:, j, :] if new else kt[:, x % 2, j, :], start=(j == 0), stop=(j == 3))
                last.then_inc(s_done, 1)

            def k_phase(u):
                turn(u, 0)
                pe.wait_ge(q_done, 2 * u + 2)
                for x in range(1, parts):
                    turn(u, x)
                    score(u, x - 1)
                turn_new(u)
                score(u, parts - 1)
                score(u, parts)

            def pv_phase(u):
                pe.wait_ge(norm_done, u + 1)
                for gi, (a, b) in enumerate(PG):
                    if gi % 2 == 0:
                        pe.wait_ge(pt_even, PE_ * u + PE_ + (gi // 2 if gi else 0))
                    else:
                        pe.wait_ge(pt_odd, PO_ * u + PO_ + (gi - 1) // 2)
                    for t in range(a, b):
                        m = P if t < tiles - 1 else FRAMES
                        last = pe.transpose(p_ps[0:m, gi % 2, (t - a) * P:(t - a + 1) * P], probs[:, t * P:t * P + m], ident[:])
                    last.then_inc(p_turned, 1)
                pe.wait_ge(pt_even, PE_ * u + 2 * PE_)
                pe.wait_ge(pt_odd, PO_ * u + 2 * PO_)
                pe.wait_ge(o_done, OC * u + OC)
                for t in range(tiles):
                    new = t == tiles - 1
                    if new:
                        pe.wait_ge(vnew_loaded, 16 * u + 16)
                    elif t % per == 0:
                        pe.wait_ge(v_loaded[t // per], 16 * u + 16)
                    for j in range(4):
                        values = vn[:, j * P:(j + 1) * P] if new else vc[:, t // per, t % per, j * P:(j + 1) * P]
                        last = pe.matmul(o_ps[:, j].rearrange("p e f -> p (e f)"), values,
                                         probs_t[0:FRAMES if new else P, t, 32 * j:32 * j + 32],
                                         start=(t == 0 and j == 0), stop=new, skip_group_check=True)
                last.then_inc(pv_done, 1)

            def step(b, g, u, is_first):
                k_phase(u)
                if not is_first:
                    pv_phase(u - 1)

            each_unit(pe, step, lambda b, g, u: pv_phase(u))
            pe.wait_ge(o_done, OC * STREAMS * groups + OC)
            for half in range(2):
                back = KG - 3 + half
                pe.wait_ge(kt_odd if back % 2 else kt_even, KE * (STREAMS * groups + 1))
                for j in range(pairs // 2):
                    last = pe.transpose(k_ps[:, half, j * P:(j + 1) * P], out_t[:, half * pairs // 2 + j, :], ident[:])
                last.then_inc(o_turned, 1)

        def copy_kt(eng, u, r):
            x = r // 4
            eng.wait_ge(k_turned, KG * u + KG + r + 1)
            if x == parts:
                half = r - 4 * parts
                eng.wait_ge(s_done, SG * u + SG)
                dst = ktn[:, 2 * half:2 * half + 2, :]
                src = k_ps[:, r % 3, 0:2 * P].rearrange("p (j f) -> p j f", j=2)[:, :, 0:FRAMES]
            else:
                eng.wait_ge(s_done, SG * u + SG + x - 1 if x >= 2 else SG * u + x + parts - 1)
                dst, src = kt[:, x % 2, r % 4, :], k_ps[:, r % 3, :]
            if r % 2:
                eng.activation(dst, src, ACT.Copy).then_inc(kt_odd, 1)
            else:
                eng.tensor_copy(dst, src).then_inc(kt_even, 1)

        def copy_probs(eng, u, gi):
            a, b = PG[gi]
            eng.wait_ge(p_turned, len(PG) * u + len(PG) + gi + 1)
            eng.wait_ge(pv_done, u + 1)
            m = P if b < tiles else FRAMES
            dst = probs_t[0:m, a:b, :]
            src = p_ps[0:m, gi % 2, 0:(b - a) * P].rearrange("p (t q) -> p t q", q=P)
            if gi % 2:
                eng.activation(dst, src, ACT.Copy).then_inc(pt_odd, 1)
            else:
                eng.tensor_copy(dst, src).then_inc(pt_even, 1)

        @block.scalar
        def _(act):
            act.nop().then_inc(kt_odd, KE)
            act.nop().then_inc(exp_done, 1)
            act.nop().then_inc(pt_odd, PO_)
            if diff:
                act.wait_ge(lam_done, 2)
                act.activation(lam_exp[:], lam_sum[:], ACT.Exp).then_inc(lam_exp_done, 1)

            def load_v(b, g, u):
                c = slice(g * width, (g + 1) * width)
                act.wait_ge(pv_done, u + 1)
                for x in range(parts):
                    act.dma_start(vc[:, x], v_cache[bass.ds(b, 1), x * span:(x + 1) * span, c].rearrange(
                        "b (t p) c -> p (b t) c", p=P)).then_inc(v_loaded[x], 16)
                act.dma_start(vn[:], v_new[bass.ds(b * FRAMES, FRAMES), c]).then_inc(vnew_loaded, 16)

            def copy_p(u):
                for gi in range(1, len(PG), 2):
                    copy_probs(act, u, gi)

            def step(b, g, u, is_first):
                for r in range(1, KG, 2):
                    copy_kt(act, u, r)
                if not is_first:
                    copy_p(u - 1)
                act.wait_ge(neg_done, u + 1)
                act.wait_ge(p_turned, len(PG) * u + len(PG))
                act.activation(probs[:], scores[:], ACT.Exp, bias=neg_top[:], scale=exp_scale,
                               accum_out=total[:]).then_inc(exp_done, 1)
                load_v(b, g, u)

            each_unit(act, step, lambda b, g, u: copy_p(u))
            act.wait_ge(o_turned, 2)
            act.activation(out[:, pairs * P // 2:], k_ps[:, 1, 0:pairs * P // 2], ACT.Copy).then_inc(out_done, 1)

        @block.vector
        def _(dve):
            dve.nop().then_inc(kt_even, KE)
            dve.nop().then_inc(s_copied, SG)
            dve.nop().then_inc(pt_even, PE_)
            dve.nop().then_inc(o_done, OC)
            if diff:
                dve.wait_ge(lam_loaded, 32)
                for x in range(2):
                    dve.tensor_tensor_reduce(lam[:, 2 * x, :], lam[:, 2 * x, :], lam[:, 2 * x + 1, :], 1.0, 0.0,
                                             ALU.mult, ALU.add, lam_sum[:, x:x + 1]).then_inc(lam_done, 1)
                dve.wait_ge(lam_exp_done, 1)
                dve.tensor_scalar(neg_lam[:], lam_exp[:, 1:2], lam_exp[:, 0:1], -LAM_INIT - 1.0, ALU.subtract,
                                  ALU.add).then_inc(lam_done, 1)
                dve.wait_ge(lam_done, 3)
                dve.tensor_scalar(weight[:], odd[:], neg_lam[:], 1.0, ALU.mult, ALU.add).then_inc(lam_done, 1)
                dve.wait_ge(lam_done, 4)
            dve.wait_ge(setup, 4)
            dve.wait_ge(q_loaded, 16)

            def blocks(b, g, u):
                for hd in range(2):
                    part = slice(DH * hd, DH * hd + DH)
                    if hd == 0:
                        dve.wait_ge(s_done, SG * u + SG)
                    dve.tensor_scalar(strided(q_blocks[part, :], FRAMES * hd, (P + 32, 4), (1, FRAMES)),
                                      q_all[part, 4 * g:4 * g + 4, bass.ds(b * FRAMES, FRAMES)], 1.0, None,
                                      ALU.mult).then_inc(q_done, 1)

            def copy_scores(u, x):
                n = FRAMES if x == parts else span
                dst, src = scores[:, x * span:x * span + n], s_ps[:, x % 2, 0:n]
                dve.wait_ge(s_done, SG * u + SG + x + 1)
                if x == 0:
                    dve.wait_ge(exp_done, u + 1)
                    if not diff:
                        dve.wait_ge(masked, u + 1)
                if diff:
                    dve.tensor_copy(dst, src).then_inc(s_copied, 1)
                else:
                    dve.scalar_tensor_tensor(out=dst, in0=src, scalar=SCALE, in1=bias[:, x * span:x * span + n],
                                             op0=ALU.mult, op1=ALU.add).then_inc(s_copied, 1)

            def copy_out(b, g, u):
                dve.wait_ge(pv_done, u + 2)
                if diff:
                    dve.tensor_copy(o_first_head[:], o_ps[:, :, 0, :]).then_inc(o_half, 1)
                    dve.wait_ge(o_half, u + 1)
                    dve.tensor_tensor(out_t[:, 4 * g:4 * g + 4, bass.ds(b * FRAMES, FRAMES)], o_first_head[:],
                                      o_ps[:, :, 1, :], ALU.add).then_inc(o_done, 1)
                else:
                    for hd in range(2):
                        part = slice(DH * hd, DH * hd + DH)
                        dve.tensor_scalar(out_t[part, 4 * g:4 * g + 4, bass.ds(b * FRAMES, FRAMES)],
                                          o_ps[part, :, hd, :], 1.0, None, ALU.mult).then_inc(o_done, 1)

            def copy_p(u):
                for gi in range(0, len(PG), 2):
                    copy_probs(dve, u, gi)

            def step(b, g, u, is_first):
                blocks(b, g, u)
                for r in range(0, 4, 2):
                    copy_kt(dve, u, r)
                for x in range(1, parts):
                    for r in range(4 * x, 4 * x + 4, 2):
                        copy_kt(dve, u, r)
                    copy_scores(u, x - 1)
                copy_kt(dve, u, 4 * parts)
                copy_scores(u, parts - 1)
                copy_scores(u, parts)
                if not is_first:
                    copy_p(u - 1)
                dve.wait_ge(s_copied, SG * u + 2 * SG)
                dve.tensor_reduce(top[:], scores[:], AX.X, ALU.max).then_inc(top_done, 1)
                dve.wait_ge(top_done, u + 1)
                dve.tensor_scalar(neg_top[:], top[:], -exp_scale, None, ALU.mult).then_inc(neg_done, 1)
                dve.wait_ge(exp_done, u + 2)
                dve.reciprocal(inv[:], total[:]).then_inc(inv_done, 1)
                dve.wait_ge(inv_done, u + 1)
                if diff:
                    dve.tensor_scalar(probs[:], probs[:], inv[:], weight[:], ALU.mult, ALU.mult).then_inc(norm_done, 1)
                else:
                    dve.tensor_scalar(probs[:], probs[:], inv[:], None, ALU.mult).then_inc(norm_done, 1)
                if not is_first:
                    copy_out(*before(b, g), u - 1)

            def flush(b, g, u):
                copy_p(u)
                copy_out(b, g, u)

            each_unit(dve, step, flush)
            dve.wait_ge(o_turned, 1)
            dve.tensor_copy(out[:, 0:pairs * P // 2], k_ps[:, 0, 0:pairs * P // 2]).then_inc(out_done, 1)


def sample_window(nc, name, qkt, k_cache, v_cache, k_new, v_new, sinks, o):
    keys = WIN + FRAMES
    with Stage(nc, name) as st:
        kc, vc = st.sb("kc", [P, 2, P]), st.sb("vc", [P, 2, P])
        kn, vn = st.sb("kn", [FRAMES, 2, P]), st.sb("vn", [FRAMES, 2, P])
        kt = st.sb("kt", [P, 2, keys])
        q_all = st.sb("q_all", [P, A_GROUP, P])
        q_blocks = st.sb("q_blocks", [P, 2, P])
        probs, probs_t, probs_tn = st.sb("probs", [P, 2, keys]), st.sb("probs_t", [P, 2, P]), st.sb("probs_tn", [FRAMES, 2, P])
        sink, neg_sink = st.sb("sink", [P, 1]), st.sb("neg_sink", [P, 1])
        top, neg_top, total, inv, sink_exp = (st.sb(n, [P, 2]) for n in ("top", "neg_top", "total", "inv", "sink_exp"))
        out_t, out = st.sb("out_t", [P, A_GROUP, P]), st.sb("out", [P, A_KV, A_GROUP, DH])
        ident = st.sb("ident", [P, P])
        k_ps, s_ps, p_ps, o_ps = (st.ps(n, [P, 2, 512]) for n in ("k_ps", "s_ps", "p_ps", "o_ps"))
        loaded = st.sems("loaded", 2)
        (setup, q_loaded, sink_loaded, sink_done, q_done, k_turned, kt_done, s_done, top_done, neg_done,
         exp_done, sink_exp_done, total_done, inv_done, norm_done, p_turned, pt_done, pv_done, o_done,
         o_turned, out_done, stored) = (st.sem(n) for n in (
             "setup", "q_loaded", "sink_loaded", "sink_done", "q_done", "k_turned", "kt_done", "s_done",
             "top_done", "neg_done", "exp_done", "sink_exp_done", "total_done", "inv_done", "norm_done",
             "p_turned", "pt_done", "pv_done", "o_done", "o_turned", "out_done", "stored"))
        block = st.block()

        @block.sync
        def _(sp):
            for kv in range(A_KV):
                sp.dma_start(q_all[DH * kv:DH * kv + DH], qkt[QA + 256 * kv:QA + 256 * kv + 256, PROMPT:TOKENS].rearrange(
                    "(g d) n -> d g n", d=DH)).then_inc(q_loaded, 16)
            for h in range(A_Q):
                sp.dma_start(sink[h * FRAMES:(h + 1) * FRAMES], rows(sinks[0:1, h:h + 1], FRAMES)).then_inc(sink_loaded, 16)
            with sp.Fori(0, STREAMS // 2) as i:
                for s in range(2):
                    b = 2 * i + s
                    sp.wait_ge(pv_done, b + 1)
                    sp.dma_start(kc[:, s], k_cache[bass.ds(b, 1)].rearrange("b k c -> (b k) c")).then_inc(loaded[s], 16)
                    sp.dma_start(vc[:, s], v_cache[bass.ds(b, 1)].rearrange("b k c -> (b k) c")).then_inc(loaded[s], 16)
                    sp.dma_start(kn[:, s], k_new[bass.ds(b * FRAMES, FRAMES)]).then_inc(loaded[s], 16)
                    sp.dma_start(vn[:, s], v_new[bass.ds(b * FRAMES, FRAMES)]).then_inc(loaded[s], 16)
            sp.wait_ge(out_done, 1)
            sp.dma_start(o[PROMPT:TOKENS, 0:A_Q * DH], out[:].rearrange("p a g d -> p (a g d)")).then_inc(stored, 16)
            sp.wait_ge(stored, 16)

        @block.gpsimd
        def _(pool):
            make_identity(pool, ident, setup)
            pool.memset(q_blocks[:], 0.0).then_inc(setup, 1)

        @block.tensor
        def _(pe):
            pe.nop().then_inc(pv_done, 2)
            pe.wait_ge(setup, 3)
            with pe.Fori(0, STREAMS // 2) as i:
                for s in range(2):
                    b = 2 * i + s
                    pe.wait_ge(loaded[s], 64 * i + 64)
                    pe.wait_ge(kt_done, b)
                    pe.transpose(k_ps[:, s, 0:P], kc[:, s], ident[:])
                    pe.transpose(k_ps[:, s, P:keys], kn[:, s], ident[0:FRAMES, 0:FRAMES]).then_inc(k_turned, 1)
                    pe.wait_ge(kt_done, b + 1)
                    pe.wait_ge(q_done, 2 * b + 2)
                    pe.matmul(s_ps[:, s, 0:keys], q_blocks[:, s], kt[:, s], start=True, stop=True).then_inc(s_done, 1)
                    pe.wait_ge(norm_done, b + 1)
                    pe.transpose(p_ps[:, s, 0:P], probs[:, s, 0:WIN], ident[:])
                    pe.transpose(p_ps[0:FRAMES, s, P:2 * P], probs[:, s, WIN:keys], ident[:]).then_inc(p_turned, 1)
                    pe.wait_ge(pt_done, 2 * b + 2)
                    pe.wait_ge(o_done, 2 * b)
                    pe.matmul(o_ps[:, s, 0:P], vc[:, s], probs_t[:, s], start=True, stop=False)
                    pe.matmul(o_ps[:, s, 0:P], vn[:, s], probs_tn[:, s], start=False, stop=True).then_inc(pv_done, 1)
            pe.wait_ge(o_done, 2 * STREAMS)
            for g in range(A_GROUP):
                last = pe.transpose(k_ps[:, 0, g * P:(g + 1) * P], out_t[:, g, :], ident[:])
            last.then_inc(o_turned, 1)

        @block.scalar
        def _(act):
            act.wait_ge(sink_loaded, 16 * A_Q)
            with act.Fori(0, STREAMS // 2) as i:
                for s in range(2):
                    b = 2 * i + s
                    act.wait_ge(neg_done, b + 1)
                    act.activation(probs[:, s], s_ps[:, s, 0:keys], ACT.Exp, bias=neg_top[:, s:s + 1], scale=SCALE,
                                   accum_out=total[:, s:s + 1]).then_inc(exp_done, 1)
                    act.activation(sink_exp[:, s:s + 1], sink[:], ACT.Exp, bias=neg_top[:, s:s + 1]).then_inc(sink_exp_done, 1)
                    act.wait_ge(p_turned, b + 1)
                    act.activation(probs_t[:, s], p_ps[:, s, 0:P], ACT.Copy).then_inc(pt_done, 1)
                    act.activation(probs_tn[:, s], p_ps[0:FRAMES, s, P:2 * P], ACT.Copy).then_inc(pt_done, 1)

        @block.vector
        def _(dve):
            dve.wait_ge(sink_loaded, 16 * A_Q)
            dve.tensor_scalar(neg_sink[:], sink[:], -1.0, None, ALU.mult).then_inc(sink_done, 1)
            dve.wait_ge(sink_done, 1)
            dve.wait_ge(q_loaded, 32)
            dve.wait_ge(setup, 3)
            with dve.Fori(0, STREAMS // 2) as i:
                for s in range(2):
                    b = 2 * i + s
                    for kv in range(A_KV):
                        part = slice(DH * kv, DH * kv + DH)
                        dve.tensor_scalar(q_blocks[part, s, DH * kv:DH * kv + DH].rearrange("p (g f) -> p g f", f=FRAMES),
                                          q_all[part, :, bass.ds(b * FRAMES, FRAMES)], 1.0, None, ALU.mult).then_inc(q_done, 1)
                    dve.wait_ge(k_turned, b + 1)
                    dve.tensor_copy(kt[:, s], k_ps[:, s, 0:keys]).then_inc(kt_done, 1)
                    dve.wait_ge(s_done, b + 1)
                    dve.tensor_reduce(top[:, s:s + 1], s_ps[:, s, 0:keys], AX.X, ALU.max).then_inc(top_done, 1)
                    dve.wait_ge(top_done, b + 1)
                    dve.tensor_scalar(neg_top[:, s:s + 1], top[:, s:s + 1], -SCALE, neg_sink[:], ALU.mult,
                                      ALU.min).then_inc(neg_done, 1)
                    dve.wait_ge(sink_exp_done, b + 1)
                    dve.tensor_tensor(total[:, s:s + 1], total[:, s:s + 1], sink_exp[:, s:s + 1], ALU.add).then_inc(total_done, 1)
                    dve.wait_ge(total_done, b + 1)
                    dve.reciprocal(inv[:, s:s + 1], total[:, s:s + 1]).then_inc(inv_done, 1)
                    dve.wait_ge(inv_done, b + 1)
                    dve.tensor_scalar(probs[:, s], probs[:, s], inv[:, s:s + 1], None, ALU.mult).then_inc(norm_done, 1)
                    dve.wait_ge(pv_done, b + 3)
                    for kv in range(A_KV):
                        part = slice(DH * kv, DH * kv + DH)
                        dve.tensor_scalar(out_t[part, :, bass.ds(b * FRAMES, FRAMES)],
                                          o_ps[part, s, DH * kv:DH * kv + DH].rearrange("p (g f) -> p g f", f=FRAMES),
                                          1.0, None, ALU.mult).then_inc(o_done, 1)
            dve.wait_ge(o_turned, 1)
            dve.tensor_copy(out[:].rearrange("p a g d -> p g a d"),
                            k_ps[:, 0, :].rearrange("p (g a d) -> p g a d", g=A_GROUP, a=A_KV)).then_inc(out_done, 1)


def forget_values(nc, name, y, bias, cache, logf_prompt, logf_sample, ck8, neg_c):
    keys = PAST + FRAMES
    n = TILES * C_H
    with Stage(nc, name) as st:
        z, soft, low, logf = (st.sb(x, [P, TILES, C_H]) for x in ("z", "soft", "low", "logf"))
        b = st.sb("b", [P, C_H])
        past = st.sb("past", [P, PAST // P, P])
        logf_p, sum_p = st.sb("logf_p", [C_H, PROMPT]), st.sb("sum_p", [C_H, PROMPT])
        logf_s, sum_s = st.sb("logf_s", [P, keys]), st.sb("sum_s", [P, keys])
        zeros = st.sb("zeros", [P, keys])
        ident = st.sb("ident", [P, P])
        p_ps, s_ps = st.ps("p_ps", [C_H, PROMPT]), st.ps("s_ps", [P, PAST])
        (setup, loaded, past_loaded, a_done, step, logf_done, turned, copied, new_loaded, summed, scaled,
         stored, zero_done) = (st.sem(x) for x in (
             "setup", "loaded", "past_loaded", "a_done", "step", "logf_done", "turned", "copied",
             "new_loaded", "summed", "scaled", "stored", "zero_done"))
        block = st.block()

        @block.sync
        def _(sp):
            sp.dma_start(z[:], y[:, C_IN - C_H:C_IN].rearrange("(t p) h -> p t h", p=P)).then_inc(loaded, 16)
            sp.dma_start(b[:], rows(bias)).then_inc(loaded, 16)
            for s in range(STREAMS):
                sp.dma_start(past[:, :, s * C_H:(s + 1) * C_H],
                             cache[s].rearrange("(t p) h -> p t h", p=P)).then_inc(past_loaded, 16)
            sp.wait_ge(logf_done, 1)
            sp.dma_start(logf_sample, logf[:, TILES_P, :]).then_inc(stored, 16)
            sp.wait_ge(stored, 16)
            for s in range(STREAMS):
                sp.dma_start(logf_s[s * C_H:(s + 1) * C_H, PAST:],
                             logf_sample[s * FRAMES:(s + 1) * FRAMES].rearrange("f h -> h f"),
                             allow_slow_non_contiguous=True).then_inc(new_loaded, 16)
            sp.dma_start(logf_prompt.rearrange("(t p) h -> p t h", p=P), logf[:, 0:TILES_P, :]).then_inc(stored, 16)
            sp.wait_ge(scaled, 1)
            sp.dma_start(ck8, sum_p[:]).then_inc(stored, 16)
            sp.wait_ge(scaled, 2)
            sp.dma_start(neg_c, sum_s[:]).then_inc(stored, 16)
            sp.wait_ge(stored, 64)

        @block.gpsimd
        def _(pool):
            make_identity(pool, ident, setup)
            pool.memset(zeros[:], 0.0).then_inc(zero_done, 1)

        @block.vector
        def _(dve):
            dve.wait_ge(loaded, 32)
            dve.tensor_tensor(z[:], z[:], b[:].unsqueeze(1).to_broadcast([P, TILES, C_H]), ALU.add).then_inc(step, 1)
            dve.wait_ge(step, 1)
            dve.tensor_scalar(low[:], z[:], 0.0, None, ALU.min).then_inc(step, 1)
            dve.wait_ge(step, 2)
            dve.scalar_tensor_tensor(out=z[:], in0=low[:], scalar=2.0, in1=z[:], op0=ALU.mult,
                                     op1=ALU.subtract).then_inc(step, 1)
            dve.wait_ge(a_done, 2)
            dve.tensor_tensor(logf[:], low[:], soft[:], ALU.subtract).then_inc(logf_done, 1)
            dve.wait_ge(turned, 1)
            dve.tensor_copy(logf_s[:, 0:PAST], s_ps[:]).then_inc(copied, 1)
            dve.wait_ge(turned, 2)
            dve.tensor_copy(logf_p[:], p_ps[:]).then_inc(copied, 1)
            dve.wait_ge(zero_done, 1)
            dve.wait_ge(copied, 2)
            dve.tensor_tensor_scan(sum_p[:], logf_p[:], zeros[0:C_H, 0:PROMPT], 0.0, ALU.add, ALU.add).then_inc(summed, 1)
            dve.wait_ge(summed, 1)
            dve.tensor_scalar(sum_p[:], sum_p[:], -1.0 / SCALE, None, ALU.mult).then_inc(scaled, 1)
            dve.wait_ge(new_loaded, 16 * STREAMS)
            dve.tensor_tensor_scan(sum_s[:], logf_s[:], zeros[:], 0.0, ALU.add, ALU.add).then_inc(summed, 1)
            dve.wait_ge(summed, 2)
            dve.tensor_scalar(sum_s[:], sum_s[:], -1.0, None, ALU.mult).then_inc(scaled, 1)

        @block.scalar
        def _(act):
            act.wait_ge(step, 3)
            act.activation(soft[:], z[:], ACT.Exp).then_inc(a_done, 1)
            act.wait_ge(a_done, 1)
            act.activation(soft[:], soft[:], ACT.Ln, bias=1.0).then_inc(a_done, 1)

        @block.tensor
        def _(pe):
            pe.wait_ge(setup, 2)
            pe.wait_ge(past_loaded, 16 * STREAMS)
            for t in range(PAST // P):
                last = pe.transpose(s_ps[:, t * P:(t + 1) * P], past[:, t, :], ident[:])
            last.then_inc(turned, 1)
            pe.wait_ge(logf_done, 1)
            for t in range(TILES_P):
                last = pe.transpose(p_ps[:, t * P:(t + 1) * P], logf[:, t, :], ident[:])
            last.then_inc(turned, 1)


def merge(nc, name, o, w, gain, x_in, x_out, subnorm=None):
    with Stage(nc, name) as st:
        raw = st.sb("raw", [P, 2, D])
        w_hi, w_lo = st.sb("w_hi", [P, KT, D], F32R), st.sb("w_lo", [P, KT, D], F32R)
        rows_o = st.sb("rows_o", [P, 2, D])
        x = st.sb("x", [P, 2, D])
        z = st.sb("z", [P, 2, D])
        squares = st.sb("squares", [P, D])
        ot_hi, ot_lo = st.sb("ot_hi", [P, 2, KT, P], F32R), st.sb("ot_lo", [P, 2, KT, P], F32R)
        g = st.sb("g", [P, D])
        ident = st.sb("ident", [P, P])
        total, var, root, inv = (st.sb(n, [P, 2]) for n in ("total", "var", "root", "inv"))
        turned, acc = st.ps("turned", [P, 2, KT // 2, P]), st.ps("acc", [P, 2, D])
        w_loaded, o_loaded, x_loaded, z_stored = (st.sems(n, 2) for n in ("w_loaded", "o_loaded", "x_loaded", "z_stored"))
        (setup, g_loaded, whi_done, wlo_done, turned_done, hi_done, lo_done, mm_done, total_done,
         var_done, root_done, inv_done, z_done, sum_done) = (st.sem(n) for n in (
             "setup", "g_loaded", "whi_done", "wlo_done", "turned_done", "hi_done", "lo_done", "mm_done",
             "total_done", "var_done", "root_done", "inv_done", "z_done", "sum_done"))
        if subnorm is not None:
            gs = st.sb("gs", [P, P])
            sub_sq = st.sb("sub_sq", [P, B_H, P])
            sub_total, sub_root, sub_inv = (st.sb(n, [P, 2, B_H]) for n in ("sub_total", "sub_root", "sub_inv"))
            sub_step, sub_root_done, sub_done = (st.sem(n) for n in ("sub_step", "sub_root_done", "sub_done"))
        first = D - B_H * P
        block = st.block()

        def tiles(eng, body):
            with eng.Fori(0, TILES_P // 2) as i:
                for s in range(2):
                    body(2 * i + s, s, i)
            body(TILES_P, 0, TILES_P // 2)


        @block.sync
        def _(sp):
            sp.dma_start(g[:], rows(gain)).then_inc(g_loaded, 16)
            if subnorm is not None:
                sp.dma_start(gs[:], rows(subnorm)).then_inc(g_loaded, 16)
            for k in range(KT):
                if k >= 2:
                    sp.wait_ge(wlo_done, k - 1)
                sp.dma_start(raw[:, k % 2], w[k * P:(k + 1) * P]).then_inc(w_loaded[k % 2], 16)

            def body(t, s, i):
                sp.wait_ge(lo_done, 2 * t + 2)
                sp.dma_start(rows_o[:, s], o[bass.ds(t * P, P)]).then_inc(o_loaded[s], 16)
                sp.wait_ge(sum_done, t + 1)
                sp.dma_start(x[:, s], x_in[bass.ds(t * P, P)]).then_inc(x_loaded[s], 16)

            tiles(sp, body)

        @block.gpsimd
        def _(pool):
            make_identity(pool, ident, setup)
            pool.nop().then_inc(sum_done, 2)

            def body(t, s, i):
                pool.wait_ge(x_loaded[s], 16 * i + 16)
                pool.wait_ge(z_done, t + 3)
                pool.tensor_tensor(z[:, s], z[:, s], x[:, s], ALU.add).then_inc(sum_done, 1)

            tiles(pool, body)

        @block.tensor
        def _(pe):
            pe.nop().then_inc(mm_done, 2)
            pe.wait_ge(setup, 2)

            def body(t, s, i):
                if subnorm is not None:
                    pe.wait_ge(sub_done, B_H * t + B_H)
                pe.wait_ge(o_loaded[s], 16 * i + 16)
                for half in range(2):
                    pe.wait_ge(lo_done, 2 * t + half + 3)
                    for k in range(KT // 2):
                        c = (half * KT // 2 + k) * P
                        last = pe.transpose(turned[:, half, k, :], rows_o[:, s, c:c + P], ident[:])
                    last.then_inc(turned_done, 1)
                pe.wait_ge(lo_done, 2 * t + 6)
                pe.wait_ge(z_done, t + 1)
                for half in range(2):
                    for k in range(KT):
                        for j, (a, b) in enumerate(((ot_hi, w_hi), (ot_hi, w_lo), (ot_lo, w_hi))):
                            last = pe.matmul(acc[:, s, half * 512:half * 512 + 512], a[:, s, k, :],
                                             b[:, k, half * 512:half * 512 + 512],
                                             start=(k == 0 and j == 0), stop=(k == KT - 1 and j == 2))
                last.then_inc(mm_done, 1)

            pe.wait_ge(wlo_done, KT)
            tiles(pe, body)

        @block.scalar
        def _(act):
            for q in z_stored:
                act.nop().then_inc(q, 16)
            for k in range(KT):
                act.wait_ge(w_loaded[k % 2], 16 * (k // 2 + 1))
                act.activation(w_hi[:, k], raw[:, k % 2], ACT.Copy).then_inc(whi_done, 1)

            def body(t, s, i):
                if subnorm is not None:
                    act.wait_ge(sub_step, 4 * t + 3)
                    act.activation(sub_root[:, s], sub_total[:, s], ACT.Sqrt).then_inc(sub_root_done, 1)
                for half in range(2):
                    act.wait_ge(turned_done, 2 * t + half + 1)
                    act.wait_ge(mm_done, t + 1)
                    act.activation(ot_hi[:, s, half * KT // 2:(half + 1) * KT // 2], turned[:, half],
                                   ACT.Copy).then_inc(hi_done, 1)
                act.wait_ge(mm_done, t + 3)
                act.wait_ge(total_done, t)
                act.activation(squares[:], acc[:, s], ACT.Square, accum_out=total[:, s:s + 1]).then_inc(total_done, 1)
                act.wait_ge(var_done, t + 1)
                act.activation(root[:, s:s + 1], var[:, s:s + 1], ACT.Sqrt).then_inc(root_done, 1)
                act.wait_ge(sum_done, t + 3)
                act.dma_start(x_out(t), z[:, s]).then_inc(z_stored[s], 16)

            tiles(act, body)
            act.wait_ge(z_stored[0], 16 * (TILES_P // 2 + 2))
            act.wait_ge(z_stored[1], 16 * (TILES_P // 2 + 1))

        @block.vector
        def _(dve):
            dve.nop().then_inc(lo_done, 4)
            dve.nop().then_inc(z_done, 2)
            for k in range(KT):
                dve.wait_ge(whi_done, k + 1)
                dve.tensor_tensor(w_lo[:, k], raw[:, k % 2], w_hi[:, k].bitcast(F32), ALU.subtract).then_inc(wlo_done, 1)
            dve.wait_ge(g_loaded, 16 if subnorm is None else 32)

            def body(t, s, i):
                if subnorm is not None:
                    heads = rows_o[:, s, first:].rearrange("p (h c) -> p h c", h=B_H)
                    dve.wait_ge(o_loaded[s], 16 * i + 16)
                    dve.tensor_tensor(sub_sq[:], heads, heads, ALU.mult).then_inc(sub_step, 1)
                    dve.wait_ge(sub_step, 4 * t + 1)
                    dve.tensor_reduce(sub_total[:, s], sub_sq[:], AX.X, ALU.add).then_inc(sub_step, 1)
                    dve.wait_ge(sub_step, 4 * t + 2)
                    scale = 1.0 / (1.0 - LAM_INIT) ** 2
                    dve.tensor_scalar(sub_total[:, s], sub_total[:, s], scale / P, scale * EPS, ALU.mult,
                                      ALU.add).then_inc(sub_step, 1)
                    dve.wait_ge(sub_root_done, t + 1)
                    dve.reciprocal(sub_inv[:, s], sub_root[:, s]).then_inc(sub_step, 1)
                    dve.wait_ge(sub_step, 4 * t + 4)
                    for h in range(B_H):
                        part = rows_o[:, s, first + h * P:first + (h + 1) * P]
                        dve.scalar_tensor_tensor(out=part, in0=part, scalar=sub_inv[:, s, h:h + 1], in1=gs[:],
                                                 op0=ALU.mult, op1=ALU.mult).then_inc(sub_done, 1)
                for half in range(2):
                    dve.wait_ge(hi_done, 2 * t + half + 1)
                    k = slice(half * KT // 2, (half + 1) * KT // 2)
                    dve.tensor_tensor(ot_lo[:, s, k], turned[:, half], ot_hi[:, s, k].bitcast(F32),
                                      ALU.subtract).then_inc(lo_done, 1)
                dve.wait_ge(total_done, t + 1)
                dve.tensor_scalar(var[:, s:s + 1], total[:, s:s + 1], 1.0 / D, EPS, ALU.mult, ALU.add).then_inc(var_done, 1)
                dve.wait_ge(root_done, t + 1)
                dve.reciprocal(inv[:, s:s + 1], root[:, s:s + 1]).then_inc(inv_done, 1)
                dve.wait_ge(inv_done, t + 1)
                dve.wait_ge(z_stored[s], 16 * i + 16)
                dve.scalar_tensor_tensor(out=z[:, s], in0=acc[:, s], scalar=inv[:, s:s + 1], in1=g[:],
                                         op0=ALU.mult, op1=ALU.mult).then_inc(z_done, 1)

            tiles(dve, body)


def feed_forward(nc, name, x_in, gain_in, w_in, w_out, gain_out, x_out):
    pieces = D_FF // P
    groups, gw = 3, TOKENS // 3
    with Stage(nc, name) as st:
        y = st.sb("y", [P, TILES, D])
        g_in = w_in.rearrange("(k p) (u n) -> p k u n", p=P, u=2)
        w_out_v = w_out.rearrange("(f p) n -> p f n", p=P)
        with Stage(nc, name + "m") as sm:
            ht_hi = sm.sb("ht_hi", [P, KT, TOKENS], F32R)
            ht_lo = sm.sb("ht_lo", [P, KT, TOKENS], F32R)
            norm_to_columns(nc, name + "n", lambda t: x_in[t * P:(t + 1) * P], gain_in, ht_hi, ht_lo)
            raw = sm.sb("raw", [P, 2, KT, 2, P])
            w_hi, w_lo = sm.sb("w_hi", [P, 2, KT, 2, P], F32R), sm.sb("w_lo", [P, 2, KT, 2, P], F32R)
            raw_o = sm.sb("raw_o", [P, 2, D])
            wo_hi, wo_lo = sm.sb("wo_hi", [P, 2, D], F32R), sm.sb("wo_lo", [P, 2, D], F32R)
            act_hi, act_lo = sm.sb("act_hi", [P, 2, TOKENS], F32R), sm.sb("act_lo", [P, 2, TOKENS], F32R)
            silu, prod = sm.sb("silu", [P, 2, gw]), sm.sb("prod", [P, 2, gw])
            gate, up = sm.ps("gate", [P, 3, 512]), sm.ps("up", [P, 3, 512])
            down = sm.ps("down", [P, 2, 512])
            raw_loaded = sm.sems("raw_loaded", 2)
            (ol_loaded, hi_done, lo_done, up_done, silu_done, prod_done, acthi_done, actlo_done,
             ohi_done, olo_done, down_done, added, zeroed) = (sm.sem(n) for n in (
                 "ol_loaded", "hi_done", "lo_done", "up_done", "silu_done", "prod_done", "acthi_done",
                 "actlo_done", "ohi_done", "olo_done", "down_done", "added", "zeroed"))
            outs = 2 * TILES
            block = sm.block()


            @block.sync
            def _(sp):
                with sp.Fori(0, pieces // 2) as i:
                    for s in range(2):
                        f = 2 * i + s
                        sp.wait_ge(lo_done, f + 1)
                        for u in range(2):
                            sp.dma_start(raw[:, s, :, u, :], g_in[:, :, u, bass.ds(f * P, P)]).then_inc(raw_loaded[s], 16)
                    sp.wait_ge(olo_done, i + 1)
                    sp.dma_start(raw_o[:], w_out_v[:, bass.ds(2 * i, 2), :]).then_inc(ol_loaded, 16)

            @block.scalar
            def _(act):
                def split_in(i, s):
                    act.wait_ge(raw_loaded[s], 32 * i + 32)
                    act.wait_ge(up_done, 3 * (2 * i + s) + 3)
                    act.activation(w_hi[:, s], raw[:, s], ACT.Copy).then_inc(hi_done, 1)

                def silus(i, s):
                    f = 2 * i + s
                    for q in range(groups):
                        m = 3 * f + q
                        act.wait_ge(up_done, 6 + m + 1)
                        b = (3 * s + q) % 2
                        act.wait_ge(actlo_done, m + 1)
                        act.activation(silu[:, b], gate[:, q, 0:gw], ACT.Silu).then_inc(silu_done, 1)
                        act.wait_ge(prod_done, 3 + m + 1)
                        act.wait_ge(down_done, outs * i + outs)
                        act.activation(act_hi[:, s, q * gw:(q + 1) * gw], prod[:, b], ACT.Copy).then_inc(acthi_done, 1)

                def pair(i, more):
                    split_in(i, 1)
                    act.wait_ge(ol_loaded, 16 * i + 16)
                    act.wait_ge(down_done, outs * i + outs)
                    act.activation(wo_hi[:], raw_o[:], ACT.Copy).then_inc(ohi_done, 1)
                    silus(i, 0)
                    if more:
                        split_in(i + 1, 0)
                    silus(i, 1)

                split_in(0, 0)
                with act.Fori(0, pieces // 2 - 1) as i:
                    pair(i, True)
                pair(pieces // 2 - 1, False)

            @block.vector
            def _(dve):
                dve.nop().then_inc(lo_done, 2)
                dve.nop().then_inc(prod_done, 3)
                dve.nop().then_inc(actlo_done, 2)
                dve.nop().then_inc(olo_done, 1)
                dve.nop().then_inc(added, 2)

                def split_in(i, s):
                    dve.wait_ge(hi_done, 2 * i + s + 1)
                    dve.tensor_tensor(w_lo[:, s], raw[:, s], w_hi[:, s].bitcast(F32), ALU.subtract).then_inc(lo_done, 1)

                def products(i, s):
                    f = 2 * i + s
                    for q in range(groups):
                        m = 3 * f + q
                        b = (3 * s + q) % 2
                        dve.wait_ge(silu_done, m + 1)
                        dve.tensor_tensor(prod[:, b], silu[:, b], up[:, q, 0:gw], ALU.mult).then_inc(prod_done, 1)
                        dve.wait_ge(acthi_done, m + 1)
                        part = slice(q * gw, (q + 1) * gw)
                        dve.tensor_tensor(act_lo[:, s, part], prod[:, b], act_hi[:, s, part].bitcast(F32),
                                          ALU.subtract).then_inc(actlo_done, 1)

                def pair(i, more):
                    split_in(i, 1)
                    dve.wait_ge(ohi_done, i + 1)
                    dve.tensor_tensor(wo_lo[:], raw_o[:], wo_hi[:].bitcast(F32), ALU.subtract).then_inc(olo_done, 1)
                    products(i, 0)
                    if more:
                        split_in(i + 1, 0)
                    products(i, 1)
                    for t in range(TILES):
                        for half in range(2):
                            d = outs * i + 2 * t + half
                            part = y[:, t, half * 512:(half + 1) * 512]
                            dve.wait_ge(down_done, outs + d + 1)
                            dve.wait_ge(added, 2 + outs * i)
                            dve.tensor_tensor(part, part, down[:, half, :], ALU.add).then_inc(added, 1)

                dve.wait_ge(zeroed, TILES)
                split_in(0, 0)
                with dve.Fori(0, pieces // 2 - 1) as i:
                    pair(i, True)
                pair(pieces // 2 - 1, False)

            @block.gpsimd
            def _(pool):
                for t in range(TILES):
                    pool.memset(y[:, t], 0.0).then_inc(zeroed, 1)

            @block.tensor
            def _(pe):
                pe.nop().then_inc(up_done, 6)
                pe.nop().then_inc(down_done, outs)
                with pe.Fori(0, pieces // 2) as i:
                    for s in range(2):
                        f = 2 * i + s
                        pe.wait_ge(lo_done, 2 + f + 1)
                        for q in range(groups):
                            pe.wait_ge(prod_done, 3 * f + q + 1)
                            token = slice(q * gw, (q + 1) * gw)
                            for u, acc in enumerate((gate, up)):
                                for k in range(KT):
                                    for j, (a, b) in enumerate(((w_hi, ht_hi), (w_hi, ht_lo), (w_lo, ht_hi))):
                                        last = pe.matmul(acc[:, q, 0:gw], a[:, s, k, u, :], b[:, k, token],
                                                         start=(k == 0 and j == 0), stop=(k == KT - 1 and j == 2))
                            last.then_inc(up_done, 1)
                    pe.wait_ge(olo_done, 1 + i + 1)
                    for t in range(TILES):
                        if t * P % gw == 0:
                            pe.wait_ge(actlo_done, 2 + 6 * i + 3 + t * P // gw + 1)
                        for half in range(2):
                            pe.wait_ge(added, outs * i + 2 * t + half + 1)
                            n = 0
                            for s in range(2):
                                for a, b in ((act_hi, wo_hi), (act_hi, wo_lo), (act_lo, wo_hi)):
                                    last = pe.matmul(down[:, half, :], a[:, s, t * P:(t + 1) * P],
                                                     b[:, s, half * 512:(half + 1) * 512], start=(n == 0), stop=(n == 5))
                                    n += 1
                            last.then_inc(down_done, 1)

        finish_rows(nc, name + "f", y, gain_out, x_in, x_out)


def finish_rows(nc, name, y, gain, x_in, x_out):
    with Stage(nc, name) as st:
        x, z = st.sb("x", [P, 2, D]), st.sb("z", [P, 2, D])
        squares, g = st.sb("squares", [P, D]), st.sb("g", [P, D])
        total, var, root, inv = (st.sb(n, [P, TILES]) for n in ("total", "var", "root", "inv"))
        x_loaded, stored = st.sems("x_loaded", 2), st.sems("stored", 2)
        g_loaded, total_done, var_done, root_done, inv_done, z_done, sum_done = (st.sem(n) for n in (
            "g_loaded", "total_done", "var_done", "root_done", "inv_done", "z_done", "sum_done"))
        block = st.block()

        @block.sync
        def _(sp):
            sp.dma_start(g[:], rows(gain)).then_inc(g_loaded, 16)
            for t in range(TILES):
                if t >= 2:
                    sp.wait_ge(sum_done, t - 1)
                sp.dma_start(x[:, t % 2], x_in[t * P:(t + 1) * P]).then_inc(x_loaded[t % 2], 16)

        @block.scalar
        def _(act):
            for t in range(TILES):
                if t >= 1:
                    act.wait_ge(total_done, t)
                act.activation(squares[:], y[:, t], ACT.Square, accum_out=total[:, t:t + 1]).then_inc(total_done, 1)
            act.wait_ge(var_done, 1)
            act.activation(root[:], var[:], ACT.Sqrt).then_inc(root_done, 1)
            for t in range(TILES):
                act.wait_ge(sum_done, t + 1)
                act.dma_start(x_out(t), z[:, t % 2]).then_inc(stored[t % 2], 16)
            for s in range(2):
                act.wait_ge(stored[s], 16 * len(range(s, TILES, 2)))

        @block.vector
        def _(dve):
            dve.wait_ge(total_done, TILES)
            dve.tensor_scalar(var[:], total[:], 1.0 / D, EPS, ALU.mult, ALU.add).then_inc(var_done, 1)
            dve.wait_ge(root_done, 1)
            dve.reciprocal(inv[:], root[:]).then_inc(inv_done, 1)
            dve.wait_ge(inv_done, 1)
            dve.wait_ge(g_loaded, 16)
            for t in range(TILES):
                if t >= 2:
                    dve.wait_ge(stored[t % 2], 16 * (t // 2))
                dve.scalar_tensor_tensor(out=z[:, t % 2], in0=y[:, t], scalar=inv[:, t:t + 1], in1=g[:],
                                         op0=ALU.mult, op1=ALU.mult).then_inc(z_done, 1)

        @block.gpsimd
        def _(pool):
            for t in range(TILES):
                pool.wait_ge(x_loaded[t % 2], 16 * (t // 2 + 1))
                pool.wait_ge(z_done, t + 1)
                pool.tensor_tensor(z[:, t % 2], z[:, t % 2], x[:, t % 2], ALU.add).then_inc(sum_done, 1)


def rope_table():
    prompt = np.arange(PROMPT)
    samples = np.tile(PAST + np.arange(FRAMES), STREAMS)
    pos = np.concatenate([prompt, samples]).astype(np.float32)
    freq = np.float32(10000.0) ** (-np.arange(HALF, dtype=np.float32) / np.float32(HALF))
    angle = pos[:, None] * freq.astype(np.float32)[None]
    cos, sin = np.cos(angle), np.sin(angle)
    table = np.stack([np.concatenate([cos, cos], 1), np.concatenate([-sin, sin], 1)], 1)
    return np.ascontiguousarray(table.reshape(TILES, P, 2, DH).transpose(1, 0, 2, 3).astype(np.float32))


def frame_mask():
    frame = np.arange(P) % FRAMES
    return np.where(np.arange(FRAMES)[None] <= frame[:, None], 0.0, NEG).astype(np.float32)


def odd_heads():
    return ((np.arange(P) // FRAMES) % 2).astype(np.float32)[:, None]


def build(nc, a, out):
    x0, x1, x2, x3 = (nc.dram_tensor(f"x{i}", (TOKENS, D), F32, kind="Internal").ap() for i in range(4))
    y_ab = nc.dram_tensor("y_ab", (TOKENS, AB_IN), F32, kind="Internal").ap()
    y_c = nc.dram_tensor("y_c", (TOKENS, C_IN), F32, kind="Internal").ap()
    qkt_ab = nc.dram_tensor("qkt_ab", (13 * P, TOKENS), F32, kind="Internal").ap()
    qkt_c = nc.dram_tensor("qkt_c", (2 * D, TOKENS), F32, kind="Internal").ap()
    o_ab, o_c = (nc.dram_tensor(n, (TOKENS, D), F32, kind="Internal").ap() for n in ("o_ab", "o_c"))
    ck8 = nc.dram_tensor("ck8", (C_H, PROMPT), F32, kind="Internal").ap()
    neg_c = nc.dram_tensor("neg_c", (P, PAST + FRAMES), F32, kind="Internal").ap()

    xp, xs = a["x_prompt"][0], a["x_sample"].rearrange("s f d -> (s f) d")
    gains = a["norm_gains"]

    def gain(layer, which):
        return gains[layer, which:which + 1, :]

    def flat(ap):
        return ap[0].rearrange("s t h d -> (s t) (h d)")

    def by_stream(ap):
        return ap[0].rearrange("s t h d -> s t (h d)")

    samples = slice(PROMPT, TOKENS)

    project(nc, "ab", lambda t: xp[t * P:(t + 1) * P] if t < TILES_P else xs, gain(0, 0), a["w_ab_in"][0], y_ab)
    keep = WIN - FRAMES
    direct = [
        (x0[0:PROMPT], xp), (x0[samples], xs),
        (flat(out["a_v_prompt"]), y_ab[PROMPT - WIN:PROMPT, VA:QB]),
        (flat(out["b_v_prompt"]), y_ab[0:PROMPT, VB:]),
        (flat(out["b_v_sample"]), y_ab[samples, VB:]),
        (by_stream(out["a_k_sample"])[:, 0:keep], by_stream(a["cache_a_k"])[:, FRAMES:]),
        (by_stream(out["a_v_sample"])[:, 0:keep], by_stream(a["cache_a_v"])[:, FRAMES:]),
        (by_stream(out["a_v_sample"])[:, keep:], y_ab[samples, VA:QB].rearrange("(s f) c -> s f c", f=FRAMES)),
    ]
    k_a = (KA, KA + A_KV * DH)
    k_b = (13 * P - 2 * B_H * DH, 13 * P)
    ka_new = nc.dram_tensor("ka_new", (P, A_KV * DH), F32, kind="Internal").ap()

    def rotated(t, z):
        z_a, z_b = z[:, k_a[0]:k_a[1]], z[:, k_b[0]:k_b[1]]
        if t == TILES_P:
            return [(flat(out["b_k_sample"]), z_b), (ka_new, z_a)] + [
                (out["a_k_sample"][0, s, keep:].rearrange("f h d -> f (h d)"), z_a[s * FRAMES:(s + 1) * FRAMES])
                for s in range(STREAMS)]
        res = [(flat(out["b_k_prompt"])[t * P:(t + 1) * P], z_b)]
        if t == TILES_P - 1:
            res.append((flat(out["a_k_prompt"]), z_a))
        return res

    turn_columns(nc, "abt", y_ab, [(QA, VA), (QB, VB - QB)], a["rope_table"], qkt_ab, direct, rotated)
    prompt_attention(nc, "pa", A_Q // 2, lambda i, e: (2 * i + e) * DH, lambda i, e: KA + (i // 2) * DH,
                     lambda i, e: VA + (i // 2) * DH, lambda i, e: (2 * i + e) * DH, qkt_ab, y_ab, o_ab, DH,
                     window=True, sinks=a["a_sinks"])
    q_b, kt_b = VA, k_b[0]
    prompt_attention(nc, "pb", B_H, lambda i, e: q_b + (2 * i + e) * DH, lambda i, e: kt_b + (2 * i + e) * DH,
                     lambda i, e: VB + i * P, lambda i, e: A_Q * DH + i * P, qkt_ab, y_ab, o_ab, P,
                     b_lambda=a["b_lambda"][0])
    sample_window(nc, "sa", qkt_ab, by_stream(a["cache_a_k"]), by_stream(a["cache_a_v"]), ka_new,
                  y_ab[samples, VA:QB], a["a_sinks"], o_ab)
    sample_attention(nc, "sb", 1, q_b, qkt_ab, by_stream(a["cache_b_k"]), by_stream(a["cache_b_v"]),
                     flat(out["b_k_sample"]), y_ab[samples, VB:], o_ab, A_Q * DH,
                     row_odd=a["odd_heads"], b_lambda=a["b_lambda"][0])
    merge(nc, "abm", o_ab, a["w_ab_out"][0], gain(0, 1), x0, lambda t: x1[bass.ds(t * P, P)], subnorm=a["b_subln"])
    feed_forward(nc, "f0", x1, gain(0, 2), a["w_ffn_in"][0], a["w_ffn_out"][0], gain(0, 3),
                 lambda t: x2[t * P:(t + 1) * P])

    project(nc, "c", lambda t: x2[t * P:(t + 1) * P], gain(1, 0), a["w_c_in"][0], y_c)
    direct = [(flat(out["c_k_prompt"]), y_c[0:PROMPT, D:2 * D]), (flat(out["c_k_sample"]), y_c[samples, D:2 * D]),
              (flat(out["c_v_prompt"]), y_c[0:PROMPT, 2 * D:3 * D]), (flat(out["c_v_sample"]), y_c[samples, 2 * D:3 * D])]
    turn_columns(nc, "ct", y_c, [(0, 2 * D)], None, qkt_c, direct, lambda t, z: [])
    forget_values(nc, "cf", y_c, a["c_forget_bias"], a["cache_c_logf"][0], out["c_logf_prompt"][0, 0],
                  out["c_logf_sample"][0].rearrange("s f h -> (s f) h"), ck8, neg_c)
    prompt_attention(nc, "pc", C_H // 2, lambda i, e: (2 * i + e) * DH, lambda i, e: D + (2 * i + e) * DH,
                     lambda i, e: 2 * D + (2 * i + e) * DH, lambda i, e: (2 * i + e) * DH, qkt_c, y_c, o_c, DH,
                     causal=True, ck8=ck8)
    sample_attention(nc, "sc", 2, 0, qkt_c, by_stream(a["cache_c_k"]), by_stream(a["cache_c_v"]),
                     y_c[samples, D:2 * D], y_c[samples, 2 * D:3 * D], o_c, 0, neg_c=neg_c, row_mask=a["frame_mask"])
    merge(nc, "cm", o_c, a["w_c_out"][0], gain(1, 1), x2, lambda t: x3[bass.ds(t * P, P)])
    yp, ys = out["y_prompt"][0], out["y_sample"].rearrange("s f d -> (s f) d")
    feed_forward(nc, "f1", x3, gain(1, 2), a["w_ffn_in"][1], a["w_ffn_out"][1], gain(1, 3),
                 lambda t: yp[t * P:(t + 1) * P] if t < TILES_P else ys)


INPUTS = ["x_prompt", "x_sample", "cache_a_k", "cache_a_v", "cache_b_k", "cache_b_v", "cache_c_k",
          "cache_c_v", "cache_c_logf", "norm_gains", "w_ab_in", "w_ab_out", "a_sinks", "b_lambda",
          "b_subln", "w_c_in", "c_forget_bias", "w_c_out", "w_ffn_in", "w_ffn_out"]
OUTPUTS = [
    ("y_prompt", (1, PROMPT, D)), ("y_sample", (STREAMS, FRAMES, D)),
    ("a_k_prompt", (1, 1, WIN, A_KV, DH)), ("a_v_prompt", (1, 1, WIN, A_KV, DH)),
    ("b_k_prompt", (1, 1, PROMPT, 2 * B_H, DH)), ("b_v_prompt", (1, 1, PROMPT, B_H, 2 * DH)),
    ("c_k_prompt", (1, 1, PROMPT, C_H, DH)), ("c_v_prompt", (1, 1, PROMPT, C_H, DH)),
    ("c_logf_prompt", (1, 1, PROMPT, C_H)),
    ("a_k_sample", (1, STREAMS, WIN, A_KV, DH)), ("a_v_sample", (1, STREAMS, WIN, A_KV, DH)),
    ("b_k_sample", (1, STREAMS, FRAMES, 2 * B_H, DH)), ("b_v_sample", (1, STREAMS, FRAMES, B_H, 2 * DH)),
    ("c_k_sample", (1, STREAMS, FRAMES, C_H, DH)), ("c_v_sample", (1, STREAMS, FRAMES, C_H, DH)),
    ("c_logf_sample", (1, STREAMS, FRAMES, C_H)),
]


def kernel(**inputs):
    import concourse.bacc as bacc
    from concourse.bass_utils import run_bass_kernel_spmd

    nc = bacc.Bacc("TRN2", target_bir_lowering=False, num_devices=1)
    arrays = {name: np.ascontiguousarray(inputs[name]) for name in INPUTS}
    arrays.update(rope_table=rope_table(), frame_mask=frame_mask(), odd_heads=odd_heads())
    a = {n: nc.dram_tensor(f"in_{n}", x.shape, F32, kind="ExternalInput").ap() for n, x in arrays.items()}
    out = {n: nc.dram_tensor(f"out_{n}", shape, F32, kind="ExternalOutput").ap() for n, shape in OUTPUTS}
    build(nc, a, out)
    result = run_bass_kernel_spmd(nc, [{f"in_{n}": x for n, x in arrays.items()}], core_ids=[0])
    return tuple(result.results[0][f"out_{n}"] for n, _ in OUTPUTS)
```

```python
import math
from contextlib import ExitStack, contextmanager

import numpy as np

import concourse.bass as bass
from concourse import mybir

F32 = mybir.dt.float32
F32R = mybir.dt.float32r
BF16 = mybir.dt.bfloat16
ALU = mybir.AluOpType
ACT = mybir.ActivationFunctionType
AX = mybir.AxisListType

P = 128
D = 1024
KT = D // P
PROMPT = 1024
TILES_P = PROMPT // P
TILES = TILES_P + 1
TOKENS = TILES * P
STREAMS, FRAMES, PAST = 8, 16, 2048
DH = 64
HALF = DH // 2
CHUNK = 64
SCALE = DH ** -0.5
EPS = 1e-6
NEG = -1e30
A_Q, A_KV, B_H, C_H = 8, 2, 4, 16
A_GROUP = A_Q // A_KV
AB_IN = A_Q * DH + 2 * A_KV * DH + 3 * 2 * B_H * DH
C_IN = 3 * D + C_H
D_FF = 2816
WIN = 128
LAM_INIT = 0.8 - 0.6 * math.exp(0.0)
QA, KA, VA, QB, KB, VB = 0, 512, 640, 768, 1280, 1792


def rows(ap, count=P):
    return bass.AP(ap.tensor, ap.offset, [[0, count]] + [list(x) for x in ap.ap[1:]])


class Stage:

    def __init__(self, nc, name):
        self.nc, self.name, self.ctx = nc, name, ExitStack()

    def __enter__(self):
        self.before = self.nc.snapshot_sems()
        return self

    def __exit__(self, *exc):
        self.ctx.close()
        self.nc.clear_and_free_semaphores(self.nc.allocated_since(self.before))
        self.nc.all_engine_barrier()

    def sb(self, name, shape, dtype=F32):
        return self.ctx.enter_context(self.nc.sbuf_tensor(f"{self.name}_{name}", shape, dtype))

    def ps(self, name, shape, dtype=F32):
        return self.ctx.enter_context(self.nc.psum_tensor(f"{self.name}_{name}", shape, dtype))

    def sem(self, name):
        return self.nc.alloc_semaphore(f"{self.name}_{name}")

    def sems(self, name, n):
        return [self.sem(f"{name}{k}") for k in range(n)]

    def block(self):
        return self.ctx.enter_context(self.nc.Block())


def make_identity(pool, ident, done):
    pool.memset(ident[:], 0.0).then_inc(done, 1)
    pool.wait_ge(done, 1)
    pool.affine_select(out=ident[:], in_=ident[:], compare_op=ALU.not_equal, fill=1.0, base=0,
                       pattern=[[-1, P]], channel_multiplier=1).then_inc(done, 1)


def inverse_root(pool, total, scale, bias, minus_half, out, done, before):
    pool.tensor_scalar(total, total, scale, bias, ALU.mult, ALU.add).then_inc(done, 1)
    pool.wait_ge(done, before + 1)
    pool.tensor_tensor(out, total, minus_half, ALU.pow).then_inc(done, 1)


def norm_to_columns(nc, name, x_tile, gain, ht_hi, ht_lo):
    slots = 4
    with Stage(nc, name) as st:
        x = st.sb("x", [P, slots, D])
        h = st.sb("h", [P, 2, D])
        squares = st.sb("squares", [P, D])
        g = st.sb("g", [P, D])
        ident, minus_half = st.sb("ident", [P, P]), st.sb("minus_half", [P, 1])
        total, inv = st.sb("total", [P, TILES]), st.sb("inv", [P, TILES])
        turned = st.ps("turned", [P, 2, KT, P])
        g_loaded, setup = st.sem("g_loaded"), st.sem("setup")
        x_loaded = st.sems("x_loaded", slots)
        total_done, inv_done, h_done, turned_done, hi_done, lo_done = (
            st.sem(n) for n in ("total_done", "inv_done", "h_done", "turned_done", "hi_done", "lo_done"))
        block = st.block()

        @block.sync
        def _(sp):
            for t in range(TILES):
                if t >= slots:
                    sp.wait_ge(h_done, t - slots + 1)
                sp.dma_start(x[:, t % slots, :], x_tile(t)).then_inc(x_loaded[t % slots], 16)
                if t == 0:
                    sp.dma_start(g[:], rows(gain)).then_inc(g_loaded, 16)

        @block.gpsimd
        def _(pool):
            make_identity(pool, ident, setup)
            pool.memset(minus_half[:], -0.5).then_inc(setup, 1)
            pool.wait_ge(setup, 3)
            for t in range(TILES):
                pool.wait_ge(total_done, t + 1)
                inverse_root(pool, total[:, t:t + 1], 1.0 / D, EPS, minus_half[:], inv[:, t:t + 1], inv_done, 2 * t)

        @block.scalar
        def _(act):
            for t in range(TILES + 2):
                if t < TILES:
                    act.wait_ge(x_loaded[t % slots], 16 * (t // slots + 1))
                    if t >= 1:
                        act.wait_ge(total_done, t)
                    act.activation(squares[:], x[:, t % slots, :], ACT.Square,
                                   accum_out=total[:, t:t + 1]).then_inc(total_done, 1)
                if t >= 2:
                    u = t - 2
                    act.wait_ge(turned_done, u + 1)
                    act.activation(ht_hi[:, :, u * P:(u + 1) * P], turned[:, u % 2, :, :],
                                   ACT.Copy).then_inc(hi_done, 1)

        @block.vector
        def _(dve):
            dve.wait_ge(g_loaded, 16)
            for t in range(1, TILES + 2):
                if t <= TILES:
                    u = t - 1
                    dve.wait_ge(inv_done, 2 * u + 2)
                    if u >= 2:
                        dve.wait_ge(turned_done, u - 1)
                    dve.scalar_tensor_tensor(out=h[:, u % 2, :], in0=x[:, u % slots, :],
                                             scalar=inv[:, u:u + 1], in1=g[:], op0=ALU.mult,
                                             op1=ALU.mult).then_inc(h_done, 1)
                if t >= 2:
                    u = t - 2
                    dve.wait_ge(hi_done, u + 1)
                    dve.tensor_tensor(ht_lo[:, :, u * P:(u + 1) * P], turned[:, u % 2, :, :],
                                      ht_hi[:, :, u * P:(u + 1) * P].bitcast(F32),
                                      ALU.subtract).then_inc(lo_done, 1)

        @block.tensor
        def _(pe):
            pe.wait_ge(setup, 2)
            for t in range(TILES):
                pe.wait_ge(h_done, t + 1)
                if t >= 2:
                    pe.wait_ge(lo_done, t - 1)
                for k in range(KT):
                    last = pe.transpose(turned[:, t % 2, k, :], h[:, t % 2, k * P:(k + 1) * P], ident[:])
                last.then_inc(turned_done, 1)


def project(nc, name, ht_hi, ht_lo, w, y):
    n = w.shape[1]
    pieces = next(c for c in range(2, 64, 2) if n % c == 0 and n // c <= 512 and n // c % 2 == 0)
    width = n // pieces
    w_v = w.rearrange("(k p) n -> p k n", p=P)
    with Stage(nc, name) as st:
        raw = st.sb("raw", [P, 2, KT, width])
        w_hi = st.sb("w_hi", [P, 2, KT, width], F32R)
        w_lo = st.sb("w_lo", [P, 2, KT, width], F32R)
        out = st.sb("out", [P, 3, width])
        acc = st.ps("acc", [P, 3, 512])
        raw_loaded = st.sems("raw_loaded", 2)
        stored = st.sems("stored", 3)
        hi_done = st.sem("hi_done")
        lo_done = st.sem("lo_done")
        mm_done = st.sem("mm_done")
        out_done = st.sem("out_done")
        block = st.block()

        @block.scalar
        def _(act):
            def load(c, s, turn):
                act.wait_ge(lo_done, c + 1)
                act.dma_start(raw[:, s], w_v[:, :, bass.ds(c * width, width)]).then_inc(raw_loaded[s], 16)

            def split(c, s, turn):
                act.wait_ge(raw_loaded[s], 16 * turn + 16)
                act.wait_ge(mm_done, TILES * c + TILES)
                act.activation(w_hi[:, s], raw[:, s], ACT.Copy).then_inc(hi_done, 1)

            load(0, 0, 0)
            with act.Fori(0, pieces // 2 - 1) as i:
                load(2 * i + 1, 1, i)
                split(2 * i, 0, i)
                load(2 * i + 2, 0, i + 1)
                split(2 * i + 1, 1, i)
            load(pieces - 1, 1, pieces // 2 - 1)
            split(pieces - 2, 0, pieces // 2 - 1)
            split(pieces - 1, 1, pieces // 2 - 1)

        @block.vector
        def _(dve):
            dve.nop().then_inc(lo_done, 2)
            dve.nop().then_inc(out_done, 3)

            def split(c, s):
                dve.wait_ge(hi_done, c + 1)
                dve.tensor_tensor(w_lo[:, s], raw[:, s], w_hi[:, s].bitcast(F32),
                                  ALU.subtract).then_inc(lo_done, 1)

            def copy_out(c, t, i):
                dve.wait_ge(mm_done, 2 * TILES + TILES * c + t + 1)
                dve.wait_ge(stored[t % 3], 16 * (3 * c + t // 3) + 16)
                dve.tensor_copy(out[:, t % 3], acc[:, t % 3, 0:width]).then_inc(out_done, 1)

            split(0, 0)
            with dve.Fori(0, pieces // 2 - 1) as i:
                for s in range(2):
                    split(2 * i + s + 1, (s + 1) % 2)
                    for t in range(TILES):
                        copy_out(2 * i + s, t, i)
            for c in (pieces - 2, pieces - 1):
                if c < pieces - 1:
                    split(c + 1, (c + 1) % 2)
                for t in range(TILES):
                    copy_out(c, t, 0)

        @block.tensor
        def _(pe):
            pe.nop().then_inc(mm_done, 2 * TILES)
            with pe.Fori(0, pieces // 2) as i:
                for s in range(2):
                    c = 2 * i + s
                    pe.wait_ge(lo_done, c + 3)
                    for t in range(TILES):
                        pe.wait_ge(out_done, TILES * c + t + 1)
                        token = slice(t * P, (t + 1) * P)
                        for k in range(KT):
                            for j, (a, b) in enumerate(((ht_hi, w_hi), (ht_hi, w_lo), (ht_lo, w_hi))):
                                last = pe.matmul(acc[:, t % 3, 0:width], a[:, k, token], b[:, s, k, :],
                                                 start=(k == 0 and j == 0), stop=(k == KT - 1 and j == 2))
                        last.then_inc(mm_done, 1)

        @block.sync
        def _(sp):
            for q in stored:
                sp.nop().then_inc(q, 16)
            with sp.Fori(0, pieces // 2) as i:
                for s in range(2):
                    c = 2 * i + s
                    for t in range(TILES):
                        sp.wait_ge(out_done, 3 + TILES * c + t + 1)
                        sp.dma_start(y[t * P:(t + 1) * P, bass.ds(c * width, width)],
                                     out[:, t % 3]).then_inc(stored[t % 3], 16)
            for q in stored:
                sp.wait_ge(q, 16 * (3 * pieces + 1))


def turn_columns(nc, name, y, groups, tables, qkt, direct, outputs):
    width = sum(n for _, n in groups)
    blocks = width // P
    heads = width // DH
    with Stage(nc, name) as st:
        z = st.sb("z", [P, 2, width])
        ident = st.sb("ident", [P, P])
        cols = st.sb("cols", [P, 2, blocks, P])
        half = (blocks + 1) // 2
        turned = st.ps("turned", [P, 2, 4 * ((half + 3) // 4), P])
        ident_done, table_loaded, direct_done = (st.sem(n) for n in ("ident_done", "table_loaded", "direct_done"))
        z_loaded, cols_stored, rows_stored = (st.sems(n, 2) for n in ("z_loaded", "cols_stored", "rows_stored"))
        cos_done, sin_done, rot_done, turned_done, cols_done = (
            st.sem(n) for n in ("cos_done", "sin_done", "rot_done", "turned_done", "cols_done"))
        if tables is not None:
            table = st.sb("table", [P, TILES, 2, DH])
            zc = st.sb("zc", [P, 2, width])
            zs = st.sb("zs", [P, 2, width])
            ready, ready_sem = zc, rot_done
        else:
            ready, ready_sem = z, None
        n_out = [len(outputs(t, ready[:, t % 2, :])) for t in range(TILES)]
        block = st.block()

        def heads_of(ap):
            return ap.rearrange("p (h d) -> p h d", d=DH)

        @block.sync
        def _(sp):
            if tables is not None:
                sp.dma_start(table[:], tables).then_inc(table_loaded, 16)
            for t in range(TILES):
                s = t % 2
                if t >= 2:
                    sp.wait_ge(turned_done, 2 * (t - 1))
                    if tables is not None:
                        sp.wait_ge(rot_done, t - 1)
                    elif sum(n_out[s:t - 1:2]):
                        sp.wait_ge(rows_stored[s], 16 * sum(n_out[s:t - 1:2]))
                at = 0
                for first, n in groups:
                    sp.dma_start(z[:, s, at:at + n], y[t * P:(t + 1) * P, first:first + n]).then_inc(z_loaded[s], 16)
                    at += n
                if t == 1:
                    for dst, src in direct:
                        sp.dma_start(dst, src).then_inc(direct_done, 16)
            sp.wait_ge(direct_done, 16 * len(direct))

        @block.gpsimd
        def _(pool):
            make_identity(pool, ident, ident_done)
            if tables is None:
                return
            pool.wait_ge(table_loaded, 16)
            for t in range(TILES):
                s = t % 2
                pool.wait_ge(z_loaded[s], 16 * len(groups) * (t // 2 + 1))
                if t >= 2:
                    pool.wait_ge(rot_done, t - 1)
                zv, sv = heads_of(z[:, s, :]), heads_of(zs[:, s, :])
                for a, b in ((0, HALF), (HALF, 0)):
                    pool.tensor_tensor(sv[:, :, a:a + HALF], zv[:, :, b:b + HALF],
                                       table[:, t, 1:2, a:a + HALF].to_broadcast([P, heads, HALF]),
                                       ALU.mult).then_inc(sin_done, 1)

        @block.vector
        def _(dve):
            if tables is not None:
                dve.wait_ge(table_loaded, 16)
                for t in range(TILES):
                    s = t % 2
                    dve.wait_ge(z_loaded[s], 16 * len(groups) * (t // 2 + 1))
                    if t >= 2:
                        dve.wait_ge(turned_done, 2 * (t - 1))
                        if sum(n_out[s:t - 1:2]):
                            dve.wait_ge(rows_stored[s], 16 * sum(n_out[s:t - 1:2]))
                    dve.tensor_tensor(heads_of(zc[:, s, :]), heads_of(z[:, s, :]),
                                      table[:, t, 0:1, :].to_broadcast([P, heads, DH]),
                                      ALU.mult).then_inc(cos_done, 1)
                    dve.wait_ge(cos_done, t + 1)
                    dve.wait_ge(sin_done, 2 * t + 2)
                    dve.tensor_tensor(zc[:, s, :], zc[:, s, :], zs[:, s, :], ALU.add).then_inc(rot_done, 1)

        @block.tensor
        def _(pe):
            pe.wait_ge(ident_done, 2)
            for t in range(TILES):
                s = t % 2
                if tables is not None:
                    pe.wait_ge(rot_done, t + 1)
                else:
                    pe.wait_ge(z_loaded[s], 16 * len(groups) * (t // 2 + 1))
                for part, (a, b) in enumerate(((0, half), (half, blocks))):
                    if t >= 1:
                        pe.wait_ge(cols_done, 2 * (t - 1) + part + 1)
                    for j in range(a, b):
                        last = pe.transpose(turned[:, part, j - a, :], ready[:, s, j * P:(j + 1) * P], ident[:])
                    last.then_inc(turned_done, 1)

        @block.scalar
        def _(act):
            q_v = qkt.rearrange("(j p) n -> p j n", p=P)
            for t in range(TILES):
                s = t % 2
                if t >= 2:
                    act.wait_ge(cols_stored[s], 16 * (t // 2))
                for part, (a, b) in enumerate(((0, half), (half, blocks))):
                    act.wait_ge(turned_done, 2 * t + part + 1)
                    act.activation(cols[:, s, a:b, :], turned[:, part, 0:b - a, :], ACT.Copy).then_inc(cols_done, 1)
                act.wait_ge(cols_done, 2 * t + 2)
                act.dma_start(q_v[:, :, t * P:(t + 1) * P], cols[:, s]).then_inc(cols_stored[s], 16)
                if tables is not None:
                    act.wait_ge(rot_done, t + 1)
                else:
                    act.wait_ge(z_loaded[s], 16 * len(groups) * (t // 2 + 1))
                for dst, src in outputs(t, ready[:, s, :]):
                    act.dma_start(dst, src).then_inc(rows_stored[s], 16)
            for s in range(2):
                act.wait_ge(cols_stored[s], 16 * len(range(s, TILES, 2)))
                if sum(n_out[s::2]):
                    act.wait_ge(rows_stored[s], 16 * sum(n_out[s::2]))


def prompt_attention(nc, name, trips, q_rows, k_rows, v_cols, o_cols, qkt, y, o, dv, window=False,
                     causal=False, sinks=None, b_lambda=None, ck=None, copies=None):
    units = 2 * TILES_P
    diff = b_lambda is not None
    first = [max(0, t - 1) if window else 0 for t in range(TILES_P)]
    count = [t + 1 - first[t] for t in range(TILES_P)]
    order = list(range(0, TILES_P, 2)) + list(range(TILES_P - 1, 0, -2))

    def place(j):
        e, r = divmod(j, TILES_P)
        return e, r, order[r]

    unit_groups, g = [], 0
    for t in order:
        mine = []
        for a in range(0, count[t], 4):
            mine.append((g, a, min(a + 4, count[t])))
            g += 1
        unit_groups.append(mine)
    groups = g
    assert groups % 2 == 0
    with Stage(nc, name) as st:
        q_raw, k_raw = st.sb("q_raw", [P, 2, PROMPT]), st.sb("k_raw", [P, 2, PROMPT])
        q_hi, k_both = st.sb("q_hi", [P, 2, PROMPT], F32R), st.sb("k_both", [P, 2, PROMPT], F32R)
        if ck is None:
            q_lo = st.sb("q_lo", [P, 2, PROMPT], F32R)
        else:
            q_lo, k_hi = (st.sb(n, [DH + 2, 2, PROMPT], F32R) for n in ("q_lo", "k_hi"))
            ones, kc_raw = st.sb("ones", [DH + 2, PROMPT]), st.sb("kc_raw", [DH + 2, 2, PROMPT])
        v = st.sb("v", [P, 2, TILES_P, dv])
        probs = st.sb("probs", [P, 4, PROMPT])
        probs_t = st.sb("probs_t", [P, 4, TILES_P, P])
        out = st.sb("out", [P, 2, TILES_P, dv])
        ident = st.sb("ident", [P, P])
        ident_b = st.sb("ident_b", [P, P], BF16)
        mask = st.sb("mask", [P, 2 * P], BF16)
        top, neg_top = st.sb("top", [P, 4]), st.sb("neg_top", [P, 4])
        total, inv = st.sb("total", [P, 4]), st.sb("inv", [P, 4])
        scores = st.ps("scores", [P, 2, PROMPT])
        turned = st.ps("turned", [P, 2, 4, P])
        pv = st.ps("pv", [P, 2, 512])
        setup, hi_split, lo_split = st.sem("setup"), st.sem("hi_split"), st.sem("lo_split")
        rows_copied = st.sem("rows_copied")
        hi_steps = 2 if ck is None else 3
        qk_loaded, loaded, stored, copied = (st.sems(n, 2) for n in ("qk_loaded", "loaded", "stored", "copied"))
        scores_done, top_done, neg_done, exp_done, turned_done, pv_done, inv_done, out_done = (
            st.sem(n) for n in ("scores_done", "top_done", "neg_done", "exp_done", "turned_done",
                                "pv_done", "inv_done", "out_done"))
        n_qk_loads = 4 if ck is None else 6
        n_loads = 1 + (sinks is not None)
        if sinks is not None:
            sink, neg_sink = st.sb("sink", [P, 2]), st.sb("neg_sink", [P, 2])
            sink_exp = st.sb("sink_exp", [P, 4])
            neg_sink_done, sink_exp_done, total_done = (
                st.sem(n) for n in ("neg_sink_done", "sink_exp_done", "total_done"))
        if diff:
            lam = st.sb("lam", [P, 4, DH])
            lam_sum, lam_exp, neg_lam = st.sb("lam_sum", [P, 2]), st.sb("lam_exp", [P, 2]), st.sb("neg_lam", [P, 1])
            lam_loaded, lam_done, lam_exp_done = (st.sem(n) for n in ("lam_loaded", "lam_done", "lam_exp_done"))
        block = st.block()

        def ahead(step, i, j, more):
            if j < units:
                step(i, j)
            elif more:
                step(i + 1, j - units)

        @block.sync
        def _(sp):
            if diff:
                sp.dma_start(lam[:], rows(b_lambda.rearrange("(a n) d -> a (n d)", a=1))).then_inc(lam_loaded, 16)

            def load_qk(i, e):
                for part in (slice(0, DH), slice(DH, P)):
                    sp.dma_start(k_raw[part, e], qkt[bass.ds(k_rows(i, e), DH), 0:PROMPT]).then_inc(qk_loaded[e], 16)
                    sp.dma_start(q_raw[part, e], qkt[bass.ds(q_rows(i, e), DH), 0:PROMPT]).then_inc(qk_loaded[e], 16)
                if ck is not None:
                    sp.dma_start(kc_raw[0:DH, e], qkt[bass.ds(k_rows(i, e), DH), 0:PROMPT]).then_inc(qk_loaded[e], 16)
                    sp.dma_start(kc_raw[DH:DH + 2, e], ck[bass.ds(2 * i + e, 1)].rearrange(
                        "h a n -> (h a) n")).then_inc(qk_loaded[e], 16)

            def load(i, e):
                sp.dma_start(v[:, e], y[0:PROMPT, bass.ds(v_cols(i, e), dv)].rearrange(
                    "(t p) d -> p t d", p=P)).then_inc(loaded[e], 16)
                if sinks is not None:
                    s_i = sinks[0:1, bass.ds(2 * i + e, 1)]
                    sp.dma_start(sink[:, e:e + 1], rows(s_i)).then_inc(loaded[e], 16)

            def copy_rows(i):
                for dst, src in copies(i) if copies is not None else []:
                    sp.dma_start(dst, src).then_inc(rows_copied, 16)

            def store(i, e):
                if diff and e == 0:
                    return
                sp.wait_ge(out_done, 2 + units * i + TILES_P * (e + 1))
                sp.dma_start(o[0:PROMPT, bass.ds(o_cols(i, e), dv)].rearrange("(t p) d -> p t d", p=P),
                             out[:, e]).then_inc(stored[e], 16)

            for q in stored:
                sp.nop().then_inc(q, 16)
            load_qk(0, 0)
            load(0, 0)
            load_qk(0, 1)
            load(0, 1)
            with sp.Fori(0, trips - 1) as i:
                for e in range(2):
                    sp.wait_ge(lo_split, 2 * (2 * i + e) + 2)
                    sp.wait_ge(hi_split, hi_steps * (2 * i + e + 1))
                    load_qk(i + 1, e)
                copy_rows(i)
                for e in range(2):
                    sp.wait_ge(pv_done, 4 + units * i + TILES_P * (e + 1))
                    load(i + 1, e)
                    store(i, e)
            copy_rows(trips - 1)
            for e in range(2):
                store(trips - 1, e)
            if copies is not None:
                sp.wait_ge(rows_copied, 16 * trips * len(copies(0)))
            sp.wait_ge(stored[1], 16 * (trips + 1))
            if not diff:
                sp.wait_ge(stored[0], 16 * (trips + 1))

        @block.gpsimd
        def _(pool):
            make_identity(pool, ident, setup)
            pool.wait_ge(setup, 2)
            pool.memset(mask[:], 0.0).then_inc(setup, 1)
            pool.wait_ge(setup, 3)
            if causal:
                pool.affine_select(out=mask[:, P:], in_=mask[:, P:], compare_op=ALU.is_ge, fill=NEG,
                                   base=0, pattern=[[-1, P]], channel_multiplier=1).then_inc(setup, 1)
            else:
                pool.memset(mask[0:CHUNK, P + CHUNK:2 * P], NEG).then_inc(setup, 1)
            pool.wait_ge(setup, 4)
            if window:
                pool.memset(mask[CHUNK:P, 0:CHUNK], NEG).then_inc(setup, 1)
            else:
                pool.nop().then_inc(setup, 1)
            pool.wait_ge(setup, 5)
            pool.tensor_copy(ident_b[:], ident[:]).then_inc(setup, 1)
            pool.wait_ge(setup, 6)
            if ck is not None:
                pool.memset(ones[DH:DH + 2], 1.0).then_inc(setup, 1)
                for e in range(2):
                    pool.wait_ge(setup, 7 + e)
                    pool.tensor_copy(q_lo[DH:DH + 2, e], ones[DH:DH + 2]).then_inc(setup, 1)
            else:
                pool.nop().then_inc(setup, 3)
            pool.wait_ge(setup, 9)

        def group_number(i, e, g):
            return groups * (2 * i + e) + g

        @block.tensor
        def _(pe):
            pe.nop().then_inc(pv_done, 4)
            pe.wait_ge(setup, 9)

            def score(i, j):
                e, r, t = place(j)
                n = units * i + j
                if r == 0:
                    pe.wait_ge(lo_split, 2 * (2 * i + e) + 2)
                    pe.wait_ge(hi_split, hi_steps * (2 * i + e + 1))
                    pe.wait_ge(loaded[e], 16 * n_loads * i + 16 * n_loads)
                pe.wait_ge(exp_done, n + 1)
                width = count[t] * P
                masked = min(2 * P if window else P, width)
                for a in range(0, width, 512):
                    b = min(a + 512, width)
                    query, key = slice(t * P, (t + 1) * P), slice(first[t] * P + a, first[t] * P + b)
                    pe.matmul(scores[:, j % 2, a:b], q_hi[:, e, query], k_both[:, e, key], start=True, stop=False)
                    pe.matmul(scores[:, j % 2, a:b], q_lo[:, e, query], (k_both if ck is None else k_hi)[:, e, key],
                              start=False, stop=(b < width))
                pe.matmul(scores[:, j % 2, width - masked:width], ident_b[:], mask[:, 2 * P - masked:],
                          start=False, stop=True).then_inc(scores_done, 1)

            def turn(i, j):
                e, r, t = place(j)
                n = units * i + j
                pe.wait_ge(exp_done, 2 + n + 1)
                for g, a, b in unit_groups[r]:
                    pe.wait_ge(copied[g % 2], (groups // 2) * (2 * i + e) + g // 2 + 1)
                    for x in range(a, b):
                        last = pe.transpose(turned[:, g % 2, x - a, :], probs[:, j % 4, x * P:(x + 1) * P], ident[:])
                    last.then_inc(turned_done, 1)

            def attend(i, j):
                e, r, t = place(j)
                n = units * i + j
                for g, a, b in unit_groups[r]:
                    pe.wait_ge(copied[g % 2], 1 + (groups // 2) * (2 * i + e) + g // 2 + 1)
                pe.wait_ge(out_done, n + 1)
                for x in range(count[t]):
                    last = pe.matmul(pv[:, j % 2, 0:dv], probs_t[:, j % 4, x, :], v[:, e, first[t] + x, :],
                                     start=(x == 0), stop=(x == count[t] - 1))
                last.then_inc(pv_done, 1)

            def trip(i, more):
                for j in range(units):
                    ahead(score, i, j + 3, more)
                    ahead(turn, i, j + 1, more)
                    attend(i, j)

            score(0, 0)
            score(0, 1)
            score(0, 2)
            turn(0, 0)
            with pe.Fori(0, trips - 1) as i:
                trip(i, True)
            trip(trips - 1, False)

        def copy_group(eng, i, j, odd):
            e, r, t = place(j)
            for g, a, b in unit_groups[r]:
                if g % 2 != odd:
                    continue
                eng.wait_ge(turned_done, group_number(i, e, g) + 1)
                eng.wait_ge(pv_done, units * i + j + 1)
                dst, src = probs_t[:, j % 4, a:b, :], turned[:, odd, 0:b - a, :]
                if odd:
                    eng.activation(dst, src, ACT.Copy).then_inc(copied[1], 1)
                else:
                    eng.tensor_copy(dst, src).then_inc(copied[0], 1)

        @block.scalar
        def _(act):
            act.nop().then_inc(exp_done, 2)
            act.nop().then_inc(copied[1], 1)
            if diff:
                act.wait_ge(lam_done, 2)
                act.activation(lam_exp[:], lam_sum[:], ACT.Exp).then_inc(lam_exp_done, 1)

            def split_high(i, e, step):
                act.wait_ge(qk_loaded[e], 16 * n_qk_loads * i + 16 * n_qk_loads)
                dst, src = [(k_both, k_raw), (q_hi, q_raw)][step] if step < 2 else (k_hi, kc_raw)
                act.activation(dst[:, e], src[:, e], ACT.Copy).then_inc(hi_split, 1)

            def copy_odd(i, j):
                copy_group(act, i, j, 1)

            def exponential(i, j):
                e, r, t = place(j)
                n = units * i + j
                act.wait_ge(neg_done, n + 1)
                act.wait_ge(pv_done, n + 1)
                act.wait_ge(inv_done, n + 1)
                act.activation(probs[:, j % 4, 0:count[t] * P], scores[:, j % 2, 0:count[t] * P], ACT.Exp,
                               bias=neg_top[:, j % 4:j % 4 + 1], scale=SCALE,
                               accum_out=total[:, j % 4:j % 4 + 1]).then_inc(exp_done, 1)
                if sinks is not None:
                    act.activation(sink_exp[:, j % 4:j % 4 + 1], sink[:, e:e + 1], ACT.Exp,
                                   bias=neg_top[:, j % 4:j % 4 + 1]).then_inc(sink_exp_done, 1)

            def trip(i, more):
                for j in range(units):
                    ahead(exponential, i, j + 2, more)
                    ahead(copy_odd, i, j + 1, more)
                    if j < hi_steps:
                        split_high(i, 1, j)
                    elif TILES_P <= j < TILES_P + hi_steps and more:
                        split_high(i + 1, 0, j - TILES_P)

            for step in range(hi_steps):
                split_high(0, 0, step)
            exponential(0, 0)
            exponential(0, 1)
            copy_odd(0, 0)
            with act.Fori(0, trips - 1) as i:
                trip(i, True)
            trip(trips - 1, False)

        @block.vector
        def _(dve):
            dve.nop().then_inc(copied[0], 1)
            dve.nop().then_inc(out_done, 2)
            dve.nop().then_inc(inv_done, 4)
            if diff:
                dve.wait_ge(lam_loaded, 16)
                for x in range(2):
                    dve.tensor_tensor_reduce(lam[:, 2 * x, :], lam[:, 2 * x, :], lam[:, 2 * x + 1, :], 1.0, 0.0,
                                             ALU.mult, ALU.add, lam_sum[:, x:x + 1]).then_inc(lam_done, 1)
                dve.wait_ge(lam_exp_done, 1)
                dve.tensor_scalar(neg_lam[:], lam_exp[:, 1:2], lam_exp[:, 0:1], -LAM_INIT, ALU.subtract,
                                  ALU.add).then_inc(lam_done, 1)
                dve.wait_ge(lam_done, 3)

            def split_low(i, e, step):
                dve.wait_ge(hi_split, hi_steps * (2 * i + e) + step + 1)
                if step == 0:
                    dve.tensor_tensor(k_both[DH:P, e], k_raw[DH:P, e], k_both[DH:P, e].bitcast(F32),
                                      ALU.subtract).then_inc(lo_split, 1)
                else:
                    part = slice(0, P if ck is None else DH)
                    dve.tensor_tensor(q_lo[part, e], q_raw[part, e], q_hi[part, e].bitcast(F32),
                                      ALU.subtract).then_inc(lo_split, 1)

            def copy_even(i, j):
                copy_group(dve, i, j, 0)

            def maximum(i, j):
                e, r, t = place(j)
                n = units * i + j
                if sinks is not None and r == 0:
                    dve.wait_ge(loaded[e], 16 * n_loads * i + 16 * n_loads)
                    dve.tensor_scalar(neg_sink[:, e:e + 1], sink[:, e:e + 1], -1.0, None,
                                      ALU.mult).then_inc(neg_sink_done, 1)
                    dve.wait_ge(neg_sink_done, 2 * i + e + 1)
                dve.wait_ge(scores_done, n + 1)
                dve.tensor_reduce(top[:, j % 4:j % 4 + 1], scores[:, j % 2, 0:count[t] * P], AX.X,
                                  ALU.max).then_inc(top_done, 1)
                dve.wait_ge(top_done, n + 1)
                if sinks is not None:
                    dve.wait_ge(sink_exp_done, n + 1)
                    dve.tensor_scalar(neg_top[:, j % 4:j % 4 + 1], top[:, j % 4:j % 4 + 1], -SCALE,
                                      neg_sink[:, e:e + 1], ALU.mult, ALU.min).then_inc(neg_done, 1)
                else:
                    dve.tensor_scalar(neg_top[:, j % 4:j % 4 + 1], top[:, j % 4:j % 4 + 1], -SCALE, None,
                                      ALU.mult).then_inc(neg_done, 1)

            def output(i, j):
                e, r, t = place(j)
                n = units * i + j
                total_j, inv_j = total[:, j % 4:j % 4 + 1], inv[:, j % 4:j % 4 + 1]
                per = 1
                if sinks is not None:
                    dve.wait_ge(sink_exp_done, 4 + n + 1)
                    dve.tensor_tensor(total_j, total_j, sink_exp[:, j % 4:j % 4 + 1], ALU.add).then_inc(total_done, 1)
                    dve.wait_ge(total_done, n + 1)
                dve.wait_ge(exp_done, 2 + n + 1)
                dve.wait_ge(out_done, n + 1)
                dve.reciprocal(inv_j, total_j).then_inc(inv_done, 1)
                dve.wait_ge(inv_done, 4 + n + 1)
                dve.wait_ge(pv_done, 4 + n + 1)
                dst, src = out[:, e, t, :], pv[:, j % 2, 0:dv]
                if diff and e == 1:
                    dve.tensor_scalar(src, src, inv_j, neg_lam[:], ALU.mult, ALU.mult).then_inc(lam_done, 1)
                    dve.wait_ge(lam_done, 3 + TILES_P * i + r + 1)
                    if r == 0:
                        dve.wait_ge(stored[1], 16 * i + 16)
                    dve.tensor_tensor(dst, src, out[:, 0, t, :], ALU.add).then_inc(out_done, 1)
                else:
                    if r == 0 and not diff:
                        dve.wait_ge(stored[e], 16 * i + 16)
                    dve.tensor_scalar(dst, src, inv_j, None, ALU.mult).then_inc(out_done, 1)

            def trip(i, more):
                for j in range(units):
                    ahead(maximum, i, j + 3, more)
                    ahead(copy_even, i, j + 1, more)
                    output(i, j)
                    if j in (1, 2):
                        split_low(i, 1, j - 1)
                    elif j in (TILES_P + 1, TILES_P + 2) and more:
                        split_low(i + 1, 0, j - TILES_P - 1)

            if sinks is not None:
                dve.nop().then_inc(sink_exp_done, 4)
            split_low(0, 0, 0)
            split_low(0, 0, 1)
            maximum(0, 0)
            maximum(0, 1)
            maximum(0, 2)
            copy_even(0, 0)
            with dve.Fori(0, trips - 1) as i:
                trip(i, True)
            trip(trips - 1, False)


def strided(ap, offset, *dims):
    return bass.AP(ap.tensor, ap.offset + offset, [list(ap.ap[0])] + [list(d) for d in dims])


def sample_attention(nc, name, groups, q_first, qkt, k_cache, v_cache, k_new, v_new, o, o_first,
                     row_odd=None, b_lambda=None, neg_c8=None, row_mask=None, selector=None):
    diff = b_lambda is not None
    width = 4 * P
    parts, per = 4, PAST // 4 // P
    span = per * P
    keys = PAST + FRAMES
    tiles = PAST // P + 1
    pairs = 4 * groups
    bank = 512
    units = STREAMS * groups
    trips = units // 2
    KG = 4 * parts + 2
    KE = KG // 2
    SG = parts + 1
    PG = [(a, min(a + 4, tiles)) for a in range(0, tiles, 4)]
    PE_, PO_ = (len(PG) + 1) // 2, len(PG) // 2
    OC = 1 if diff else 2
    with Stage(nc, name) as st:
        kc = st.sb("kc", [P, parts, per, width])
        vc = st.sb("vc", [P, 2, parts, per, width])
        kn, vn = st.sb("kn", [P, width]), st.sb("vn", [FRAMES, 2, width])
        kt = st.sb("kt", [P, 2, 4, span])
        ktn = st.sb("ktn", [P, 4, FRAMES])
        q_all = st.sb("q_all", [P, pairs, P])
        q_blocks = st.sb("q_blocks", [P, 4, 2 * FRAMES])
        scores = st.sb("scores", [P, keys])
        probs = st.sb("probs", [P, keys])
        probs_t = st.sb("probs_t", [P, tiles, P])
        top, neg_top, total = (st.sb(n, [P, 1]) for n in ("top", "neg_top", "total"))
        inv = st.sb("inv", [P, 2])
        out_t = st.sb("out_t", [P, pairs, P])
        out = st.sb("out", [P, pairs * P])
        ident = st.sb("ident", [P, P])
        k_ps = st.ps("k_ps", [P, 3, bank])
        s_ps = st.ps("s_ps", [P, 2, bank])
        p_ps = st.ps("p_ps", [P, 2, bank])
        o_ps = st.ps("o_ps", [P, 2, P])
        o_rows = st.sb("o_rows", [P, P])
        setup = st.sem("setup")
        k_loaded, v_loaded = st.sems("k_loaded", parts), st.sems("v_loaded", 2 * parts)
        vnew_loaded = st.sems("vnew_loaded", 2)
        (new_loaded, q_loaded, q_done, k_turned, kt_even, kt_odd, s_done, s_copied, top_done,
         neg_done, exp_done, inv_done, p_turned, pt_even, pt_odd, pv_done, scaled, row_turned,
         o_done, o_turned, out_done, stored) = (st.sem(n) for n in (
             "new_loaded", "q_loaded", "q_done", "k_turned", "kt_even", "kt_odd", "s_done",
             "s_copied", "top_done", "neg_done", "exp_done", "inv_done", "p_turned", "pt_even",
             "pt_odd", "pv_done", "scaled", "row_turned", "o_done", "o_turned", "out_done", "stored"))
        if diff:
            lam, lam_sum, lam_exp, neg_lam = (st.sb("lam", [P, 4, DH]), st.sb("lam_sum", [P, 2]),
                                              st.sb("lam_exp", [P, 2]), st.sb("neg_lam", [P, 1]))
            odd, weight = st.sb("odd", [P, 1]), st.sb("weight", [P, 1])
            o_first_head = st.sb("o_first_head", [P, 4, FRAMES])
            lam_loaded, lam_done, lam_exp_done, o_half = (
                st.sem(n) for n in ("lam_loaded", "lam_done", "lam_exp_done", "o_half"))
        else:
            bias_raw, bias = st.sb("bias_raw", [16, 2, keys]), st.sb("bias", [16, keys], F32R)
            later, select_raw, select = (st.sb("later", [P, FRAMES]), st.sb("select_raw", [16, P]),
                                         st.sb("select", [16, P], F32R))
            bias_loaded, later_loaded = st.sems("bias_loaded", 2), st.sem("later_loaded")
            bias_done, select_done = st.sem("bias_done"), st.sem("select_done")
        block = st.block()

        def stream_of(i, k):
            return 2 * i + k if groups == 1 else i

        def group_of(k):
            return 0 if groups == 1 else k

        def each_unit(eng, step, flush=None):
            step(0, 0, True)
            step(0, 1, False)
            with eng.Fori(1, trips) as i:
                step(i, 0, False)
                step(i, 1, False)
            if flush is not None:
                flush(trips - 1, 1)

        def last_unit(step, i, k):
            step(i, 0) if k else step(i - 1, 1)

        @block.sync
        def _(sp):
            sp.dma_start(q_all[:], qkt[q_first:q_first + pairs * P, PROMPT:TOKENS].rearrange(
                "(j p) n -> p j n", p=P)).then_inc(q_loaded, 16)
            if diff:
                sp.dma_start(lam[:], rows(b_lambda.rearrange("(a n) d -> a (n d)", a=1))).then_inc(lam_loaded, 16)
                sp.dma_start(odd[:], row_odd).then_inc(lam_loaded, 16)
            else:
                sp.dma_start(later[:], row_mask).then_inc(later_loaded, 16)
                sp.dma_start(select_raw[:], selector).then_inc(later_loaded, 16)
            sp.wait_ge(setup, 4)

            def load_k(i, k):
                u, b = 2 * i + k, stream_of(i, k)
                c = slice(group_of(k) * width, (group_of(k) + 1) * width)
                for x in range(parts):
                    sp.wait_ge(k_turned, KG * u + 4 * (x + 1))
                    if x == 0 and not diff:
                        for part in range(2):
                            sp.dma_start(bias_raw[8 * part:8 * part + 8, k], neg_c8[bass.ds(b * C_H + 8 * group_of(k), 8), part]
                                         ).then_inc(bias_loaded[k], 16)
                    sp.dma_start(kc[:, x], k_cache[bass.ds(b, 1), x * span:(x + 1) * span, c].rearrange(
                        "b (t p) c -> p (b t) c", p=P)).then_inc(k_loaded[x], 16)
                sp.wait_ge(k_turned, KG * u + KG)
                sp.dma_start(kn[0:FRAMES], k_new[bass.ds(b * FRAMES, FRAMES), c]).then_inc(new_loaded, 16)

            def load_v(i, k):
                u, b = 2 * i + k, stream_of(i, k)
                c = slice(group_of(k) * width, (group_of(k) + 1) * width)
                sp.wait_ge(pv_done, u + 1)
                for x in range(parts):
                    if x == 0:
                        sp.dma_start(vn[:, k], v_new[bass.ds(b * FRAMES, FRAMES), c]).then_inc(vnew_loaded[k], 16)
                    sp.dma_start(vc[:, k, x], v_cache[bass.ds(b, 1), x * span:(x + 1) * span, c].rearrange(
                        "b (t p) c -> p (b t) c", p=P)).then_inc(v_loaded[parts * k + x], 16)

            with sp.Fori(0, trips) as i:
                for k in range(2):
                    load_k(i, k)
                    load_v(i, k)
            sp.wait_ge(out_done, 2)
            sp.dma_start(o[PROMPT:TOKENS, o_first:o_first + pairs * P], out[:]).then_inc(stored, 16)
            sp.wait_ge(stored, 16)

        @block.gpsimd
        def _(pool):
            make_identity(pool, ident, setup)
            pool.memset(q_blocks[:], 0.0).then_inc(setup, 1)
            pool.memset(kn[:], 0.0).then_inc(setup, 1)
        @block.tensor
        def _(pe):
            pe.nop().then_inc(k_turned, KG)
            pe.nop().then_inc(s_done, SG)
            pe.nop().then_inc(p_turned, len(PG))
            pe.nop().then_inc(pv_done, 2)
            pe.nop().then_inc(row_turned, 1)
            pe.wait_ge(setup, 4)
            if not diff:
                pe.wait_ge(later_loaded, 32)
                pe.wait_ge(select_done, 1)

            def k_slot_free(u, r):
                back = r - 3 if r >= 3 else r - 3 + KG
                count = KE * u + back // 2 + 1 + (KE if r >= 3 else 0)
                pe.wait_ge(kt_odd if back % 2 else kt_even, count)

            def turn(u, x):
                pe.wait_ge(k_loaded[x], 16 * u + 16)
                for j in range(4):
                    r = 4 * x + j
                    k_slot_free(u, r)
                    for t in range(per):
                        last = pe.transpose(k_ps[:, r % 3, t * P:(t + 1) * P], kc[:, x, t, j * P:(j + 1) * P], ident[:])
                    last.then_inc(k_turned, 1)

            def turn_new(u):
                pe.wait_ge(new_loaded, 16 * u + 16)
                for half in range(2):
                    r = 4 * parts + half
                    k_slot_free(u, r)
                    for j in range(2):
                        last = pe.transpose(k_ps[:, r % 3, j * P:(j + 1) * P],
                                            kn[:, (2 * half + j) * P:(2 * half + j + 1) * P], ident[:])
                    last.then_inc(k_turned, 1)

            def score(i, k, x):
                u = 2 * i + k
                new = x == parts
                copies = KE * u + KE + (KE if new else 2 * x + 2)
                pe.wait_ge(kt_even, copies)
                pe.wait_ge(kt_odd, copies)
                pe.wait_ge(s_copied, SG * u + SG + x - 1 if x >= 2 else SG * u + SG - x)
                n = FRAMES if new else span
                for j in range(4):
                    last = pe.matmul(s_ps[32 * j:32 * j + 32, x % 2, 0:n], q_blocks[:, j, :],
                                     ktn[:, j, :] if new else kt[:, x % 2, j, :], start=True, stop=diff,
                                     skip_group_check=True)
                if not diff:
                    if x == 0:
                        pe.wait_ge(bias_done, u + 1)
                    if new:
                        pe.matmul(s_ps[:, x % 2, 0:n], ident[:], later[:], start=False, stop=False,
                                  skip_group_check=True)
                    last = pe.matmul(s_ps[:, x % 2, 0:n], select[:], bias[:, x * span:x * span + n],
                                     start=False, stop=True, skip_group_check=True)
                last.then_inc(s_done, 1)

            def k_phase(i, k):
                u = 2 * i + k
                turn(u, 0)
                pe.wait_ge(q_done, 2 * u + 2)
                for x in range(1, parts):
                    turn(u, x)
                    score(i, k, x - 1)
                turn_new(u)
                score(i, k, parts - 1)
                score(i, k, parts)

            def pv_phase(i, k):
                u = 2 * i + k
                pe.wait_ge(exp_done, u + 2)
                for gi, (a, b) in enumerate(PG):
                    if gi % 2 == 0:
                        pe.wait_ge(pt_even, PE_ * u + PE_ + (gi // 2 if gi else 0))
                    else:
                        pe.wait_ge(pt_odd, PO_ * u + PO_ + (gi - 1) // 2)
                    for t in range(a, b):
                        m = P if t < tiles - 1 else FRAMES
                        last = pe.transpose(p_ps[0:m, gi % 2, (t - a) * P:(t - a + 1) * P], probs[:, t * P:t * P + m], ident[:])
                    last.then_inc(p_turned, 1)
                pe.wait_ge(pt_even, PE_ * u + 2 * PE_)
                pe.wait_ge(pt_odd, PO_ * u + 2 * PO_)
                pe.wait_ge(scaled, u + 1)
                for t in range(tiles):
                    new = t == tiles - 1
                    m = FRAMES if new else P
                    if t == 0:
                        pe.wait_ge(vnew_loaded[k], 16 * i + 16)
                    if t % per == 0 and not new:
                        pe.wait_ge(v_loaded[parts * k + t // per], 16 * i + 16)
                    for j in range(4):
                        values = vn[:, k, j * P:(j + 1) * P] if new else vc[:, k, t // per, t % per, j * P:(j + 1) * P]
                        last = pe.matmul(o_ps[32 * j:32 * j + 32, 0, :], probs_t[0:m, t, 32 * j:32 * j + 32], values,
                                         start=(t == 0), stop=new, skip_group_check=True)
                last.then_inc(pv_done, 1)

            def turn_output(i, k):
                u = 2 * i + k
                pe.wait_ge(scaled, u + 2)
                pe.wait_ge(o_done, OC * u + OC)
                pe.transpose(o_ps[:, 1, :], o_rows[:], ident[:]).then_inc(row_turned, 1)

            def step(i, k, is_first):
                k_phase(i, k)
                if not is_first:
                    last_unit(pv_phase, i, k)
                    last_unit(turn_output, i, k)

            def flush(i, k):
                pv_phase(i, k)
                turn_output(i, k)

            each_unit(pe, step, flush)
            pe.wait_ge(o_done, OC * units + OC)
            for half in range(2):
                back = KG - 3 + half
                pe.wait_ge(kt_odd if back % 2 else kt_even, KE * (units + 1))
                for j in range(pairs // 2):
                    last = pe.transpose(k_ps[:, half, j * P:(j + 1) * P], out_t[:, half * pairs // 2 + j, :], ident[:])
                last.then_inc(o_turned, 1)

        def copy_kt(eng, u, r):
            x = r // 4
            eng.wait_ge(k_turned, KG * u + KG + r + 1)
            if x == parts:
                half = r - 4 * parts
                eng.wait_ge(s_done, SG * u + SG)
                dst = ktn[:, 2 * half:2 * half + 2, :]
                src = k_ps[:, r % 3, 0:2 * P].rearrange("p (j f) -> p j f", j=2)[:, :, 0:FRAMES]
            else:
                eng.wait_ge(s_done, SG * u + SG + x - 1 if x >= 2 else SG * u + x + parts - 1)
                dst, src = kt[:, x % 2, r % 4, :], k_ps[:, r % 3, :]
            if r % 2:
                eng.activation(dst, src, ACT.Copy).then_inc(kt_odd, 1)
            else:
                eng.tensor_copy(dst, src).then_inc(kt_even, 1)

        def copy_probs(eng, u, gi):
            a, b = PG[gi]
            eng.wait_ge(p_turned, len(PG) * u + len(PG) + gi + 1)
            eng.wait_ge(pv_done, u + 2)
            m = P if b < tiles else FRAMES
            dst = probs_t[0:m, a:b, :]
            src = p_ps[0:m, gi % 2, 0:(b - a) * P].rearrange("p (t q) -> p t q", q=P)
            if gi % 2:
                eng.activation(dst, src, ACT.Copy).then_inc(pt_odd, 1)
            else:
                eng.tensor_copy(dst, src).then_inc(pt_even, 1)

        @block.scalar
        def _(act):
            act.nop().then_inc(kt_odd, KE)
            act.nop().then_inc(s_copied, SG)
            if not diff:
                act.wait_ge(later_loaded, 32)
                act.activation(select[:], select_raw[:], ACT.Copy).then_inc(select_done, 1)
            act.nop().then_inc(exp_done, 1)
            act.nop().then_inc(pt_odd, PO_)
            if diff:
                act.wait_ge(lam_done, 2)
                act.activation(lam_exp[:], lam_sum[:], ACT.Exp).then_inc(lam_exp_done, 1)

            def copy_p(i, k):
                for gi in range(1, len(PG), 2):
                    copy_probs(act, 2 * i + k, gi)

            def copy_scores(u, x):
                n = FRAMES if x == parts else span
                act.wait_ge(s_done, SG * u + SG + x + 1)
                if x == 0:
                    act.wait_ge(exp_done, u + 1)
                act.activation(scores[:, x * span:x * span + n], s_ps[:, x % 2, 0:n], ACT.Copy).then_inc(s_copied, 1)

            def step(i, k, is_first):
                u = 2 * i + k
                if not diff:
                    act.wait_ge(bias_loaded[k], 32 * i + 32)
                    act.wait_ge(s_done, SG * u + SG)
                    act.activation(bias[:], bias_raw[:, k], ACT.Copy).then_inc(bias_done, 1)
                for x in range(parts + 1):
                    for r in range(4 * x + 1, min(4 * x + 4, KG), 2):
                        copy_kt(act, u, r)
                    if x:
                        copy_scores(u, x - 1)
                copy_scores(u, parts)
                if not is_first:
                    last_unit(copy_p, i, k)
                act.wait_ge(neg_done, u + 1)
                act.wait_ge(p_turned, len(PG) * u + len(PG))
                act.activation(probs[:], scores[:], ACT.Exp, bias=neg_top[:], scale=SCALE,
                               accum_out=total[:]).then_inc(exp_done, 1)

            each_unit(act, step, copy_p)
            act.wait_ge(o_turned, 2)
            act.activation(out[:, pairs * P // 2:], k_ps[:, 1, 0:pairs * P // 2], ACT.Copy).then_inc(out_done, 1)

        @block.vector
        def _(dve):
            dve.nop().then_inc(kt_even, KE)
            dve.nop().then_inc(scaled, 1)
            dve.nop().then_inc(pt_even, PE_)
            dve.nop().then_inc(o_done, OC)
            if diff:
                dve.wait_ge(lam_loaded, 32)
                for x in range(2):
                    dve.tensor_tensor_reduce(lam[:, 2 * x, :], lam[:, 2 * x, :], lam[:, 2 * x + 1, :], 1.0, 0.0,
                                             ALU.mult, ALU.add, lam_sum[:, x:x + 1]).then_inc(lam_done, 1)
                dve.wait_ge(lam_exp_done, 1)
                dve.tensor_scalar(neg_lam[:], lam_exp[:, 1:2], lam_exp[:, 0:1], -LAM_INIT - 1.0, ALU.subtract,
                                  ALU.add).then_inc(lam_done, 1)
                dve.wait_ge(lam_done, 3)
                dve.tensor_scalar(weight[:], odd[:], neg_lam[:], 1.0, ALU.mult, ALU.add).then_inc(lam_done, 1)
                dve.wait_ge(lam_done, 4)
            else:
                dve.wait_ge(later_loaded, 32)
            dve.wait_ge(setup, 4)
            dve.wait_ge(q_loaded, 16)

            def blocks(i, k):
                u, g, b = 2 * i + k, group_of(k), stream_of(i, k)
                for hd in range(2):
                    part = slice(DH * hd, DH * hd + DH)
                    if hd == 0:
                        dve.wait_ge(s_done, SG * u + SG)
                    dve.tensor_scalar(q_blocks[part, :, FRAMES * hd:FRAMES * (hd + 1)],
                                      q_all[part, 4 * g:4 * g + 4, bass.ds(b * FRAMES, FRAMES)], 1.0, None,
                                      ALU.mult).then_inc(q_done, 1)

            def scale_output(i, k):
                u = 2 * i + k
                dve.wait_ge(pv_done, u + 3)
                dve.wait_ge(row_turned, u + 1)
                if diff:
                    dve.tensor_scalar(o_rows[:], o_ps[:, 0, :], inv[:, k:k + 1], weight[:], ALU.mult,
                                      ALU.mult).then_inc(scaled, 1)
                else:
                    dve.tensor_scalar(o_rows[:], o_ps[:, 0, :], inv[:, k:k + 1], None, ALU.mult).then_inc(scaled, 1)

            def copy_out(i, k):
                u, g, b = 2 * i + k, group_of(k), stream_of(i, k)
                o_turn = o_ps[:, 1, :].rearrange("p (j e f) -> p j e f", j=4, e=2)
                dve.wait_ge(row_turned, u + 2)
                if diff:
                    dve.tensor_copy(o_first_head[:], o_turn[:, :, 0, :]).then_inc(o_half, 1)
                    dve.wait_ge(o_half, u + 1)
                    dve.tensor_tensor(out_t[:, 4 * g:4 * g + 4, bass.ds(b * FRAMES, FRAMES)], o_first_head[:],
                                      o_turn[:, :, 1, :], ALU.add).then_inc(o_done, 1)
                else:
                    for hd in range(2):
                        part = slice(DH * hd, DH * hd + DH)
                        dve.tensor_scalar(out_t[part, 4 * g:4 * g + 4, bass.ds(b * FRAMES, FRAMES)],
                                          o_turn[part, :, hd, :], 1.0, None, ALU.mult).then_inc(o_done, 1)

            def copy_p(i, k):
                for gi in range(0, len(PG), 2):
                    copy_probs(dve, 2 * i + k, gi)

            def step(i, k, is_first):
                u = 2 * i + k
                blocks(i, k)
                for r in range(0, 4, 2):
                    copy_kt(dve, u, r)
                for x in range(1, parts):
                    for r in range(4 * x, 4 * x + 4, 2):
                        copy_kt(dve, u, r)
                copy_kt(dve, u, 4 * parts)
                if not is_first:
                    last_unit(copy_p, i, k)
                dve.wait_ge(s_copied, SG * u + 2 * SG)
                dve.tensor_reduce(top[:], scores[:], AX.X, ALU.max).then_inc(top_done, 1)
                dve.wait_ge(top_done, u + 1)
                dve.tensor_scalar(neg_top[:], top[:], -SCALE, None, ALU.mult).then_inc(neg_done, 1)
                dve.wait_ge(exp_done, u + 2)
                dve.reciprocal(inv[:, k:k + 1], total[:]).then_inc(inv_done, 1)
                if not is_first:
                    dve.wait_ge(inv_done, u)
                    last_unit(scale_output, i, k)
                    last_unit(copy_out, i, k)

            def flush(i, k):
                copy_p(i, k)
                dve.wait_ge(inv_done, units)
                scale_output(i, k)
                copy_out(i, k)

            each_unit(dve, step, flush)
            dve.wait_ge(o_turned, 1)
            dve.tensor_copy(out[:, 0:pairs * P // 2], k_ps[:, 0, 0:pairs * P // 2]).then_inc(out_done, 1)


def sample_window(nc, name, qkt, k_cache, v_cache, k_new, v_new, sinks, o):
    keys = WIN + FRAMES
    with Stage(nc, name) as st:
        kc, vc = st.sb("kc", [P, STREAMS, P]), st.sb("vc", [P, STREAMS, P])
        kn, vn = st.sb("kn", [FRAMES, STREAMS, P]), st.sb("vn", [FRAMES, STREAMS, P])
        kt = st.sb("kt", [P, 2, keys])
        q_all = st.sb("q_all", [P, A_GROUP, P])
        q_blocks = st.sb("q_blocks", [P, 2, P])
        probs, probs_t, probs_tn = st.sb("probs", [P, 2, keys]), st.sb("probs_t", [P, 2, P]), st.sb("probs_tn", [FRAMES, 2, P])
        sink, neg_sink = st.sb("sink", [P, 1]), st.sb("neg_sink", [P, 1])
        top, neg_top, total, inv, sink_exp = (st.sb(n, [P, 2]) for n in ("top", "neg_top", "total", "inv", "sink_exp"))
        out_t, out = st.sb("out_t", [P, A_GROUP, P]), st.sb("out", [P, A_KV, A_GROUP, DH])
        ident = st.sb("ident", [P, P])
        k_ps, s_ps, p_ps, o_ps = (st.ps(n, [P, 2, 512]) for n in ("k_ps", "s_ps", "p_ps", "o_ps"))
        (setup, loaded, q_loaded, sink_loaded, sink_done, q_done, k_turned, kt_done, s_done, top_done, neg_done,
         exp_done, sink_exp_done, total_done, inv_done, norm_done, p_turned, pt_done, pv_done, o_done,
         o_turned, out_done, stored) = (st.sem(n) for n in (
             "setup", "loaded", "q_loaded", "sink_loaded", "sink_done", "q_done", "k_turned", "kt_done", "s_done",
             "top_done", "neg_done", "exp_done", "sink_exp_done", "total_done", "inv_done", "norm_done",
             "p_turned", "pt_done", "pv_done", "o_done", "o_turned", "out_done", "stored"))
        block = st.block()

        def staggered(step):
            order = [None] + [(b, b % 2) for b in range(STREAMS)] + [None]
            for old, new in zip(order, order[1:]):
                step(new, old)

        @block.sync
        def _(sp):
            sp.dma_start(kc[:], k_cache.rearrange("b k c -> k b c")).then_inc(loaded, 16)
            sp.dma_start(kn[:], k_new.rearrange("(b f) c -> f b c", f=FRAMES)).then_inc(loaded, 16)
            sp.dma_start(vc[:], v_cache.rearrange("b k c -> k b c")).then_inc(loaded, 16)
            sp.dma_start(vn[:], v_new.rearrange("(b f) c -> f b c", f=FRAMES)).then_inc(loaded, 16)
            for kv in range(A_KV):
                sp.dma_start(q_all[DH * kv:DH * kv + DH], qkt[QA + 256 * kv:QA + 256 * kv + 256, PROMPT:TOKENS].rearrange(
                    "(g d) n -> d g n", d=DH)).then_inc(q_loaded, 16)
            for h in range(A_Q):
                sp.dma_start(sink[h * FRAMES:(h + 1) * FRAMES], rows(sinks[0:1, h:h + 1], FRAMES)).then_inc(sink_loaded, 16)
            sp.wait_ge(out_done, 1)
            sp.dma_start(o[PROMPT:TOKENS, 0:A_Q * DH], out[:].rearrange("p a g d -> p (a g d)")).then_inc(stored, 16)
            sp.wait_ge(stored, 16)

        @block.gpsimd
        def _(pool):
            make_identity(pool, ident, setup)
            pool.memset(q_blocks[:], 0.0).then_inc(setup, 1)

        @block.tensor
        def _(pe):
            pe.nop().then_inc(pv_done, 2)
            pe.wait_ge(setup, 3)

            pe.wait_ge(loaded, 64)

            def step(new, old):
                if new:
                    b, s = new
                    pe.wait_ge(kt_done, b + 1)
                    pe.transpose(k_ps[:, s, 0:P], kc[:, b], ident[:])
                    pe.transpose(k_ps[:, s, P:keys], kn[:, b], ident[0:FRAMES, 0:FRAMES]).then_inc(k_turned, 1)
                    pe.wait_ge(kt_done, b + 2)
                    pe.wait_ge(q_done, 2 * b + 2)
                    pe.matmul(s_ps[:, s, 0:keys], q_blocks[:, s], kt[:, s], start=True, stop=True).then_inc(s_done, 1)
                if old:
                    b, s = old
                    pe.wait_ge(norm_done, b + 1)
                    pe.transpose(p_ps[:, s, 0:P], probs[:, s, 0:WIN], ident[:])
                    pe.transpose(p_ps[0:FRAMES, s, P:2 * P], probs[:, s, WIN:keys], ident[:]).then_inc(p_turned, 1)
                    pe.wait_ge(pt_done, 2 * b + 2)
                    pe.wait_ge(o_done, 2 * b + 2)
                    pe.matmul(o_ps[:, s, 0:P], vc[:, b], probs_t[:, s], start=True, stop=False)
                    pe.matmul(o_ps[:, s, 0:P], vn[:, b], probs_tn[:, s], start=False, stop=True).then_inc(pv_done, 1)

            staggered(step)
            pe.wait_ge(o_done, 2 * STREAMS + 2)
            for g in range(A_GROUP):
                last = pe.transpose(k_ps[:, 0, g * P:(g + 1) * P], out_t[:, g, :], ident[:])
            last.then_inc(o_turned, 1)

        @block.scalar
        def _(act):
            act.wait_ge(sink_loaded, 16 * A_Q)

            def step(new, old):
                if old:
                    b, s = old
                    act.wait_ge(p_turned, b + 1)
                    act.activation(probs_t[:, s], p_ps[:, s, 0:P], ACT.Copy).then_inc(pt_done, 1)
                    act.activation(probs_tn[:, s], p_ps[0:FRAMES, s, P:2 * P], ACT.Copy).then_inc(pt_done, 1)
                if new:
                    b, s = new
                    act.wait_ge(neg_done, b + 1)
                    act.activation(probs[:, s], s_ps[:, s, 0:keys], ACT.Exp, bias=neg_top[:, s:s + 1], scale=SCALE,
                                   accum_out=total[:, s:s + 1]).then_inc(exp_done, 1)
                    act.activation(sink_exp[:, s:s + 1], sink[:], ACT.Exp, bias=neg_top[:, s:s + 1]).then_inc(sink_exp_done, 1)

            staggered(step)

        @block.vector
        def _(dve):
            dve.nop().then_inc(kt_done, 1)
            dve.nop().then_inc(o_done, 2)
            dve.wait_ge(sink_loaded, 16 * A_Q)
            dve.tensor_scalar(neg_sink[:], sink[:], -1.0, None, ALU.mult).then_inc(sink_done, 1)
            dve.wait_ge(sink_done, 1)
            dve.wait_ge(q_loaded, 32)
            dve.wait_ge(setup, 3)

            def step(new, old):
                if new:
                    b, s = new
                    for kv in range(A_KV):
                        part = slice(DH * kv, DH * kv + DH)
                        dve.tensor_scalar(q_blocks[part, s, DH * kv:DH * kv + DH].rearrange("p (g f) -> p g f", f=FRAMES),
                                          q_all[part, :, b * FRAMES:(b + 1) * FRAMES], 1.0, None, ALU.mult).then_inc(q_done, 1)
                    dve.wait_ge(k_turned, b + 1)
                    dve.tensor_copy(kt[:, s], k_ps[:, s, 0:keys]).then_inc(kt_done, 1)
                if old:
                    b, s = old
                    dve.wait_ge(sink_exp_done, b + 1)
                    dve.tensor_tensor(total[:, s:s + 1], total[:, s:s + 1], sink_exp[:, s:s + 1], ALU.add).then_inc(total_done, 1)
                    dve.wait_ge(total_done, b + 1)
                    dve.reciprocal(inv[:, s:s + 1], total[:, s:s + 1]).then_inc(inv_done, 1)
                    dve.wait_ge(inv_done, b + 1)
                    dve.tensor_scalar(probs[:, s], probs[:, s], inv[:, s:s + 1], None, ALU.mult).then_inc(norm_done, 1)
                if new:
                    b, s = new
                    dve.wait_ge(s_done, b + 1)
                    dve.tensor_reduce(top[:, s:s + 1], s_ps[:, s, 0:keys], AX.X, ALU.max).then_inc(top_done, 1)
                    dve.wait_ge(top_done, b + 1)
                    dve.tensor_scalar(neg_top[:, s:s + 1], top[:, s:s + 1], -SCALE, neg_sink[:], ALU.mult,
                                      ALU.min).then_inc(neg_done, 1)
                if old:
                    b, s = old
                    dve.wait_ge(pv_done, b + 3)
                    for kv in range(A_KV):
                        part = slice(DH * kv, DH * kv + DH)
                        dve.tensor_scalar(out_t[part, :, b * FRAMES:(b + 1) * FRAMES],
                                          o_ps[part, s, DH * kv:DH * kv + DH].rearrange("p (g f) -> p g f", f=FRAMES),
                                          1.0, None, ALU.mult).then_inc(o_done, 1)

            staggered(step)
            dve.wait_ge(o_turned, 1)
            dve.tensor_copy(out[:].rearrange("p a g d -> p g a d"),
                            k_ps[:, 0, :].rearrange("p (g a d) -> p g a d", g=A_GROUP, a=A_KV)).then_inc(out_done, 1)


def forget_values(nc, name, y, bias, cache, logf_prompt, logf_sample, ck, neg_c8):
    keys = PAST + FRAMES
    with Stage(nc, name) as st:
        z, soft, low, logf = (st.sb(x, [P, TILES, C_H]) for x in ("z", "soft", "low", "logf"))
        b = st.sb("b", [P, C_H])
        past = st.sb("past", [P, PAST // P, P])
        logf_p, sum_p = st.sb("logf_p", [C_H, PROMPT]), st.sb("sum_p", [C_H, PROMPT])
        sum_hi, sum_lo = st.sb("sum_hi", [C_H, PROMPT], F32R), st.sb("sum_lo", [C_H, PROMPT])
        logf_s, sum_s = st.sb("logf_s", [P, keys]), st.sb("sum_s", [P, keys])
        s_hi, s_lo = st.sb("s_hi", [P, keys], F32R), st.sb("s_lo", [P, keys])
        zeros = st.sb("zeros", [P, keys])
        ident = st.sb("ident", [P, P])
        p_ps, s_ps = st.ps("p_ps", [C_H, PROMPT]), st.ps("s_ps", [P, PAST])
        (setup, loaded, past_loaded, a_done, step, logf_done, turned, copied, new_loaded, summed, scaled,
         stored, zero_done) = (st.sem(x) for x in (
             "setup", "loaded", "past_loaded", "a_done", "step", "logf_done", "turned", "copied",
             "new_loaded", "summed", "scaled", "stored", "zero_done"))
        block = st.block()

        @block.sync
        def _(sp):
            sp.dma_start(z[:], y[:, C_IN - C_H:C_IN].rearrange("(t p) h -> p t h", p=P)).then_inc(loaded, 16)
            sp.dma_start(b[:], rows(bias)).then_inc(loaded, 16)
            for s in range(STREAMS):
                sp.dma_start(past[:, :, s * C_H:(s + 1) * C_H],
                             cache[s].rearrange("(t p) h -> p t h", p=P)).then_inc(past_loaded, 16)
            sp.wait_ge(logf_done, 1)
            sp.dma_start(logf_sample, logf[:, TILES_P, :]).then_inc(stored, 16)
            sp.wait_ge(stored, 16)
            for s in range(STREAMS):
                sp.dma_start(logf_s[s * C_H:(s + 1) * C_H, PAST:],
                             logf_sample[s * FRAMES:(s + 1) * FRAMES].rearrange("f h -> h f"),
                             allow_slow_non_contiguous=True).then_inc(new_loaded, 16)
            sp.dma_start(logf_prompt.rearrange("(t p) h -> p t h", p=P), logf[:, 0:TILES_P, :]).then_inc(stored, 16)
            sp.wait_ge(scaled, 3)
            sp.dma_start(ck[:, 0], sum_hi[:].bitcast(F32)).then_inc(stored, 16)
            sp.dma_start(ck[:, 1], sum_lo[:]).then_inc(stored, 16)
            sp.wait_ge(scaled, 6)
            sp.dma_start(neg_c8[:, 0], s_hi[:].bitcast(F32)).then_inc(stored, 16)
            sp.dma_start(neg_c8[:, 1], s_lo[:]).then_inc(stored, 16)
            sp.wait_ge(stored, 96)

        @block.gpsimd
        def _(pool):
            make_identity(pool, ident, setup)
            pool.memset(zeros[:], 0.0).then_inc(zero_done, 1)

        @block.vector
        def _(dve):
            dve.wait_ge(loaded, 32)
            dve.tensor_tensor(z[:], z[:], b[:].unsqueeze(1).to_broadcast([P, TILES, C_H]), ALU.add).then_inc(step, 1)
            dve.wait_ge(step, 1)
            dve.tensor_scalar(low[:], z[:], 0.0, None, ALU.min).then_inc(step, 1)
            dve.wait_ge(step, 2)
            dve.scalar_tensor_tensor(out=z[:], in0=low[:], scalar=2.0, in1=z[:], op0=ALU.mult,
                                     op1=ALU.subtract).then_inc(step, 1)
            dve.wait_ge(a_done, 2)
            dve.tensor_tensor(logf[:], low[:], soft[:], ALU.subtract).then_inc(logf_done, 1)
            dve.wait_ge(turned, 1)
            dve.tensor_copy(logf_s[:, 0:PAST], s_ps[:]).then_inc(copied, 1)
            dve.wait_ge(turned, 2)
            dve.tensor_copy(logf_p[:], p_ps[:]).then_inc(copied, 1)
            dve.wait_ge(zero_done, 1)
            dve.wait_ge(copied, 2)
            dve.tensor_tensor_scan(sum_p[:], logf_p[:], zeros[0:C_H, 0:PROMPT], 0.0, ALU.add, ALU.add).then_inc(summed, 1)
            dve.wait_ge(summed, 1)
            dve.tensor_scalar(sum_p[:], sum_p[:], -1.0 / SCALE, None, ALU.mult).then_inc(scaled, 1)
            dve.wait_ge(scaled, 1)
            dve.tensor_copy(sum_hi[:], sum_p[:]).then_inc(scaled, 1)
            dve.wait_ge(scaled, 2)
            dve.tensor_tensor(sum_lo[:], sum_p[:], sum_hi[:].bitcast(F32), ALU.subtract).then_inc(scaled, 1)
            dve.wait_ge(new_loaded, 16 * STREAMS)
            dve.tensor_tensor_scan(sum_s[:], logf_s[:], zeros[:], 0.0, ALU.add, ALU.add).then_inc(summed, 1)
            dve.wait_ge(summed, 2)
            dve.tensor_scalar(sum_s[:], sum_s[:], -1.0 / SCALE, None, ALU.mult).then_inc(scaled, 1)
            dve.wait_ge(scaled, 4)
            dve.tensor_copy(s_hi[:], sum_s[:]).then_inc(scaled, 1)
            dve.wait_ge(scaled, 5)
            dve.tensor_tensor(s_lo[:], sum_s[:], s_hi[:].bitcast(F32), ALU.subtract).then_inc(scaled, 1)

        @block.scalar
        def _(act):
            act.wait_ge(step, 3)
            act.activation(soft[:], z[:], ACT.Exp).then_inc(a_done, 1)
            act.wait_ge(a_done, 1)
            act.activation(soft[:], soft[:], ACT.Ln, bias=1.0).then_inc(a_done, 1)

        @block.tensor
        def _(pe):
            pe.wait_ge(setup, 2)
            pe.wait_ge(past_loaded, 16 * STREAMS)
            for t in range(PAST // P):
                last = pe.transpose(s_ps[:, t * P:(t + 1) * P], past[:, t, :], ident[:])
            last.then_inc(turned, 1)
            pe.wait_ge(logf_done, 1)
            for t in range(TILES_P):
                last = pe.transpose(p_ps[:, t * P:(t + 1) * P], logf[:, t, :], ident[:])
            last.then_inc(turned, 1)


def merge(nc, name, o, w, gain, x_in, x_out, gain_next, ht_hi, ht_lo, subnorm=None):
    with Stage(nc, name) as st:
        w_hi, w_lo = st.sb("w_hi", [P, KT, D], F32R), st.sb("w_lo", [P, KT, D], F32R)
        rows_o, x, z, h = (st.sb(n, [P, 2, D]) for n in ("rows_o", "x", "z", "h"))
        raw = [z[:, 0], z[:, 1], h[:, 0], h[:, 1]]
        squares = st.sb("squares", [P, D])
        ot_hi, ot_lo = st.sb("ot_hi", [P, 2, KT, P], F32R), st.sb("ot_lo", [P, 2, KT, P], F32R)
        g, g_next = st.sb("g", [P, D]), st.sb("g_next", [P, D])
        ident, minus_half = st.sb("ident", [P, P]), st.sb("minus_half", [P, B_H])
        total, inv, total_x, inv_x = (st.sb(n, [P, TILES]) for n in ("total", "inv", "total_x", "inv_x"))
        turned, turned_h = st.ps("turned", [P, 2, KT // 2, P]), st.ps("turned_h", [P, 2, KT // 2, P])
        acc = st.ps("acc", [P, 2, D])
        o_loaded, x_loaded, z_stored = (st.sems(n, 2) for n in ("o_loaded", "x_loaded", "z_stored"))
        w_loaded = st.sems("w_loaded", len(raw))
        (setup, g_loaded, whi_done, wlo_done, turned_done, hi_done, lo_done, mm_done, total_done,
         inv_done, z_done, sum_done, total_x_done, inv_x_done, h_done, h_turned, hhi_done, hlo_done) = (
             st.sem(n) for n in (
                 "setup", "g_loaded", "whi_done", "wlo_done", "turned_done", "hi_done", "lo_done", "mm_done",
                 "total_done", "inv_done", "z_done", "sum_done", "total_x_done", "inv_x_done", "h_done",
                 "h_turned", "hhi_done", "hlo_done"))
        if subnorm is not None:
            gs = st.sb("gs", [P, P])
            sub_sq = st.sb("sub_sq", [P, B_H, P])
            sub_total, sub_inv = (st.sb(n, [P, TILES, B_H]) for n in ("sub_total", "sub_inv"))
            sub_total_done, sub_inv_done, sub_done = (st.sem(n) for n in ("sub_total_done", "sub_inv_done", "sub_done"))
        first = D - B_H * P
        block = st.block()

        halves = [(half, slice(half * KT // 2, (half + 1) * KT // 2)) for half in range(2)]

        @block.sync
        def _(sp):
            def load_o(t):
                sp.dma_start(rows_o[:, t % 2], o[t * P:(t + 1) * P]).then_inc(o_loaded[t % 2], 16)

            def load_x(t):
                sp.dma_start(x[:, t % 2], x_in[t * P:(t + 1) * P]).then_inc(x_loaded[t % 2], 16)

            def store(t):
                sp.wait_ge(sum_done, t + 1)
                sp.dma_start(x_out(t), z[:, t % 2]).then_inc(z_stored[t % 2], 16)

            load_o(0)
            load_o(1)
            if subnorm is not None:
                sp.dma_start(gs[:], rows(subnorm)).then_inc(g_loaded, 16)
            sp.dma_start(g[:], rows(gain)).then_inc(g_loaded, 16)
            sp.dma_start(g_next[:], rows(gain_next)).then_inc(g_loaded, 16)
            for k in range(KT):
                if k >= len(raw):
                    sp.wait_ge(wlo_done, k - len(raw) + 1)
                sp.dma_start(raw[k % len(raw)], w[k * P:(k + 1) * P]).then_inc(w_loaded[k % len(raw)], 16)
            load_x(0)
            for t in range(TILES):
                if t + 2 < TILES:
                    sp.wait_ge(turned_done, 2 * t + 2)
                    load_o(t + 2)
                if t >= 1:
                    store(t - 1)
                if t + 1 < TILES:
                    load_x(t + 1)
            store(TILES - 1)
            for s in range(2):
                sp.wait_ge(z_stored[s], 16 * len(range(s, TILES, 2)))

        @block.gpsimd
        def _(pool):
            make_identity(pool, ident, setup)
            pool.memset(minus_half[:], -0.5).then_inc(setup, 1)
            pool.wait_ge(setup, 3)

            def sub(t):
                if subnorm is None or t >= TILES:
                    return
                pool.wait_ge(sub_total_done, B_H * (t + 1))
                scale = 1.0 / (1.0 - LAM_INIT) ** 2
                inverse_root(pool, sub_total[:, t], scale / P, scale * EPS, minus_half[:], sub_inv[:, t],
                             sub_inv_done, 2 * t)

            def norm(t):
                pool.wait_ge(total_done, t + 1)
                inverse_root(pool, total[:, t:t + 1], 1.0 / D, EPS, minus_half[:, 0:1], inv[:, t:t + 1],
                             inv_done, 2 * t)

            def add(t):
                pool.wait_ge(x_loaded[t % 2], 16 * (t // 2 + 1))
                pool.wait_ge(z_done, t + 1)
                pool.tensor_tensor(z[:, t % 2], z[:, t % 2], x[:, t % 2], ALU.add).then_inc(sum_done, 1)

            def norm_x(t):
                pool.wait_ge(total_x_done, t + 1)
                inverse_root(pool, total_x[:, t:t + 1], 1.0 / D, EPS, minus_half[:, 0:1], inv_x[:, t:t + 1],
                             inv_x_done, 2 * t)

            sub(0)
            sub(1)
            for t in range(TILES + 1):
                if t >= 1:
                    norm(t - 1)
                sub(t + 2)
                if t >= 1:
                    add(t - 1)
                    norm_x(t - 1)

        @block.tensor
        def _(pe):
            def turn_o(t, s, turn, again):
                pe.wait_ge(o_loaded[s], 16 * turn + 16)
                if subnorm is not None:
                    pe.wait_ge(sub_done, B_H * t + B_H)
                for half, ks in halves:
                    if again:
                        pe.wait_ge(lo_done, 2 * t + half - 1)
                    for k in range(KT // 2):
                        c = (half * KT // 2 + k) * P
                        last = pe.transpose(turned[:, half, k, :], rows_o[:, s, c:c + P], ident[:])
                    last.then_inc(turned_done, 1)

            def turn_h(t, s, again):
                pe.wait_ge(h_done, t + 1)
                for half, ks in halves:
                    if again:
                        pe.wait_ge(hlo_done, 2 * t + half - 1)
                    for k in range(KT // 2):
                        c = (half * KT // 2 + k) * P
                        last = pe.transpose(turned_h[:, half, k, :], h[:, s, c:c + P], ident[:])
                    last.then_inc(h_turned, 1)

            def multiply(t, s, again):
                pe.wait_ge(lo_done, 2 * t + 2)
                if again:
                    pe.wait_ge(z_done, t - 1)
                for half in range(2):
                    for k in range(KT):
                        last = multiply_piece(s, half, k)
                last.then_inc(mm_done, 1)

            def multiply_piece(s, half, k):
                for j, (a, b) in enumerate(((ot_hi, w_hi), (ot_hi, w_lo), (ot_lo, w_hi))):
                    last = pe.matmul(acc[:, s, half * 512:half * 512 + 512], a[:, s, k, :],
                                     b[:, k, half * 512:half * 512 + 512],
                                     start=(k == 0 and j == 0), stop=(k == KT - 1 and j == 2))
                return last

            def multiply_first():
                pe.wait_ge(lo_done, 2)
                for k in range(KT):
                    pe.wait_ge(wlo_done, k + 1)
                    for half in range(2):
                        last = multiply_piece(0, half, k)
                last.then_inc(mm_done, 1)

            pe.wait_ge(setup, 2)
            turn_o(0, 0, 0, False)
            for t in range(4):
                turn_o(t + 1, (t + 1) % 2, (t + 1) // 2, True)
                if t >= 2:
                    turn_h(t - 2, t % 2, t >= 3)
                if t == 0:
                    multiply_first()
                else:
                    multiply(t, t % 2, t >= 2)
            with pe.Fori(2, TILES_P // 2) as i:
                for s in range(2):
                    t = 2 * i + s
                    if s == 0:
                        turn_o(t + 1, 1, i, True)
                    else:
                        turn_o(t + 1, 0, i + 1, True)
                    turn_h(t - 2, s, True)
                    multiply(t, s, True)
            turn_h(TILES - 3, 0, True)
            multiply(TILES - 1, 0, True)
            turn_h(TILES - 2, 1, True)
            turn_h(TILES - 1, 0, True)

        @block.scalar
        def _(act):
            def sub_squares(t):
                if subnorm is None or t >= TILES:
                    return
                act.wait_ge(o_loaded[t % 2], 16 * (t // 2 + 1))
                if t:
                    act.wait_ge(sub_total_done, B_H * t)
                for q in range(B_H):
                    act.activation(sub_sq[:, q], rows_o[:, t % 2, first + q * P:first + (q + 1) * P], ACT.Square,
                                   accum_out=sub_total[:, t, q:q + 1]).then_inc(sub_total_done, 1)

            def high_o(t):
                if t >= TILES:
                    return
                for half, ks in halves:
                    act.wait_ge(turned_done, 2 * t + half + 1)
                    if t >= 2:
                        act.wait_ge(mm_done, t - 1)
                    act.activation(ot_hi[:, t % 2, ks], turned[:, half], ACT.Copy).then_inc(hi_done, 1)

            def high_h(t):
                for half, ks in halves:
                    act.wait_ge(h_turned, 2 * t + half + 1)
                    act.activation(ht_hi[:, ks, t * P:(t + 1) * P], turned_h[:, half], ACT.Copy).then_inc(hhi_done, 1)

            def square(t):
                act.wait_ge(mm_done, t + 1)
                if t >= 1:
                    act.wait_ge(total_x_done, t)
                act.activation(squares[:], acc[:, t % 2], ACT.Square, accum_out=total[:, t:t + 1]).then_inc(total_done, 1)

            def square_x(t):
                act.wait_ge(sum_done, t + 1)
                act.wait_ge(total_done, t + 1)
                act.activation(squares[:], z[:, t % 2], ACT.Square, accum_out=total_x[:, t:t + 1]).then_inc(total_x_done, 1)

            sub_squares(0)
            sub_squares(1)
            high_o(0)
            for k in range(KT):
                act.wait_ge(w_loaded[k % len(raw)], 16 * (k // len(raw) + 1))
                act.activation(w_hi[:, k], raw[k % len(raw)], ACT.Copy).then_inc(whi_done, 1)
            for t in range(TILES + 2):
                high_o(t + 1)
                if 1 <= t <= TILES:
                    square(t - 1)
                if t >= 2:
                    high_h(t - 2)
                sub_squares(t + 2)
                if 1 <= t <= TILES:
                    square_x(t - 1)

        @block.vector
        def _(dve):
            def sub_scale(t):
                if subnorm is None or t >= TILES:
                    return
                dve.wait_ge(sub_inv_done, 2 * t + 2)
                for q in range(B_H):
                    part = rows_o[:, t % 2, first + q * P:first + (q + 1) * P]
                    dve.scalar_tensor_tensor(out=part, in0=part, scalar=sub_inv[:, t, q:q + 1], in1=gs[:],
                                             op0=ALU.mult, op1=ALU.mult).then_inc(sub_done, 1)

            def low_o(t):
                if t >= TILES:
                    return
                for half, ks in halves:
                    dve.wait_ge(hi_done, 2 * t + half + 1)
                    dve.tensor_tensor(ot_lo[:, t % 2, ks], turned[:, half], ot_hi[:, t % 2, ks].bitcast(F32),
                                      ALU.subtract).then_inc(lo_done, 1)

            def low_h(t):
                for half, ks in halves:
                    dve.wait_ge(hhi_done, 2 * t + half + 1)
                    token = slice(t * P, (t + 1) * P)
                    dve.tensor_tensor(ht_lo[:, ks, token], turned_h[:, half], ht_hi[:, ks, token].bitcast(F32),
                                      ALU.subtract).then_inc(hlo_done, 1)

            def scale_rows(t):
                dve.wait_ge(inv_done, 2 * t + 2)
                if t >= 2:
                    dve.wait_ge(z_stored[t % 2], 16 * (t // 2))
                dve.scalar_tensor_tensor(out=z[:, t % 2], in0=acc[:, t % 2], scalar=inv[:, t:t + 1], in1=g[:],
                                         op0=ALU.mult, op1=ALU.mult).then_inc(z_done, 1)

            def scale_h(t):
                dve.wait_ge(inv_x_done, 2 * t + 2)
                if t >= 2:
                    dve.wait_ge(h_turned, 2 * (t - 1))
                dve.scalar_tensor_tensor(out=h[:, t % 2], in0=z[:, t % 2], scalar=inv_x[:, t:t + 1], in1=g_next[:],
                                         op0=ALU.mult, op1=ALU.mult).then_inc(h_done, 1)

            dve.wait_ge(g_loaded, 32 if subnorm is None else 48)
            sub_scale(0)
            sub_scale(1)
            low_o(0)
            for k in range(KT):
                dve.wait_ge(whi_done, k + 1)
                dve.tensor_tensor(w_lo[:, k], raw[k % len(raw)], w_hi[:, k].bitcast(F32), ALU.subtract).then_inc(wlo_done, 1)
            dve.wait_ge(wlo_done, KT)
            for t in range(TILES + 2):
                low_o(t + 1)
                if 1 <= t <= TILES:
                    scale_rows(t - 1)
                if t >= 2:
                    low_h(t - 2)
                sub_scale(t + 2)
                if 1 <= t <= TILES:
                    scale_h(t - 1)


def feed_forward(nc, name, x_in, ht_hi, ht_lo, w_in, w_out, gain, x_out, gain_next=None):
    following = gain_next is not None
    pieces = D_FF // P
    groups, gw = 3, TOKENS // 3
    with Stage(nc, name) as st:
        y = st.sb("y", [P, TILES, D])
        g_in = w_in.rearrange("(k p) (u n) -> p k u n", p=P, u=2)
        w_out_v = w_out.rearrange("(f p) n -> p f n", p=P)
        raw = st.sb("raw", [P, 2, KT, 2, P])
        w_hi, w_lo = st.sb("w_hi", [P, 2, KT, 2, P], F32R), st.sb("w_lo", [P, 2, KT, 2, P], F32R)
        raw_o = st.sb("raw_o", [P, 2, D])
        wo_hi, wo_lo = st.sb("wo_hi", [P, 2, D], F32R), st.sb("wo_lo", [P, 2, D], F32R)
        act_hi, act_lo = st.sb("act_hi", [P, 2, TOKENS], F32R), st.sb("act_lo", [P, 2, TOKENS], F32R)
        gated = st.sb("gated", [P, 4, gw])
        silu, prod = gated[:, 0:2], gated[:, 2:4]
        gate, up = st.ps("gate", [P, 3, 512]), st.ps("up", [P, 3, 512])
        down = st.ps("down", [P, 2, 512])
        raw_loaded = st.sems("raw_loaded", 2)
        (ol_loaded, hi_done, lo_done, up_done, silu_done, prod_done, acthi_done, actlo_done,
         ohi_done, olo_done, down_done, added, zeroed) = (st.sem(n) for n in (
             "ol_loaded", "hi_done", "lo_done", "up_done", "silu_done", "prod_done", "acthi_done",
             "actlo_done", "ohi_done", "olo_done", "down_done", "added", "zeroed"))
        outs = 2 * TILES
        x = [raw[:, 0].rearrange("p k u n -> p (k u n)")[:, s * D:(s + 1) * D] for s in range(2)]
        g, g_next = (raw[:, 1].rearrange("p k u n -> p (k u n)")[:, s * D:(s + 1) * D] for s in range(2))
        h = [raw_o[:, 1], gated[:].rearrange("p a n -> p (a n)")[:, 0:D]]
        squares = raw_o[:, 0]
        turned = gate[:, 0:2].rearrange("p a (k n) -> p a k n", n=P)
        ident, minus_half = st.sb("ident", [P, P]), st.sb("minus_half", [P, 1])
        total, inv, total_x, inv_x = (st.sb(n, [P, TILES]) for n in ("total", "inv", "total_x", "inv_x"))
        x_loaded = st.sems("x_loaded", 2)
        (setup, g_loaded, total_done, inv_done, scaled, sum_done, stored, total_x_done, inv_x_done,
         h_done, h_turned, hhi_done, hlo_done) = (st.sem(n) for n in (
             "setup", "g_loaded", "total_done", "inv_done", "scaled", "sum_done", "stored",
             "total_x_done", "inv_x_done", "h_done", "h_turned", "hhi_done", "hlo_done"))
        halves = [(half, slice(half * KT // 2, (half + 1) * KT // 2)) for half in range(2)]
        last_pair = pieces // 2 - 1
        block = st.block()


        @block.sync
        def _(sp):
            with sp.Fori(0, pieces // 2) as i:
                for s in range(2):
                    f = 2 * i + s
                    sp.wait_ge(lo_done, f + 1)
                    for u in range(2):
                        sp.dma_start(raw[:, s, :, u, :], g_in[:, :, u, bass.ds(f * P, P)]).then_inc(raw_loaded[s], 16)
                sp.wait_ge(olo_done, i + 1)
                sp.dma_start(raw_o[:], w_out_v[:, bass.ds(2 * i, 2), :]).then_inc(ol_loaded, 16)

            def load_x(t):
                sp.dma_start(x[t % 2], x_in[t * P:(t + 1) * P]).then_inc(x_loaded[t % 2], 16)

            sp.wait_ge(lo_done, 2 + pieces)
            load_x(0)
            sp.dma_start(g, rows(gain)).then_inc(g_loaded, 16)
            if following:
                sp.dma_start(g_next, rows(gain_next)).then_inc(g_loaded, 16)
            load_x(1)
            for t in range(TILES):
                sp.wait_ge(sum_done, t + 1)
                sp.dma_start(x_out(t), y[:, t]).then_inc(stored, 16)
                if t + 2 < TILES:
                    load_x(t + 2)
            sp.wait_ge(stored, 16 * TILES)

        @block.scalar
        def _(act):
            def split_in(i, s):
                act.wait_ge(raw_loaded[s], 32 * i + 32)
                act.wait_ge(up_done, 3 * (2 * i + s) + 3)
                act.activation(w_hi[:, s], raw[:, s], ACT.Copy).then_inc(hi_done, 1)

            def silus(i, s):
                f = 2 * i + s
                for q in range(groups):
                    m = 3 * f + q
                    act.wait_ge(up_done, 6 + m + 1)
                    b = (3 * s + q) % 2
                    act.wait_ge(actlo_done, m + 1)
                    act.activation(silu[:, b], gate[:, q, 0:gw], ACT.Silu).then_inc(silu_done, 1)
                    act.wait_ge(prod_done, 3 + m + 1)
                    act.wait_ge(down_done, outs * i + outs)
                    act.activation(act_hi[:, s, q * gw:(q + 1) * gw], prod[:, b], ACT.Copy).then_inc(acthi_done, 1)

            def pair(i, more):
                split_in(i, 1)
                act.wait_ge(ol_loaded, 16 * i + 16)
                act.wait_ge(down_done, outs * i + outs)
                act.activation(wo_hi[:], raw_o[:], ACT.Copy).then_inc(ohi_done, 1)
                silus(i, 0)
                if more:
                    split_in(i + 1, 0)
                silus(i, 1)

            split_in(0, 0)
            with act.Fori(0, pieces // 2 - 1) as i:
                pair(i, True)
            pair(pieces // 2 - 1, False)

            def square(t):
                if t == 0:
                    act.wait_ge(olo_done, 2 + last_pair)
                elif following and t >= 2:
                    act.wait_ge(total_x_done, t - 1)
                else:
                    act.wait_ge(total_done, t)
                act.wait_ge(added, 2 + outs * last_pair + 2 * t + 2)
                act.activation(squares, y[:, t], ACT.Square, accum_out=total[:, t:t + 1]).then_inc(total_done, 1)

            def square_x(t):
                act.wait_ge(total_done, min(t + 2, TILES))
                act.wait_ge(sum_done, t + 1)
                act.activation(squares, y[:, t], ACT.Square, accum_out=total_x[:, t:t + 1]).then_inc(total_x_done, 1)

            def high(t):
                for half, ks in halves:
                    act.wait_ge(h_turned, 2 * t + half + 1)
                    act.activation(ht_hi[:, ks, t * P:(t + 1) * P], turned[:, half], ACT.Copy).then_inc(hhi_done, 1)

            for t in range(TILES + 3):
                if t < TILES:
                    square(t)
                if following:
                    if t >= 3:
                        high(t - 3)
                    if 1 <= t <= TILES:
                        square_x(t - 1)

        @block.vector
        def _(dve):
            dve.nop().then_inc(lo_done, 2)
            dve.nop().then_inc(prod_done, 3)
            dve.nop().then_inc(actlo_done, 2)
            dve.nop().then_inc(olo_done, 1)
            dve.nop().then_inc(added, 2)

            def split_in(i, s):
                dve.wait_ge(hi_done, 2 * i + s + 1)
                dve.tensor_tensor(w_lo[:, s], raw[:, s], w_hi[:, s].bitcast(F32), ALU.subtract).then_inc(lo_done, 1)

            def products(i, s):
                f = 2 * i + s
                for q in range(groups):
                    m = 3 * f + q
                    b = (3 * s + q) % 2
                    dve.wait_ge(silu_done, m + 1)
                    dve.tensor_tensor(prod[:, b], silu[:, b], up[:, q, 0:gw], ALU.mult).then_inc(prod_done, 1)
                    dve.wait_ge(acthi_done, m + 1)
                    part = slice(q * gw, (q + 1) * gw)
                    dve.tensor_tensor(act_lo[:, s, part], prod[:, b], act_hi[:, s, part].bitcast(F32),
                                      ALU.subtract).then_inc(actlo_done, 1)

            def pair(i, more):
                split_in(i, 1)
                dve.wait_ge(ohi_done, i + 1)
                dve.tensor_tensor(wo_lo[:], raw_o[:], wo_hi[:].bitcast(F32), ALU.subtract).then_inc(olo_done, 1)
                products(i, 0)
                if more:
                    split_in(i + 1, 0)
                products(i, 1)
                if more:
                    for t in range(TILES):
                        add(i, t)

            def add(i, t):
                for half in range(2):
                    d = outs * i + 2 * t + half
                    part = y[:, t, half * 512:(half + 1) * 512]
                    dve.wait_ge(down_done, outs + d + 1)
                    dve.wait_ge(added, 2 + outs * i)
                    dve.tensor_tensor(part, part, down[:, half, :], ALU.add).then_inc(added, 1)

            def scale_rows(t):
                dve.wait_ge(inv_done, 2 * t + 2)
                dve.scalar_tensor_tensor(out=y[:, t], in0=y[:, t], scalar=inv[:, t:t + 1], in1=g,
                                         op0=ALU.mult, op1=ALU.mult).then_inc(scaled, 1)

            def scale_h(t):
                dve.wait_ge(inv_x_done, 2 * t + 2)
                if t >= 2:
                    dve.wait_ge(h_turned, 2 * (t - 1))
                dve.scalar_tensor_tensor(out=h[t % 2], in0=y[:, t], scalar=inv_x[:, t:t + 1], in1=g_next,
                                         op0=ALU.mult, op1=ALU.mult).then_inc(h_done, 1)

            def low(t):
                for half, ks in halves:
                    dve.wait_ge(hhi_done, 2 * t + half + 1)
                    token = slice(t * P, (t + 1) * P)
                    dve.tensor_tensor(ht_lo[:, ks, token], turned[:, half], ht_hi[:, ks, token].bitcast(F32),
                                      ALU.subtract).then_inc(hlo_done, 1)

            dve.wait_ge(zeroed, TILES)
            split_in(0, 0)
            with dve.Fori(0, pieces // 2 - 1) as i:
                pair(i, True)
            pair(pieces // 2 - 1, False)
            dve.wait_ge(g_loaded, 32 if following else 16)
            dve.wait_ge(actlo_done, 2 + 3 * pieces)
            for t in range(TILES + 3):
                if t < TILES:
                    add(last_pair, t)
                if 1 <= t <= TILES:
                    scale_rows(t - 1)
                if following:
                    if 2 <= t <= TILES + 1:
                        scale_h(t - 2)
                    if t >= 3:
                        low(t - 3)

        @block.gpsimd
        def _(pool):
            for t in range(TILES):
                pool.memset(y[:, t], 0.0).then_inc(zeroed, 1)
            make_identity(pool, ident, setup)
            pool.memset(minus_half[:], -0.5).then_inc(setup, 1)
            pool.wait_ge(setup, 3)

            def norm(t, sums, roots, summed, done):
                pool.wait_ge(summed, t + 1)
                inverse_root(pool, sums[:, t:t + 1], 1.0 / D, EPS, minus_half[:], roots[:, t:t + 1], done, 2 * t)

            for t in range(TILES + 1):
                if t < TILES:
                    norm(t, total, inv, total_done, inv_done)
                if t >= 1:
                    pool.wait_ge(x_loaded[(t - 1) % 2], 16 * ((t - 1) // 2 + 1))
                    pool.wait_ge(scaled, t)
                    pool.tensor_tensor(y[:, t - 1], y[:, t - 1], x[(t - 1) % 2], ALU.add).then_inc(sum_done, 1)
                    if following:
                        norm(t - 1, total_x, inv_x, total_x_done, inv_x_done)

        @block.tensor
        def _(pe):
            pe.nop().then_inc(up_done, 6)
            pe.nop().then_inc(down_done, outs)

            def products(i, s):
                f = 2 * i + s
                pe.wait_ge(lo_done, 2 + f + 1)
                for q in range(groups):
                    pe.wait_ge(prod_done, 3 * f + q + 1)
                    token = slice(q * gw, (q + 1) * gw)
                    for u, acc in enumerate((gate, up)):
                        for k in range(KT):
                            for j, (a, b) in enumerate(((w_hi, ht_hi), (w_hi, ht_lo), (w_lo, ht_hi))):
                                last = pe.matmul(acc[:, q, 0:gw], a[:, s, k, u, :], b[:, k, token],
                                                 start=(k == 0 and j == 0), stop=(k == KT - 1 and j == 2))
                    last.then_inc(up_done, 1)

            def output(i, t):
                if t * P % gw == 0:
                    pe.wait_ge(actlo_done, 2 + 6 * i + 3 + t * P // gw + 1)
                for half in range(2):
                    pe.wait_ge(added, outs * i + 2 * t + half + 1)
                    n = 0
                    for s in range(2):
                        for a, b in ((act_hi, wo_hi), (act_hi, wo_lo), (act_lo, wo_hi)):
                            last = pe.matmul(down[:, half, :], a[:, s, t * P:(t + 1) * P],
                                             b[:, s, half * 512:(half + 1) * 512], start=(n == 0), stop=(n == 5))
                            n += 1
                    last.then_inc(down_done, 1)

            def turn(t):
                pe.wait_ge(h_done, t + 1)
                for half, ks in halves:
                    if t >= 1:
                        pe.wait_ge(hlo_done, 2 * t + half - 1)
                    for k in range(KT // 2):
                        c = (half * KT // 2 + k) * P
                        last = pe.transpose(turned[:, half, k, :], h[t % 2][:, c:c + P], ident[:])
                    last.then_inc(h_turned, 1)

            with pe.Fori(0, last_pair) as i:
                products(i, 0)
                products(i, 1)
                pe.wait_ge(olo_done, 1 + i + 1)
                for t in range(TILES):
                    output(i, t)
            products(last_pair, 0)
            products(last_pair, 1)
            pe.wait_ge(olo_done, 1 + last_pair + 1)
            if following:
                pe.wait_ge(setup, 3)
                pe.wait_ge(prod_done, 3 + 3 * pieces)
            for t in range(TILES + 3):
                if t < TILES:
                    output(last_pair, t)
                if following and t >= 3:
                    turn(t - 3)


def rope_table():
    prompt = np.arange(PROMPT)
    samples = np.tile(PAST + np.arange(FRAMES), STREAMS)
    pos = np.concatenate([prompt, samples]).astype(np.float32)
    freq = np.float32(10000.0) ** (-np.arange(HALF, dtype=np.float32) / np.float32(HALF))
    angle = pos[:, None] * freq.astype(np.float32)[None]
    cos, sin = np.cos(angle), np.sin(angle)
    table = np.stack([np.concatenate([cos, cos], 1), np.concatenate([-sin, sin], 1)], 1)
    return np.ascontiguousarray(table.reshape(TILES, P, 2, DH).transpose(1, 0, 2, 3).astype(np.float32))


def frame_mask():
    frame = np.arange(P) % FRAMES
    return np.where(np.arange(FRAMES)[None] <= frame[:, None], 0.0, NEG).astype(np.float32)


def odd_heads():
    return ((np.arange(P) // FRAMES) % 2).astype(np.float32)[:, None]


def head_rows():
    return (np.arange(P)[None] // FRAMES == np.arange(16)[:, None] % 8).astype(np.float32)


def build(nc, a, out):
    x0, x1, x2, x3 = (nc.dram_tensor(f"x{i}", (TOKENS, D), F32, kind="Internal").ap() for i in range(4))
    y_ab = nc.dram_tensor("y_ab", (TOKENS, AB_IN), F32, kind="Internal").ap()
    y_c = nc.dram_tensor("y_c", (TOKENS, C_IN), F32, kind="Internal").ap()
    qkt_ab = nc.dram_tensor("qkt_ab", (13 * P, TOKENS), F32, kind="Internal").ap()
    qkt_c = nc.dram_tensor("qkt_c", (2 * D, TOKENS), F32, kind="Internal").ap()
    o_ab, o_c = (nc.dram_tensor(n, (TOKENS, D), F32, kind="Internal").ap() for n in ("o_ab", "o_c"))
    ck = nc.dram_tensor("ck", (C_H, 2, PROMPT), F32, kind="Internal").ap()
    neg_c8 = nc.dram_tensor("neg_c8", (P, 2, PAST + FRAMES), F32, kind="Internal").ap()

    xp, xs = a["x_prompt"][0], a["x_sample"].rearrange("s f d -> (s f) d")
    gains = a["norm_gains"]

    def gain(layer, which):
        return gains[layer, which:which + 1, :]

    def flat(ap):
        return ap[0].rearrange("s t h d -> (s t) (h d)")

    def by_stream(ap):
        return ap[0].rearrange("s t h d -> s t (h d)")

    def columns(st):
        return st.sb("ht_hi", [P, KT, TOKENS], F32R), st.sb("ht_lo", [P, KT, TOKENS], F32R)

    samples = slice(PROMPT, TOKENS)

    with Stage(nc, "ab") as st:
        ht_hi, ht_lo = columns(st)
        norm_to_columns(nc, "abn", lambda t: xp[t * P:(t + 1) * P] if t < TILES_P else xs, gain(0, 0), ht_hi, ht_lo)
        project(nc, "abp", ht_hi, ht_lo, a["w_ab_in"][0], y_ab)
    keep = WIN - FRAMES
    direct = [
        (x0[samples], xs),
        (flat(out["a_v_prompt"]), y_ab[PROMPT - WIN:PROMPT, VA:QB]),
        (flat(out["b_v_sample"]), y_ab[samples, VB:]),
        (by_stream(out["a_k_sample"])[:, 0:keep], by_stream(a["cache_a_k"])[:, FRAMES:]),
        (by_stream(out["a_v_sample"])[:, 0:keep], by_stream(a["cache_a_v"])[:, FRAMES:]),
        (by_stream(out["a_v_sample"])[:, keep:], y_ab[samples, VA:QB].rearrange("(s f) c -> s f c", f=FRAMES)),
    ]
    k_a = (KA, KA + A_KV * DH)
    k_b = (13 * P - 2 * B_H * DH, 13 * P)
    ka_new = nc.dram_tensor("ka_new", (P, A_KV * DH), F32, kind="Internal").ap()

    def rotated(t, z):
        z_a, z_b = z[:, k_a[0]:k_a[1]], z[:, k_b[0]:k_b[1]]
        if t == TILES_P:
            return [(flat(out["b_k_sample"]), z_b), (ka_new, z_a)] + [
                (out["a_k_sample"][0, s, keep:].rearrange("f h d -> f (h d)"), z_a[s * FRAMES:(s + 1) * FRAMES])
                for s in range(STREAMS)]
        res = [(flat(out["b_k_prompt"])[t * P:(t + 1) * P], z_b)]
        if t == TILES_P - 1:
            res.append((flat(out["a_k_prompt"]), z_a))
        return res

    turn_columns(nc, "abt", y_ab, [(QA, VA), (QB, VB - QB)], a["rope_table"], qkt_ab, direct, rotated)
    prompt_attention(nc, "pa", A_Q // 2, lambda i, e: (2 * i + e) * DH, lambda i, e: KA + (i // 2) * DH,
                     lambda i, e: VA + (i // 2) * DH, lambda i, e: (2 * i + e) * DH, qkt_ab, y_ab, o_ab, DH,
                     window=True, sinks=a["a_sinks"])
    share = PROMPT // B_H

    def copies_b(i):
        some = bass.ds(i * share, share)
        return [(x0[some], xp[some]), (flat(out["b_v_prompt"])[some], y_ab[some, VB:])]

    q_b, kt_b = VA, k_b[0]
    prompt_attention(nc, "pb", B_H, lambda i, e: q_b + (2 * i + e) * DH, lambda i, e: kt_b + (2 * i + e) * DH,
                     lambda i, e: VB + i * P, lambda i, e: A_Q * DH + i * P, qkt_ab, y_ab, o_ab, P,
                     b_lambda=a["b_lambda"][0], copies=copies_b)
    sample_window(nc, "sa", qkt_ab, by_stream(a["cache_a_k"]), by_stream(a["cache_a_v"]), ka_new,
                  y_ab[samples, VA:QB], a["a_sinks"], o_ab)
    sample_attention(nc, "sb", 1, q_b, qkt_ab, by_stream(a["cache_b_k"]), by_stream(a["cache_b_v"]),
                     flat(out["b_k_sample"]), y_ab[samples, VB:], o_ab, A_Q * DH,
                     row_odd=a["odd_heads"], b_lambda=a["b_lambda"][0])
    with Stage(nc, "m0") as st:
        ht_hi, ht_lo = columns(st)
        merge(nc, "abm", o_ab, a["w_ab_out"][0], gain(0, 1), x0, lambda t: x1[t * P:(t + 1) * P], gain(0, 2),
              ht_hi, ht_lo, subnorm=a["b_subln"])
        feed_forward(nc, "f0", x1, ht_hi, ht_lo, a["w_ffn_in"][0], a["w_ffn_out"][0], gain(0, 3),
                     lambda t: x2[t * P:(t + 1) * P], gain_next=gain(1, 0))

        project(nc, "c", ht_hi, ht_lo, a["w_c_in"][0], y_c)
    direct = [(flat(out["c_k_sample"]), y_c[samples, D:2 * D]), (flat(out["c_v_sample"]), y_c[samples, 2 * D:3 * D])]

    def copies_c(i):
        some = bass.ds(i * P, P)
        return [(flat(out["c_k_prompt"])[some], y_c[some, D:2 * D]),
                (flat(out["c_v_prompt"])[some], y_c[some, 2 * D:3 * D])]

    turn_columns(nc, "ct", y_c, [(0, 2 * D)], None, qkt_c, direct, lambda t, z: [])
    forget_values(nc, "cf", y_c, a["c_forget_bias"], a["cache_c_logf"][0], out["c_logf_prompt"][0, 0],
                  out["c_logf_sample"][0].rearrange("s f h -> (s f) h"), ck, neg_c8)
    prompt_attention(nc, "pc", C_H // 2, lambda i, e: (2 * i + e) * DH, lambda i, e: D + (2 * i + e) * DH,
                     lambda i, e: 2 * D + (2 * i + e) * DH, lambda i, e: (2 * i + e) * DH, qkt_c, y_c, o_c, DH,
                     causal=True, ck=ck, copies=copies_c)
    sample_attention(nc, "sc", 2, 0, qkt_c, by_stream(a["cache_c_k"]), by_stream(a["cache_c_v"]),
                     y_c[samples, D:2 * D], y_c[samples, 2 * D:3 * D], o_c, 0, neg_c8=neg_c8,
                     row_mask=a["frame_mask"], selector=a["head_rows"])
    yp, ys = out["y_prompt"][0], out["y_sample"].rearrange("s f d -> (s f) d")
    with Stage(nc, "m1") as st:
        ht_hi, ht_lo = columns(st)
        merge(nc, "cm", o_c, a["w_c_out"][0], gain(1, 1), x2, lambda t: x3[t * P:(t + 1) * P], gain(1, 2),
              ht_hi, ht_lo)
        feed_forward(nc, "f1", x3, ht_hi, ht_lo, a["w_ffn_in"][1], a["w_ffn_out"][1], gain(1, 3),
                     lambda t: yp[t * P:(t + 1) * P] if t < TILES_P else ys)


INPUTS = ["x_prompt", "x_sample", "cache_a_k", "cache_a_v", "cache_b_k", "cache_b_v", "cache_c_k",
          "cache_c_v", "cache_c_logf", "norm_gains", "w_ab_in", "w_ab_out", "a_sinks", "b_lambda",
          "b_subln", "w_c_in", "c_forget_bias", "w_c_out", "w_ffn_in", "w_ffn_out"]
OUTPUTS = [
    ("y_prompt", (1, PROMPT, D)), ("y_sample", (STREAMS, FRAMES, D)),
    ("a_k_prompt", (1, 1, WIN, A_KV, DH)), ("a_v_prompt", (1, 1, WIN, A_KV, DH)),
    ("b_k_prompt", (1, 1, PROMPT, 2 * B_H, DH)), ("b_v_prompt", (1, 1, PROMPT, B_H, 2 * DH)),
    ("c_k_prompt", (1, 1, PROMPT, C_H, DH)), ("c_v_prompt", (1, 1, PROMPT, C_H, DH)),
    ("c_logf_prompt", (1, 1, PROMPT, C_H)),
    ("a_k_sample", (1, STREAMS, WIN, A_KV, DH)), ("a_v_sample", (1, STREAMS, WIN, A_KV, DH)),
    ("b_k_sample", (1, STREAMS, FRAMES, 2 * B_H, DH)), ("b_v_sample", (1, STREAMS, FRAMES, B_H, 2 * DH)),
    ("c_k_sample", (1, STREAMS, FRAMES, C_H, DH)), ("c_v_sample", (1, STREAMS, FRAMES, C_H, DH)),
    ("c_logf_sample", (1, STREAMS, FRAMES, C_H)),
]


def kernel(**inputs):
    import concourse.bacc as bacc
    from concourse.bass_utils import run_bass_kernel_spmd

    nc = bacc.Bacc("TRN2", target_bir_lowering=False, num_devices=1)
    arrays = {name: np.ascontiguousarray(inputs[name]) for name in INPUTS}
    arrays.update(rope_table=rope_table(), frame_mask=frame_mask(), odd_heads=odd_heads(), head_rows=head_rows())
    a = {n: nc.dram_tensor(f"in_{n}", x.shape, F32, kind="ExternalInput").ap() for n, x in arrays.items()}
    out = {n: nc.dram_tensor(f"out_{n}", shape, F32, kind="ExternalOutput").ap() for n, shape in OUTPUTS}
    build(nc, a, out)
    result = run_bass_kernel_spmd(nc, [{f"in_{n}": x for n, x in arrays.items()}], core_ids=[0])
    return tuple(result.results[0][f"out_{n}"] for n, _ in OUTPUTS)
```
